# Optimizing a Trainium2 kernel written in Bass

```python
import jax, jax.numpy as jnp
from jax import lax
import numpy as np

D_MODEL = 1024
BATCH = 1
SEQ = 512
DEPTH = 2
DEC_BATCH = 8
DEC_SEQ = 16
PAST_LEN = 512

CHUNK = 64
Q_BLOCK = 128
MIX_DIM = D_MODEL
D_FF = 2816
FFN_RES = 0.5
EPS = 1e-6
MLA_HEADS = 8
MLA_NOPE = 64
MLA_ROPE = 32
MLA_V = 64
MLA_Q_LORA = 256
MLA_KV_LORA = 128
ROPE_THETA = 10000.0
MLA_SCALE = (MLA_NOPE + MLA_ROPE) ** -0.5
ML_HEADS = 4
ML_DK = 64
ML_DV = 64
ML_CONV = 4
HG_HEADS = 4
HG_DK = 64
HG_DV = 64

SPLIT_SIZES = (MLA_Q_LORA, MLA_KV_LORA, MLA_ROPE,
               2 * ML_HEADS * ML_DK, ML_HEADS * ML_DV, ML_HEADS * ML_DV, ML_HEADS, ML_HEADS,
               HG_HEADS * HG_DK, HG_HEADS * HG_DK, HG_HEADS * HG_DV, HG_HEADS * HG_DV)
IN_DIM = sum(SPLIT_SIZES)

kernel_name = 'hybrid_stream_mla_mlstm_hgrn2_step'

def _split_points():
    pts, acc = [], 0
    for s in SPLIT_SIZES[:-1]:
        acc += s
        pts.append(acc)
    return pts

def rmsnorm(x, g):
    xf = x.astype(jnp.float32)
    y = xf * lax.rsqrt(jnp.mean(xf * xf, axis=-1, keepdims=True) + EPS)
    return (y * g.astype(jnp.float32)).astype(x.dtype)

def swiglu(x, w_in, w_out):
    gate, up = jnp.split(x @ w_in, 2, axis=-1)
    return (jax.nn.silu(gate) * up) @ w_out

def rope_tables(pos):
    inv = ROPE_THETA ** (-jnp.arange(0, MLA_ROPE, 2, dtype=jnp.float32) / MLA_ROPE)
    ang = pos.astype(jnp.float32)[:, None] * inv[None, :]
    return jnp.cos(ang), jnp.sin(ang)

def apply_rope(x, cos, sin):
    x1, x2 = jnp.split(x.astype(jnp.float32), 2, axis=-1)
    return jnp.concatenate([x1 * cos - x2 * sin, x2 * cos + x1 * sin], axis=-1).astype(x.dtype)

def mla_attend(q_lat, q_pe, ckv, kpe, q_pos, k_pos):
    s = jnp.einsum('bqhc,bkc->bhqk', q_lat, ckv) + jnp.einsum('bqhr,bkr->bhqk', q_pe, kpe)
    s = s.astype(jnp.float32) * MLA_SCALE
    mask = (k_pos[None, :] // CHUNK) <= (q_pos[:, None] // CHUNK)
    s = jnp.where(mask[None, None], s, jnp.finfo(jnp.float32).min)
    p = jax.nn.softmax(s, axis=-1).astype(ckv.dtype)
    return jnp.einsum('bhqk,bkc->bqhc', p, ckv)

def mla_prompt(q_lat, q_pe, ckv, kpe, pos):
    B, T, H, C = q_lat.shape
    nb = T // Q_BLOCK

    def blocks(a):
        return jnp.moveaxis(a.reshape((B, nb, Q_BLOCK) + a.shape[2:]), 1, 0)

    def one(args):
        ql, qp, qpos = args
        return mla_attend(ql, qp, ckv, kpe, qpos, pos)

    o = lax.map(one, (blocks(q_lat), blocks(q_pe), pos.reshape(nb, Q_BLOCK)))
    return jnp.moveaxis(o, 0, 1).reshape(B, T, H, C)

def mlstm_chunkwise(q, k, v, li, lf, c0, n0, m0):
    B, T, H, _ = q.shape
    L = min(CHUNK, T)
    nc = T // L
    causal = jnp.tril(jnp.ones((L, L), dtype=bool))

    def chunks(a):
        return jnp.moveaxis(a.reshape((B, nc, L) + a.shape[2:]), 1, 0)

    def step(carry, inp):
        c, n, m = carry
        qc, kc, vc, lic, lfc = inp
        b = jnp.cumsum(lfc, axis=1)
        logw = b[:, :, None, :] - b[:, None, :, :] + lic[:, None, :, :]
        logw = jnp.where(causal[None, :, :, None], logw, -jnp.inf)
        log_inter = b + m[:, None, :]
        m_t = jnp.maximum(log_inter, jnp.max(logw, axis=2))
        w_intra = jnp.exp(logw - m_t[:, :, None, :])
        w_inter = jnp.exp(log_inter - m_t)
        qk = jnp.einsum('bthd,bshd->btsh', qc, kc) * w_intra
        num = jnp.einsum('btsh,bshv->bthv', qk, vc) + w_inter[..., None] * jnp.einsum('bthd,bhdv->bthv', qc, c)
        den = jnp.sum(qk, axis=2) + w_inter * jnp.einsum('bthd,bhd->bth', qc, n)
        h = num / jnp.maximum(jnp.abs(den), jnp.exp(-m_t))[..., None]
        m_new = m_t[:, -1]
        w_s = jnp.exp(b[:, -1:] - b + lic - m_new[:, None])
        decay = jnp.exp(b[:, -1] + m - m_new)
        kw = kc * w_s[..., None]
        c_new = decay[..., None, None] * c + jnp.einsum('bshd,bshv->bhdv', kw, vc)
        n_new = decay[..., None] * n + jnp.sum(kw, axis=1)
        return (c_new, n_new, m_new), h

    (c1, n1, m1), h = lax.scan(step, (c0, n0, m0), tuple(chunks(a) for a in (q, k, v, li, lf)))
    h = jnp.moveaxis(h, 0, 1).reshape(B, T, H, v.shape[-1])
    return h, c1, n1, m1

def hgrn2_chunkwise(q, k, i, logf, s0):
    B, T, H, _ = q.shape
    L = min(CHUNK, T)
    nc = T // L
    causal = jnp.tril(jnp.ones((L, L), dtype=bool))

    def chunks(a):
        return jnp.moveaxis(a.reshape((B, nc, L) + a.shape[2:]), 1, 0)

    def step(s, inp):
        qc, kc, ic, lfc = inp
        b = jnp.cumsum(lfc, axis=1)
        diff = b[:, :, None] - b[:, None]
        dec = jnp.exp(jnp.where(causal[None, :, :, None, None], diff, -jnp.inf))
        a = jnp.sum(qc[:, :, None] * kc[:, None] * dec, axis=-1)
        o = jnp.einsum('btsh,bshv->bthv', a, ic) + jnp.einsum('bthd,bhdv->bthv', qc * jnp.exp(b), s)
        b_last = b[:, -1]
        s_new = jnp.exp(b_last)[..., None] * s + jnp.einsum('bshd,bshv->bhdv', kc * jnp.exp(b_last[:, None] - b), ic)
        return s_new, o

    s1, o = lax.scan(step, s0, tuple(chunks(a) for a in (q, k, i, logf)))
    o = jnp.moveaxis(o, 0, 1).reshape(B, T, H, i.shape[-1])
    return o, s1

def token_mixers(hn, pos, past, lw):
    B, T, _ = hn.shape
    f32 = jnp.float32
    (cq, ckv_raw, kpe_raw, ml_qk, ml_v, ml_o, ml_i, ml_f,
     hg_q, hg_f, hg_i, hg_g) = jnp.split(hn @ lw['w_in'], _split_points(), axis=-1)

    cq = rmsnorm(cq, lw['q_norm'])
    q = (cq @ lw['w_uq']).reshape(B, T, MLA_HEADS, MLA_NOPE + MLA_ROPE)
    cos, sin = rope_tables(pos)
    q_pe = apply_rope(q[..., MLA_NOPE:], cos[:, None], sin[:, None])
    q_lat = jnp.einsum('bthn,chn->bthc', q[..., :MLA_NOPE], lw['w_uk'])
    ckv_new = rmsnorm(ckv_raw, lw['kv_norm'])
    kpe_new = apply_rope(kpe_raw, cos, sin)
    if past is None:
        o_lat = mla_prompt(q_lat, q_pe, ckv_new, kpe_new, pos)
    else:
        ckv_all = jnp.concatenate([past[0].astype(ckv_new.dtype), ckv_new], axis=1)
        kpe_all = jnp.concatenate([past[1].astype(kpe_new.dtype), kpe_new], axis=1)
        k_pos = jnp.arange(ckv_all.shape[1])
        o_lat = mla_attend(q_lat, q_pe, ckv_all, kpe_all, pos, k_pos)
    mla_out = jnp.einsum('bthc,chv->bthv', o_lat, lw['w_uv']).reshape(B, T, MLA_HEADS * MLA_V)

    if past is None:
        conv0 = jnp.zeros((B, ML_CONV - 1, 2 * ML_HEADS * ML_DK), ml_qk.dtype)
        c0 = jnp.zeros((B, ML_HEADS, ML_DK, ML_DV), f32)
        n0 = jnp.zeros((B, ML_HEADS, ML_DK), f32)
        m0 = jnp.zeros((B, ML_HEADS), f32)
        s0 = jnp.zeros((B, HG_HEADS, HG_DK, HG_DV), f32)
    else:
        conv0 = past[5].astype(ml_qk.dtype)
        c0, n0, m0, s0 = (past[2].astype(f32), past[3].astype(f32), past[4].astype(f32), past[6].astype(f32))
    ext = jnp.concatenate([conv0, ml_qk], axis=1)
    conv_new = ext[:, -(ML_CONV - 1):]
    nch = ext.shape[-1]
    conv = lax.conv_general_dilated(ext, lw['conv_w'].astype(ext.dtype)[:, None, :], window_strides=(1,),
                                    padding='VALID', dimension_numbers=('NWC', 'WIO', 'NWC'),
                                    feature_group_count=nch)
    qk = jax.nn.silu(conv + lw['conv_b'].astype(conv.dtype)).astype(f32)
    mq, mk = jnp.split(qk, 2, axis=-1)
    mq = mq.reshape(B, T, ML_HEADS, ML_DK)
    mk = mk.reshape(B, T, ML_HEADS, ML_DK) * (ML_DK ** -0.5)
    mv = ml_v.astype(f32).reshape(B, T, ML_HEADS, ML_DV)
    gb = lw['gate_bias'].astype(f32)
    li = ml_i.astype(f32) + gb[0]
    lf = jax.nn.log_sigmoid(ml_f.astype(f32) + gb[1])
    h, c1, n1, m1 = mlstm_chunkwise(mq, mk, mv, li, lf, c0, n0, m0)
    ml_out = (jax.nn.sigmoid(ml_o.astype(f32)) * h.reshape(B, T, ML_HEADS * ML_DV)).astype(hn.dtype)

    lb = lw['lb']
    z = hg_f.astype(f32)
    logf = jnp.logaddexp(jnp.log(lb), jnp.log1p(-lb) + jax.nn.log_sigmoid(z))
    kk = (1.0 - lb) * jax.nn.sigmoid(-z)
    hq = jax.nn.silu(hg_q.astype(f32))
    sh = (B, T, HG_HEADS, HG_DK)
    o, s1 = hgrn2_chunkwise(hq.reshape(sh), kk.reshape(sh), hg_i.astype(f32).reshape(B, T, HG_HEADS, HG_DV),
                            logf.reshape(sh), s0)
    gate = jax.nn.silu(hg_g.astype(f32).reshape(B, T, HG_HEADS, HG_DV))
    hg_out = (rmsnorm(o, lw['hg_norm']) * gate).reshape(B, T, HG_HEADS * HG_DV).astype(hn.dtype)

    mix = jnp.concatenate([mla_out, ml_out, hg_out], axis=-1) @ lw['w_out']
    return mix, (ckv_new, kpe_new, c1, n1, m1, conv_new, s1)

def trunk_layer(x, pos, past, lw):
    g = lw['ln']
    h = swiglu(rmsnorm(x, g[0]), lw['ffn_in'][0], lw['ffn_out'][0])
    x = x + FFN_RES * rmsnorm(h, g[1])
    mix, state = token_mixers(rmsnorm(x, g[2]), pos, past, lw)
    x = x + rmsnorm(mix, g[3])
    h = swiglu(rmsnorm(x, g[4]), lw['ffn_in'][1], lw['ffn_out'][1])
    x = x + FFN_RES * rmsnorm(h, g[5])
    return x, state

def setup_inputs(seed: int = 0) -> dict:
    key = jax.random.key(seed)
    ks = jax.random.split(key, 26)
    f32 = jnp.float32

    def nrm(k, shape, s):
        return s * jax.random.normal(k, shape, f32)

    f_bias = jnp.broadcast_to(jnp.linspace(3.0, 6.0, ML_HEADS, dtype=f32), (DEPTH, ML_HEADS)) + nrm(ks[24], (DEPTH, ML_HEADS), 0.1)
    gate_bias = jnp.stack([nrm(ks[21], (DEPTH, ML_HEADS), 0.1), f_bias], axis=1)
    return {
        'x_prompt': nrm(ks[0], (BATCH, SEQ, D_MODEL), 1.0),
        'x_sample': nrm(ks[1], (DEC_BATCH, DEC_SEQ, D_MODEL), 1.0),
        'cache_ckv': nrm(ks[2], (DEPTH, DEC_BATCH, PAST_LEN, MLA_KV_LORA), 1.0),
        'cache_kpe': nrm(ks[3], (DEPTH, DEC_BATCH, PAST_LEN, MLA_ROPE), 1.0),
        'state_mlstm_c': nrm(ks[4], (DEPTH, DEC_BATCH, ML_HEADS, ML_DK, ML_DV), 0.1),
        'state_mlstm_n': nrm(ks[5], (DEPTH, DEC_BATCH, ML_HEADS, ML_DK), 0.5),
        'state_mlstm_m': nrm(ks[6], (DEPTH, DEC_BATCH, ML_HEADS), 1.0),
        'state_mlstm_conv': nrm(ks[7], (DEPTH, DEC_BATCH, ML_CONV - 1, 2 * ML_HEADS * ML_DK), 1.0),
        'state_hgrn': nrm(ks[8], (DEPTH, DEC_BATCH, HG_HEADS, HG_DK, HG_DV), 0.3),
        'ln_gains': 1.0 + nrm(ks[9], (DEPTH, 6, D_MODEL), 0.05),
        'w_ffn_in': nrm(ks[10], (DEPTH, 2, D_MODEL, 2 * D_FF), D_MODEL ** -0.5),
        'w_ffn_out': nrm(ks[11], (DEPTH, 2, D_FF, D_MODEL), D_FF ** -0.5),
        'w_in': nrm(ks[12], (DEPTH, D_MODEL, IN_DIM), D_MODEL ** -0.5),
        'w_out': nrm(ks[13], (DEPTH, MIX_DIM, D_MODEL), MIX_DIM ** -0.5),
        'mla_q_norm': 1.0 + nrm(ks[14], (DEPTH, MLA_Q_LORA), 0.05),
        'mla_kv_norm': 1.0 + nrm(ks[15], (DEPTH, MLA_KV_LORA), 0.05),
        'mla_w_uq': nrm(ks[16], (DEPTH, MLA_Q_LORA, MLA_HEADS * (MLA_NOPE + MLA_ROPE)), MLA_Q_LORA ** -0.5),
        'mla_w_uk': nrm(ks[17], (DEPTH, MLA_KV_LORA, MLA_HEADS, MLA_NOPE), MLA_KV_LORA ** -0.5),
        'mla_w_uv': nrm(ks[18], (DEPTH, MLA_KV_LORA, MLA_HEADS, MLA_V), MLA_KV_LORA ** -0.5),
        'ml_conv_w': nrm(ks[19], (DEPTH, ML_CONV, 2 * ML_HEADS * ML_DK), ML_CONV ** -0.5),
        'ml_conv_b': nrm(ks[20], (DEPTH, 2 * ML_HEADS * ML_DK), 0.01),
        'ml_gate_bias': gate_bias,
        'hg_lb_raw': nrm(ks[22], (DEPTH, HG_HEADS * HG_DK), 0.5),
        'hg_norm': 1.0 + nrm(ks[23], (DEPTH, HG_DV), 0.05),
    }

def reference(x_prompt, x_sample, cache_ckv, cache_kpe, state_mlstm_c, state_mlstm_n, state_mlstm_m,
              state_mlstm_conv, state_hgrn, ln_gains, w_ffn_in, w_ffn_out, w_in, w_out,
              mla_q_norm, mla_kv_norm, mla_w_uq, mla_w_uk, mla_w_uv, ml_conv_w, ml_conv_b,
              ml_gate_bias, hg_lb_raw, hg_norm):
    lb_all = jnp.cumsum(jax.nn.softmax(hg_lb_raw.astype(jnp.float32), axis=0), axis=0)
    lb_all = lb_all - lb_all[:1]
    past_len = cache_ckv.shape[2]
    pos_p = jnp.arange(x_prompt.shape[1])
    pos_s = past_len + jnp.arange(x_sample.shape[1])
    yp, ys = x_prompt, x_sample
    p_lists = [[] for _ in range(7)]
    s_lists = [[] for _ in range(7)]
    for l in range(DEPTH):
        lw = {'ln': ln_gains[l], 'ffn_in': w_ffn_in[l], 'ffn_out': w_ffn_out[l], 'w_in': w_in[l],
              'w_out': w_out[l], 'q_norm': mla_q_norm[l], 'kv_norm': mla_kv_norm[l], 'w_uq': mla_w_uq[l],
              'w_uk': mla_w_uk[l], 'w_uv': mla_w_uv[l], 'conv_w': ml_conv_w[l], 'conv_b': ml_conv_b[l],
              'gate_bias': ml_gate_bias[l], 'lb': lb_all[l], 'hg_norm': hg_norm[l]}
        yp, st_p = trunk_layer(yp, pos_p, None, lw)
        past = (cache_ckv[l], cache_kpe[l], state_mlstm_c[l], state_mlstm_n[l], state_mlstm_m[l],
                state_mlstm_conv[l], state_hgrn[l])
        ys, st_s = trunk_layer(ys, pos_s, past, lw)
        for lst, a in zip(p_lists, st_p):
            lst.append(a)
        for lst, a in zip(s_lists, st_s):
            lst.append(a)
    p_ckv, p_kpe, p_c, p_n, p_m, p_conv, p_hg = [jnp.stack(a) for a in p_lists]
    s_ckv, s_kpe, s_c, s_n, s_m, s_conv, s_hg = [jnp.stack(a) for a in s_lists]
    return (yp, ys, p_ckv, p_kpe, p_c, p_n, p_m, p_conv, p_hg,
            s_ckv, s_kpe, s_c, s_n, s_m, s_conv, s_hg)


_drawn_inputs = setup_inputs


def setup_inputs(seed=0):
    import zlib

    import numpy as np

    out = dict(_drawn_inputs(seed))
    spreads = {}
    factors = {'mla_q_norm': 3.989, 'ml_conv_b': 2.897}
    for name, (base, spread) in spreads.items():
        noise = np.random.default_rng([zlib.crc32(name.encode()), seed]).standard_normal(out[name].shape)
        drawn = base * np.exp(spread * noise) if base else spread * noise
        out[name] = __import__('jax').numpy.asarray(drawn.astype(out[name].dtype))
    for name, factor in factors.items():
        out[name] = (out[name] * factor).astype(out[name].dtype)
    return out
```

```python
from contextlib import ExitStack

import numpy as np

import concourse.bass as bass
from concourse import mybir

F32 = mybir.dt.float32
F32R = mybir.dt.float32r
U8 = mybir.dt.uint8
ACT = mybir.ActivationFunctionType
ALU = mybir.AluOpType
AX_X = mybir.AxisListType.X

P = 128
LAYERS, D, DFF = 2, 1024, 2816
TP, NSEQ, TS = 512, 8, 16
T = TP + NSEQ * TS
HALF = T // 2
KD = D // P
TILES = T // P
PT_ = TP // P
PAST = 512
CBUF = 3
CACHE_TURNS = [len(range(c, NSEQ, CBUF)) for c in range(CBUF)]
H, NOPE, ROPE, QL, KVL = 8, 64, 32, 256, 128
QK = NOPE + ROPE
MLA_SCALE = float(QK) ** -0.5
MH, DK = 4, 64
AUG = DK + 1
EPS = 1e-6
FAR = 1e30

UP_A, UP_B = 12, 10
DOWN = KD
FFN_UNITS = UP_A + DOWN + UP_B + DOWN
PROJ_UNITS, OUT_UNITS = 10, 4
FFN0 = 0
PROJ = FFN_UNITS
WOUT = PROJ + PROJ_UNITS
FFN1 = WOUT + OUT_UNITS
UNITS = FFN1 + FFN_UNITS
CREDIT = 2
LOAD_INC = 64
C_CQ, C_CKV, C_KPE, C_QK, C_V, C_O, C_I, C_F = 0, 256, 384, 416, 928, 1184, 1440, 1444
C_HQ, C_HF, C_HI, C_HG = 1448, 1704, 1960, 2216
SQ_PRE = {0: 0, 1: 16, 2: 32}
SQ_POST = {0: 8, 1: 24, 2: 40}
SPLIT_PRE = {0: 0, 1: 8, 2: 24}
SPLIT_MIX = 16
G_LN, G_Q, G_KV, G_CW, G_CB, G_END = 0, 48, 50, 51, 67, 71
NB_COLS = G_END - G_Q
LEVELS = (64, 32, 16, 8, 4, 2, 1)
NLEV = len(LEVELS) + 1


def shape_constants():
    inv = (10000.0 ** (-np.arange(0, ROPE, 2, dtype=np.float32) / ROPE)).astype(np.float32)
    pos = np.concatenate([np.arange(TP), np.tile(PAST + np.arange(TS), NSEQ)]).astype(np.float32)
    ang = inv[:, None] * pos[None, :]
    rope = np.zeros((2, QK, T), np.float32)
    rope[0, NOPE:] = np.concatenate([np.cos(ang)] * 2)
    rope[1, NOPE:] = np.concatenate([-np.sin(ang), np.sin(ang)])
    swap = np.zeros((QK, QK), np.float32)
    for j in range(ROPE):
        swap[NOPE + (j + ROPE // 2) % ROPE, NOPE + j] = 1.0
    s, t = np.arange(P)[:, None], np.arange(P)[None, :]
    causal = np.where(s <= t, 0.0, -FAR)
    streams = np.where((s <= t) & (s // TS == t // TS), 0.0, -FAR)
    masks = np.stack([causal, streams], axis=1).astype(np.float32)
    level = np.zeros((P, NLEV, P), np.float32)
    for n, h in enumerate(LEVELS):
        level[:, n] = (s // (2 * h) == t // (2 * h)) & (s % (2 * h) < h) & (t % (2 * h) >= h)
    level[:, NLEV - 1] = s == t
    starts = np.zeros(T, bool)
    starts[0:TP:P] = True
    starts[TP::TS] = True
    going = np.broadcast_to(1.0 - starts.astype(np.float32), (P, T))
    drop = np.zeros((MH, T), np.float32)
    drop[:, TP::TS] = -FAR
    select = np.zeros((MH, MH, P), np.float32)
    for h in range(MH):
        select[h, h] = 1.0
    owner = (np.arange(P)[:, None] // TS == np.arange(NSEQ)[None, :]).astype(np.float32)
    return {"c_rope": rope, "c_swap": swap, "c_mask": masks, "c_level": level,
            "c_going": np.ascontiguousarray(going), "c_drop": drop, "c_select": select, "c_owner": owner,
            "c_ident": np.eye(P, dtype=np.float32), "c_ones": np.ones((P, P), np.float32)}


ACT_STEPS, DVE_STEPS, POOL_STEPS = 15, 201, 7


class Event:

    def __init__(self, sem, per_layer, credit=0):
        self.sem, self.per_layer, self.credit = sem, per_layer, credit

    def nth(self, l, k):
        return self.sem, l * self.per_layer + (k + 1 + self.credit)


class Chain:

    def __init__(self, eng, sem, per_layer):
        self.eng, self.sem, self.per_layer, self.n, self.l = eng, sem, per_layer, 0, 0

    def link(self, ins):
        self.n += 1
        ins.then_inc(self.sem, 1)
        self.eng.wait_ge(self.sem, self.l * self.per_layer + self.n)

    def close(self):
        assert self.n == self.per_layer, (self.n, self.per_layer)


def encoder(nc, A, O):
    ctx = ExitStack()
    ctx.enter_context(nc.allow_non_contiguous_dma(reason="single columns of small states and biases"))

    def tile(stack, name, shape, dt=F32):
        return stack.enter_context(nc.sbuf_tensor(name, shape, dt))

    def sem(name):
        return ctx.enter_context(nc.semaphore(name))

    def event(name, per_layer, credit=0):
        return Event(sem(name), per_layer, credit)

    X = tile(ctx, "x", [P, KD, T])
    Y = tile(ctx, "y", [P, KD, T])
    RAW = tile(ctx, "raw", [P, 2, 2048])
    WH = tile(ctx, "wh", [P, 2, 2048], F32R)
    WL = tile(ctx, "wl", [P, 2, 2048], F32R)
    GB = tile(ctx, "gb", [P, 2, T])
    UB = tile(ctx, "ub", [P, 2, T])
    R = tile(ctx, "r", [P, T])
    IDENT = tile(ctx, "ident", [P, P])
    ONES = tile(ctx, "ones", [P, P])
    PAR = tile(ctx, "par", [P, LAYERS * G_END + 2 * LAYERS])
    LP = tile(ctx, "lp", [P, G_END])
    GBIAS = tile(ctx, "gbias", [36, LAYERS])
    GBL = tile(ctx, "gbl", [36, 1])
    HGN = tile(ctx, "hgn", [P, LAYERS, DK])
    HGNL = tile(ctx, "hgnl", [P, DK])
    HB = tile(ctx, "hb", [P, LAYERS, 6])
    HBL = tile(ctx, "hbl", [P, 6])
    EPSC = tile(ctx, "epsc", [P, 1])
    PS = ctx.enter_context(nc.psum_tensor("ps", [P, 8, 512], F32))
    SY, SX = UB[:, 0, :], UB[:, 1, :]
    psf = PS[:, :, :].rearrange("p b n -> p (b n)")

    s_io = ExitStack()
    XIO = tile(s_io, "xio", [P, TILES, D])
    PROW = tile(s_io, "prow", [P, 2, P])
    HROW = tile(s_io, "hrow", [1, LAYERS * DK])
    LB = tile(s_io, "lb", [P, 4, 2])
    s_io.close()

    s_xn = ExitStack()
    XH = tile(s_xn, "xh", [P, KD, T], F32R)
    XL = tile(s_xn, "xl", [P, KD, T], F32R)
    s_h = ExitStack()
    HH = tile(s_h, "hh", [P, UP_A, T], F32R)
    HL = tile(s_h, "hl", [P, UP_A, T], F32R)
    s_h.close()
    s_hg, s_ml, s_mla = ExitStack(), ExitStack(), ExitStack()
    HI = tile(s_hg, "hi", [P, TILES, MH, DK])
    HGG = tile(s_hg, "hgg", [P, TILES, MH, DK])
    HQ = tile(s_hg, "hq", [P, 2, T])
    HF = tile(s_hg, "hf", [P, 2, T])
    VA = tile(s_ml, "va", [P, TILES, MH, AUG])
    OG = tile(s_ml, "og", [P, TILES, MH * DK])
    EXTP = tile(s_ml, "extp", [P, 4, TP + 3])
    EXTS = tile(s_ml, "exts", [P, 4, NSEQ, TS + 3])
    MISC = tile(s_ml, "misc", [P, T])
    CQ = tile(s_mla, "cq", [P, 2, T])
    CKVT = tile(s_mla, "ckvt", [P, T])
    KPER = tile(s_mla, "kper", [QK, T])
    WUQ = tile(s_mla, "wuq", [P, 2, H * QK])
    WUK = tile(s_mla, "wuk", [P, H, NOPE])
    WUV = tile(s_mla, "wuv", [P, H * 64])
    SWAP = tile(s_mla, "swap", [QK, QK])
    MX = tile(s_mla, "mx", [P, 2, 4])
    s_mla.close()
    VMSK = tile(s_ml, "vmsk", [P, NSEQ, MH * AUG])
    G3 = tile(s_ml, "g3", [P, T])
    MASK = tile(s_ml, "mask", [P, 2, P])
    SEL = tile(s_ml, "sel", [MH, MH, P])
    GOING = tile(s_ml, "going", [MH, T])
    DROP = tile(s_ml, "drop", [MH, T])
    SC = tile(s_ml, "sc", [NSEQ * 3, 512])
    OWN = tile(s_ml, "own", [P, NSEQ])
    CNT = tile(s_ml, "cnt", [P, 4, NSEQ * 3])
    s_ml.close()
    KK = tile(s_hg, "kk", [P, 2, T])
    BC = tile(s_hg, "bc", [P, 2, T])
    QE = tile(s_hg, "qe", [P, 2, T])
    KDF = tile(s_hg, "kdf", [P, 2, T])
    DD0 = tile(s_hg, "dd0", [P, 2, T])
    QK0 = tile(s_hg, "qk0", [P, 2, T])
    AT = tile(s_hg, "at", [P, TILES, 2, 2, P])
    HGO = tile(s_hg, "hgo", [P, T])
    LVL = tile(s_hg, "lvl", [P, NLEV, P], U8)
    s_hg.close()
    s_xn.close()

    s_w = ExitStack()
    QLAT = tile(s_w, "qlat", [P, NSEQ, H, TS])
    QPE = tile(s_w, "qpe", [ROPE, NSEQ, H, TS])
    CTOK = tile(s_w, "ctok", [P, TILES, KVL])
    s_p = ExitStack()
    WUKT = tile(s_p, "wukt", [NOPE, H, P])
    QT = tile(s_p, "qt", [QK, 2, T])
    KT = tile(s_p, "kt", [QK, 2, TP])
    VM = tile(s_p, "vm", [P, PT_, H * 64])
    PB = tile(s_p, "pb", [P, 2, TP])
    PTB = tile(s_p, "ptb", [P, 2, TP])
    s_p.close()
    CC = tile(s_w, "cc", [P, CBUF, 4, KVL])
    CK = tile(s_w, "ck", [P, CBUF, 4, ROPE])
    CT = tile(s_w, "ct", [P, 2, PAST])
    SP = tile(s_w, "sp", [P, 2, PAST + TS])
    PNEW = tile(s_w, "pnew", [P, NSEQ, P])
    SPT = tile(s_w, "spt", [P, 2, T])
    OLAT = tile(s_w, "olat", [P, H, P])
    KN = tile(s_w, "kn", [ROPE, P])
    s_w.close()
    ROPET, TMP, KPT = UB, GB[:, 0, :], GB

    s_w = ExitStack()
    QKC = tile(s_w, "qkc", [P, 4, T])
    CST = tile(s_w, "cst", [P, 2, 2 * AUG])
    CSS = tile(s_w, "css", [P, 2, NSEQ, 2 * AUG])
    QM = tile(s_w, "qm", [P, 2, NSEQ, P])
    DGB = tile(s_w, "dgb", [P, MH, 12])
    GT = tile(s_w, "gt", [P, TILES, P])
    DARG = tile(s_w, "darg", [P, MH, P])
    WT = tile(s_w, "wt", [P, MH, P])
    NI = tile(s_w, "ni", [P, MH, AUG])
    HM = tile(s_w, "hm", [P, MH * DK])
    KW = tile(s_w, "kw", [P, MH, DK])
    DEN = tile(s_w, "den", [P, 2, MH])
    M0 = tile(s_w, "m0", [MH, NSEQ])
    MPV = tile(s_w, "mpv", [MH, 12])
    GE = tile(s_w, "ge", [MH, 12])
    WIE = tile(s_w, "wie", [MH, 12])
    s_w.close()

    s_w = ExitStack()
    ST = tile(s_w, "st", [P, 2, P])
    SS = tile(s_w, "ss", [P, 2, NSEQ, P])
    QM2 = tile(s_w, "qm2", [P, 2, NSEQ, P])
    IM = tile(s_w, "im", [P, NSEQ, MH * DK])
    KDT = tile(s_w, "kdt", [P, MH * DK])
    OO = tile(s_w, "oo", [P, MH, DK])
    OSQ = tile(s_w, "osq", [P, MH, DK])
    ORM = tile(s_w, "orm", [P, 2, MH])
    EBL = tile(s_w, "ebl", [P, 2, 12])
    DD1 = tile(s_w, "dd1", [P, 2, T])
    QK1 = tile(s_w, "qk1", [P, 2, T])
    OWN2 = tile(s_w, "own2", [P, NSEQ])
    s_w.close()
    DD, QKL = (DD0, DD1), (QK0, QK1)

    loaded = [sem("loaded0"), sem("loaded1")]
    hi_ready = sem("hi_ready")
    lo_ready = sem("lo_ready")
    unit_done = sem("unit_done")
    drained = sem("drained")
    setup_in = sem("setup_in")
    setup_ps, setup_sb = sem("setup_ps"), sem("setup_sb")
    xin_ps, x_init = sem("xin_ps"), sem("x_init")
    lp_ready = event("lp_ready", 1)
    sq_ready = event("sq_ready", 48)
    sq_added = event("sq_added", 48)
    ms_ready = event("ms_ready", 6)
    r_ready = event("r_ready", 6)
    x_ready = event("x_ready", 24)
    xt_ready = event("xt_ready", KD)
    xh_ready = event("xh_ready", 32)
    xl_ready = event("xl_ready", 32)
    n_h = 2 * (UP_A + UP_B)
    gate_ready = event("gate_ready", n_h)
    silu_ready = event("silu_ready", n_h)
    h_ready = event("h_ready", n_h)
    hh_ready = event("hh_ready", n_h)
    hl_ready = event("hl_ready", n_h, 2)
    mla_in = sem("mla_in")
    wukt_ps, wukt_sb = event("wukt_ps", 1), event("wukt_sb", 1)
    proj_sb = event("proj_sb", 2)
    mla_sq, mla_ms, mla_r = event("mla_sq", 1), event("mla_ms", 1), event("mla_r", 1)
    cq_ready, kswap_ps, kpe_ready = event("cq_ready", 1), event("kswap_ps", 1), event("kpe_ready", 1)
    kper_zero, kt_rope = event("kper_zero", 1), event("kt_rope", 1)
    tok_ps, tok_sb = event("tok_ps", 1), event("tok_sb", 1)
    v_ps, v_sb = event("v_ps", PT_), event("v_sb", PT_)
    qk_ps, qk_sb, sw_ps = event("qk_ps", H), event("qk_sb", H), event("sw_ps", H)
    q_ready, ql_ps, ql_sb = event("q_ready", H), event("ql_ps", H), event("ql_sb", H)
    NT = H * PT_
    s_ps, nm_sb, exp_sb = event("s_ps", NT), event("nm_sb", NT), event("exp_sb", NT)
    p_sb, t_ps, pt_sb = event("p_sb", NT), event("t_ps", NT), event("pt_sb", NT)
    pv_ps, o_sb = event("pv_ps", NT), event("o_sb", H // 2)
    cache_in = [sem(f"cache_in{c}") for c in range(CBUF)]
    pn_zero, kn_sb = event("pn_zero", 1), event("kn_sb", 1)
    ct_ps, ct_sb = event("ct_ps", NSEQ), event("ct_sb", NSEQ)
    ss_ps, snm_sb, sexp_sb = event("ss_ps", NSEQ), event("snm_sb", NSEQ), event("sexp_sb", NSEQ)
    sp_sb, spt_ps, spt_sb = event("sp_sb", NSEQ), event("spt_ps", NSEQ), event("spt_sb", NSEQ)
    spv_ps, ol_sb = event("spv_ps", NSEQ), event("ol_sb", NSEQ)
    uo_ps, mla_done = event("uo_ps", 1), event("mla_done", 1)
    ml_in, ml_zero = sem("ml_in"), event("ml_zero", 1)
    cnt_sb = event("cnt_sb", 1)
    cs_ps, cn_ps, cn_sb = event("cs_ps", 1), event("cn_ps", 1), event("cn_sb", 1)
    ext_sb, conv_sb, csilu_sb, qk_final = (event(n, 1) for n in ("ext_sb", "conv_sb", "csilu_sb", "qk_final"))
    ga_sb, gab_sb, gl_sb, gd_sb, ge_sb = (event(n, 1) for n in ("ga_sb", "gab_sb", "gl_sb", "gd_sb", "ge_sb"))
    gt_ps, gt_sb, oexp_sb, msk_sb = (event(n, 1) for n in ("gt_ps", "gt_sb", "oexp_sb", "msk_sb"))
    nb_ps, mk_ps, arg_sb, wexp_sb, wt_sb, kw_sb = (
        event(n, TILES) for n in ("nb_ps", "mk_ps", "arg_sb", "wexp_sb", "wt_sb", "kw_sb"))
    mo_ps, ni_sb, hm_sb, hmt_ps, hmt_sb = (
        event(n, TILES) for n in ("mo_ps", "ni_sb", "hm_sb", "hmt_ps", "hmt_sb"))
    cst_sb, upd_ps = event("cst_sb", PT_), event("upd_ps", PT_)
    csu_ps, csu_sb = event("csu_ps", 2), event("csu_sb", 2)
    hg_in, hg_zero = sem("hg_in"), event("hg_zero", 1)
    level_in, lvl_sb = sem("level_in"), event("lvl_sb", 1)
    za_sb, zl_sb, zs_sb, zk_sb, zd_sb, ze_sb, bc_sb = (
        event(n, 1) for n in ("za_sb", "zl_sb", "zs_sb", "zk_sb", "zd_sb", "ze_sb", "bc_sb"))
    kk_sb, hd_sb, he_sb, hq_sb = event("kk_sb", 1), event("hd_sb", 7), event("he_sb", 7), event("hq_sb", 8)
    NLV = 3 * PT_ + 5 * TILES
    lv_ps, lv_sb = event("lv_ps", NLV), event("lv_sb", NLV)
    kd_sb, qe_sb, hmsk_sb = event("kd_sb", 2), event("qe_sb", 2), event("hmsk_sb", 1)
    kdt_ps, kdt_sb, ho_ps, hsq_sb, hrs_sb, hr_sb, oo_sb, hot_ps, hot_sb = (
        event(n, TILES) for n in ("kdt_ps", "kdt_sb", "ho_ps", "hsq_sb", "hrs_sb", "hr_sb", "oo_sb",
                                  "hot_ps", "hot_sb"))
    hup_ps, st_sb = event("hup_ps", PT_ + 2), event("st_sb", PT_ + 2)
    passed = {eng: sem(name) for eng, name in ((nc.tensor, "pe_passed"), (nc.vector, "dve_passed"),
                                               (nc.gpsimd, "pool_passed"))}
    cn_stored = sem("cn_stored")
    stored = sem("stored")
    y_ps, y_sb, y_stored = sem("y_ps"), sem("y_sb"), sem("y_stored")
    act_chain, dve_chain, pool_chain = sem("act_chain"), sem("dve_chain"), sem("pool_chain")
    act_setup, dve_setup = sem("act_setup"), sem("dve_setup")

    LAYER_STORES = 30
    SETUP_LOADS = 7 + 4 * LAYERS + 2
    block = ctx.enter_context(nc.Block())

    def unit(l, base, i, j):
        return l * UNITS + (base + j) + 2 * i

    def turn(l, base, i, j):
        return (l * (UNITS // 2) + (base // 2 + 1) + i) * LOAD_INC

    def held(eng):
        eng.sem_inc(passed[eng], 1)

    def latent_out(b):
        return PS[:, 5 + 2 * ((b + 1) % 2), 256:256 + P]

    @block.sync
    def _(sp):
        def load(u, j, pieces):
            sp.wait_ge(lo_ready, u + 1)
            for dst, src in pieces:
                sp.dma_start(dst, src).then_inc(loaded[j], LOAD_INC // len(pieces))

        def slot(j, n, w):
            return RAW[:, j, 0:n * w].rearrange("p (k n) -> p k n", n=w)

        def up(l, f, base, first, pairs):
            src = A["w_ffn_in"][l, f].rearrange("(k p) n -> p k n", p=P)
            with sp.Fori(0, pairs) as i:
                for j in range(2):
                    at = i * (2 * P) + (first + j) * P
                    load(unit(l, base, i, j), j,
                         [(slot(j, KD, 256)[:, :, g * P:(g + 1) * P], src[:, :, bass.ds(at + g * DFF, P)])
                          for g in range(2)])

        def down(l, f, base, first, n):
            src = A["w_ffn_out"][l, f].rearrange("(k p) n -> p k n", p=P)
            with sp.Fori(0, DOWN // 2) as i:
                for j in range(2):
                    at = i * (2 * P) + j * P
                    load(unit(l, base, i, j), j,
                         [(slot(j, n, P)[:, h * n // 2:(h + 1) * n // 2, :],
                           src[:, first + h * n // 2:first + (h + 1) * n // 2, bass.ds(at, P)])
                          for h in range(2)])

        def ffn(l, f, base):
            up(l, f, base, 0, UP_A // 2)
            down(l, f, base + UP_A, 0, UP_A)
            up(l, f, base + UP_A + DOWN, UP_A, UP_B // 2)
            down(l, f, base + UP_A + DOWN + UP_B, UP_A, UP_B)

        def proj(l):
            src = A["w_in"][l].rearrange("(k p) n -> p k n", p=P)
            for n, c in enumerate((C_CQ, None, C_QK, C_QK + 256, C_HQ, C_HF, C_V, C_O, C_HI, C_HG)):
                j = n % 2
                dst = slot(j, KD, 256)
                if c is None:
                    cuts = [(0, C_CKV, P), (P, C_I, 32), (P + 32, C_F, 32), (P + 64, C_KPE, 64)]
                else:
                    cuts = [(0, c, P), (P, c + P, P)]
                load(unit(l, PROJ, n // 2, j), j,
                     [(dst[:, :, o:o + w], src[:, :, s:s + w]) for o, s, w in cuts])

        def wout(l):
            src = A["w_out"][l].rearrange("(k p) n -> p k n", p=P)
            for n in range(OUT_UNITS):
                j = n % 2
                load(unit(l, WOUT, n // 2, j), j,
                     [(slot(j, KD, 256)[:, :, g * P:(g + 1) * P], src[:, :, n * 256 + g * P:n * 256 + (g + 1) * P])
                      for g in range(2)])

        for dst, src in (
            (PROW[0:96, 0, :], A["ln_gains"].rearrange("l j (c f) -> (l j c) f", f=P)),
            (HROW[:, :], A["hg_norm"].rearrange("l (a v) -> a (l v)", a=1)),
            (IDENT[:, :], A["c_ident"]), (ONES[:, :], A["c_ones"]),
            (GBIAS[0:4, :], A["ml_gate_bias"][:, 0, :].rearrange("l h -> h l")),
            (GBIAS[32:36, :], A["ml_gate_bias"][:, 1, :].rearrange("l h -> h l")),
            (PROW[46:50, 1, :], A["hg_lb_raw"].rearrange("l (c f) -> (l c) f", f=P)),
            *((PROW[b + l * NB_COLS:b + l * NB_COLS + n, 1, :], src) for l in range(LAYERS) for b, n, src in (
                (0, 2, A["mla_q_norm"][l].rearrange("(c f) -> c f", f=P)),
                (2, 1, A["mla_kv_norm"][l].rearrange("(c f) -> c f", f=P)),
                (3, 16, A["ml_conv_w"][l].rearrange("j (c f) -> (j c) f", f=P)),
                (19, 4, A["ml_conv_b"][l].rearrange("(c f) -> c f", f=P)))),
            (XIO[:, 0:PT_, :], A["x_prompt"][0].rearrange("(t p) f -> p t f", p=P)),
            (XIO[:, PT_, :], A["x_sample"].rearrange("b t f -> (b t) f")),
        ):
            sp.dma_start(dst, src).then_inc(setup_in, 16)
        with sp.Fori(0, LAYERS) as l:
            ffn(l, 0, FFN0)
            proj(l)
            wout(l)
            ffn(l, 1, FFN1)
        load(LAYERS * UNITS, 0, [(RAW[:, 0, h * 1024:(h + 1) * 1024],
                                  A["w_ffn_in"][0, 0, 0:P, h * 1024:(h + 1) * 1024]) for h in range(2)])
        for t in range(TILES):
            sp.wait_ge(y_sb, t + 1)
            dst = O["y_prompt"][0, t * P:(t + 1) * P, :] if t < PT_ else O["y_sample"].rearrange("b t f -> (b t) f")
            sp.dma_start(dst, XIO[:, t, :]).then_inc(y_stored, 16)
        sp.wait_ge(y_stored, 16 * TILES)
        sp.wait_ge(stored, 16 * LAYER_STORES * LAYERS)
        sp.wait_ge(cn_stored, 32 * LAYERS)

    @block.tensor
    def _(pe):
        def three(out, wh, wl, xh, xl, first, last):
            pe.matmul(out, wh, xh, start=first, stop=False)
            pe.matmul(out, wh, xl, start=False, stop=False)
            return pe.matmul(out, wl, xh, start=False, stop=last)

        def halves(j, b, k, n, w, col, xh, xl, ncols):
            wh = WH[:, j, k * w + col:k * w + col + P]
            wl = WL[:, j, k * w + col:k * w + col + P]
            for h in range(2):
                mm = three(PS[:, b + h, 0:HALF], wh, wl, xh[:, k, h * HALF:(h + 1) * HALF],
                           xl[:, k, h * HALF:(h + 1) * HALF], k == 0, k == n - 1)
            return mm

        def begin(u):
            pe.wait_ge(lo_ready, u + 3)
            pe.wait_ge(drained, u + 1)

        def wide_unit(l, u, j, split_at):
            begin(u)
            for k in range(KD):
                if split_at is not None:
                    pe.wait_ge(*xl_ready.nth(l, split_at + k))
                for part in range(2):
                    mm = halves(j, 4 * j + 2 * part, k, KD, 256, part * P, XH, XL, None)
            mm.then_inc(unit_done, 1)

        def sum_squares(l, q, sq, total):
            pe.wait_ge(*sq_added.nth(l, sq + KD - 1))
            for h in range(2):
                mm = pe.matmul(PS[:, 6 + h, 0:HALF], ONES[:, :], total[:, h * HALF:(h + 1) * HALF],
                               start=True, stop=True)
            mm.then_inc(ms_ready.sem, 1)

        def up(l, base, pairs, pre):
            if pre is not None:
                wide_unit(l, unit(l, base, 0, 0), 0, SPLIT_PRE[pre])
                sum_squares(l, 2 * pre, SQ_PRE[pre], SX)
                pe.wait_ge(*r_ready.nth(l, 2 * pre))
                wide_unit(l, unit(l, base, 0, 1), 1, None)
            held(pe)
            with pe.Fori(0 if pre is None else 1, pairs) as i:
                for j in range(2):
                    wide_unit(l, unit(l, base, i, j), j, None)

        def down(l, base, n, h_from):
            pe.wait_ge(*hl_ready.nth(l, h_from + n - 1))
            held(pe)
            with pe.Fori(0, DOWN // 2) as i:
                for j in range(2):
                    begin(unit(l, base, i, j))
                    for k in range(n):
                        mm = halves(j, 4 * j, k, n, P, 0, HH, HL, None)
                    mm.then_inc(unit_done, 1)

        def ffn(l, f, base):
            h0 = f * (UP_A + UP_B)
            up(l, base, UP_A // 2, 2 * f)
            down(l, base + UP_A, UP_A, h0)
            up(l, base + UP_A + DOWN, UP_B // 2, None)
            down(l, base + UP_A + DOWN + UP_B, UP_B, h0 + UP_A)
            sum_squares(l, 2 * (2 * f) + 1, SQ_POST[2 * f], SY)

        def proj(l):
            sum_squares(l, 2, SQ_PRE[1], SX)
            pe.wait_ge(*r_ready.nth(l, 2))
            held(pe)
            with pe.Fori(0, 3) as i:
                for j in range(2):
                    wide_unit(l, unit(l, PROJ, i, j), j, SPLIT_PRE[1] if j == 0 else None)
            with pe.Fori(0, 2) as i:
                for j in range(2):
                    begin(unit(l, PROJ + 6, i, j))
                    for t in range(TILES):
                        out = PS[:, 4 * j + t // 2, (t % 2) * 256:(t % 2) * 256 + 256]
                        for k in range(KD):
                            xh, xl = XH[:, k, t * P:(t + 1) * P], XL[:, k, t * P:(t + 1) * P]
                            mm = three(out, xh, xl, WH[:, j, k * 256:(k + 1) * 256],
                                       WL[:, j, k * 256:(k + 1) * 256], k == 0, k == KD - 1)
                    mm.then_inc(unit_done, 1)
            pe.wait_ge(drained, unit(l, PROJ, 0, 9) + 3)

        def wout(l):
            with pe.Fori(0, 2) as i:
                for j in range(2):
                    wide_unit(l, unit(l, WOUT, i, j), j, SPLIT_MIX if j == 0 else None)
            sum_squares(l, 3, SQ_POST[1], SY)

        def mla_prep(l):
            pe.wait_ge(mla_in, (l + 1) * 80)
            held(pe)
            for h in range(H):
                mm = pe.transpose(PS[0:NOPE, h // 4, (h % 4) * P:(h % 4) * P + P], WUK[:, h, :], IDENT[:, :])
            mm.then_inc(wukt_ps.sem, 1)
            pe.wait_ge(*mla_sq.nth(l, 0))
            for h in range(2):
                cut = slice(h * HALF, (h + 1) * HALF)
                for c in range(2):
                    pe.matmul(PS[:, 2 + h, 0:HALF], ONES[:, :], GB[:, c, cut], start=c == 0, stop=c == 1)
            for h in range(2):
                mm = pe.matmul(PS[:, 4 + h, 0:HALF], ONES[:, :], R[:, h * HALF:(h + 1) * HALF],
                               start=True, stop=True)
            mm.then_inc(mla_ms.sem, 1)
            for h in range(2):
                mm = pe.matmul(PS[0:QK, 6 + h, 0:HALF], SWAP[:, :], MISC[0:QK, h * HALF:(h + 1) * HALF],
                               start=True, stop=True)
            mm.then_inc(kswap_ps.sem, 1)
            pe.wait_ge(*cq_ready.nth(l, 0))
            pe.wait_ge(*kpe_ready.nth(l, 0))
            pe.wait_ge(*kper_zero.nth(l, 0))
            for t in range(TILES):
                pe.transpose(psf[:, 6 * 512 + t * P:6 * 512 + (t + 1) * P], CKVT[:, t * P:(t + 1) * P], IDENT[:, :])
            for t in range(TILES):
                mm = pe.transpose(PS[:, 5, t * QK:(t + 1) * QK], KPER[:, t * P:(t + 1) * P],
                                  IDENT[0:QK, 0:QK])
            mm.then_inc(tok_ps.sem, 1)
            pe.wait_ge(*wukt_sb.nth(l, 0))
            for t in range(PT_):
                pe.matmul(PS[:, t, :], CKVT[:, t * P:(t + 1) * P], WUV[:, :], start=True, stop=True)\
                    .then_inc(v_ps.sem, 1)
            pe.wait_ge(*v_sb.nth(l, PT_ - 1))
            pe.wait_ge(*tok_sb.nth(l, 0))

        def head_prep(l, h):
            if h:
                pe.wait_ge(*q_ready.nth(l, h - 1))
                pe.wait_ge(*ql_sb.nth(l, h - 1))
            for half in range(2):
                cut = slice(half * HALF, (half + 1) * HALF)
                for c in range(2):
                    pe.matmul(PS[0:QK, half, 0:HALF], WUQ[:, c, h * QK:(h + 1) * QK], CQ[:, c, cut],
                              start=c == 0, stop=c == 1)
            pe.matmul(PS[0:NOPE, 2, :], WUK[:, h, :], CKVT[:, 0:TP], start=True, stop=True)\
                .then_inc(qk_ps.sem, 1)

        def head_rotate(l, h):
            pe.wait_ge(*qk_sb.nth(l, h))
            for half in range(2):
                mm = pe.matmul(PS[0:QK, half, 0:HALF], SWAP[:, :], QT[:, h % 2, half * HALF:(half + 1) * HALF],
                               start=True, stop=True)
            mm.then_inc(sw_ps.sem, 1)
            pe.matmul(PS[:, 2, 0:P], WUKT[:, h, :], QT[0:NOPE, h % 2, TP:T], start=True, stop=True)\
                .then_inc(ql_ps.sem, 1)

        def attend_scores(l, n):
            h, i = divmod(n, PT_)
            if i == 0:
                pe.wait_ge(*q_ready.nth(l, h))
                if h == 0:
                    pe.wait_ge(*kt_rope.nth(l, 0))
            if n >= 2:
                pe.wait_ge(*exp_sb.nth(l, n - 2))
            pe.matmul(PS[:, 3 + n % 2, 0:(i + 1) * P], QT[:, h % 2, i * P:(i + 1) * P],
                      KT[:, h % 2, 0:(i + 1) * P], start=True, stop=True).then_inc(s_ps.sem, 1)

        def attend_transpose(l, n):
            h, i = divmod(n, PT_)
            pe.wait_ge(*p_sb.nth(l, n))
            if n >= 2:
                pe.wait_ge(*pt_sb.nth(l, n - 2))
            for k in range(i + 1):
                mm = pe.transpose(PS[:, 5 + n % 2, k * P:(k + 1) * P], PB[:, n % 2, k * P:(k + 1) * P], IDENT[:, :])
            mm.then_inc(t_ps.sem, 1)

        def attend_values(l, n):
            h, i = divmod(n, PT_)
            pe.wait_ge(*pt_sb.nth(l, n))
            if n >= 8 and n % 8 == 0:
                pe.wait_ge(*o_sb.nth(l, n // 8 - 1))
            row = 64 * (h % 2)
            for k in range(i + 1):
                mm = pe.matmul(PS[row:row + 64, 7, i * P:(i + 1) * P], VM[:, k, h * 64:(h + 1) * 64],
                               PTB[:, n % 2, k * P:(k + 1) * P], start=k == 0, stop=k == i)
            mm.then_inc(pv_ps.sem, 1)

        def stream_keys(l, b):
            c = b % CBUF
            pe.wait_ge(cache_in[c], (l * CACHE_TURNS[c] + (b // CBUF + 1)) * 32)
            if b:
                pe.wait_ge(*ct_sb.nth(l, b - 1))
            for k in range(4):
                pe.transpose(PS[:, 0, k * P:(k + 1) * P], CC[:, c, k, :], IDENT[:, :])
            for k in range(4):
                mm = pe.transpose(PS[0:ROPE, 1, k * P:(k + 1) * P], CK[:, c, k, :], IDENT[:, :])
            mm.then_inc(ct_ps.sem, 1)

        def stream_scores(l, b):
            pe.wait_ge(*ct_sb.nth(l, b))
            if b >= 2:
                pe.wait_ge(*sexp_sb.nth(l, b - 2))
            if b >= 3:
                pe.wait_ge(*ol_sb.nth(l, b - 3))
            ql = QLAT[:, b, :, :].rearrange("c h t -> c (h t)")
            qp = QPE[:, b, :, :].rearrange("c h t -> c (h t)")
            bank = 4 + 2 * (b % 2)
            pe.matmul(PS[:, bank, :], ql, CT[:, b % 2, :], start=True, stop=False)
            pe.matmul(PS[:, bank, :], qp, KPT[0:ROPE, b % 2, 0:PAST], start=False, stop=True)
            pe.matmul(PS[:, bank + 1, 0:TS], ql, CKVT[:, TP + b * TS:TP + (b + 1) * TS], start=True, stop=False)
            pe.matmul(PS[:, bank + 1, 0:TS], qp, KN[:, b * TS:(b + 1) * TS], start=False, stop=True)\
                .then_inc(ss_ps.sem, 1)

        def stream_transpose(l, b):
            pe.wait_ge(*sp_sb.nth(l, b))
            if b:
                pe.wait_ge(*spt_sb.nth(l, b - 1))
            for k in range(4):
                pe.transpose(PS[:, 2, k * P:(k + 1) * P], SP[:, b % 2, k * P:(k + 1) * P], IDENT[:, :])
            pe.transpose(PS[:, 3, 0:P], PNEW[:, b, :], IDENT[:, :]).then_inc(spt_ps.sem, 1)

        def stream_values(l, b):
            pe.wait_ge(*spt_sb.nth(l, b))
            for k in range(5):
                keys = CC[:, b % CBUF, k, :] if k < 4 else CTOK[:, PT_, :]
                mm = pe.matmul(latent_out(b), keys, SPT[:, b % 2, k * P:(k + 1) * P],
                               start=k == 0, stop=k == 4)
            mm.then_inc(spv_ps.sem, 1)

        def mla(l):
            mla_prep(l)
            head_prep(l, 0)
            head_rotate(l, 0)
            attend_scores(l, 0)
            attend_scores(l, 1)
            attend_transpose(l, 0)
            for n in range(NT):
                if n % PT_ == 0 and n // PT_ + 1 < H:
                    head_prep(l, n // PT_ + 1)
                if n % PT_ == 1 and n // PT_ + 1 < H:
                    head_rotate(l, n // PT_ + 1)
                if n + 2 < NT:
                    attend_scores(l, n + 2)
                if n + 1 < NT:
                    attend_transpose(l, n + 1)
                attend_values(l, n)
            pe.wait_ge(*ql_sb.nth(l, H - 1))
            pe.wait_ge(*o_sb.nth(l, H // 2 - 1))
            pe.wait_ge(*pn_zero.nth(l, 0))
            pe.wait_ge(*kn_sb.nth(l, 0))
            stream_keys(l, 0)
            stream_scores(l, 0)
            stream_keys(l, 1)
            stream_transpose(l, 0)
            stream_scores(l, 1)
            for b in range(NSEQ):
                if b + 2 < NSEQ:
                    stream_keys(l, b + 2)
                if b + 1 < NSEQ:
                    stream_transpose(l, b + 1)
                if b + 2 < NSEQ:
                    stream_scores(l, b + 2)
                stream_values(l, b)
            pe.wait_ge(*ol_sb.nth(l, NSEQ - 1))
            for h in range(H):
                row = 64 * (h % 2)
                mm = pe.matmul(PS[row:row + 64, 0, (h // 2) * P:(h // 2 + 1) * P], WUV[:, h * 64:(h + 1) * 64],
                               OLAT[:, h, :], start=True, stop=True)
            mm.then_inc(uo_ps.sem, 1)

        def mlstm(l):
            pe.wait_ge(*mla_done.nth(l, 0))
            pe.wait_ge(ml_in, (l + 1) * 240)
            held(pe)
            for c in range(4):
                mm = pe.transpose(PS[:, 0, c * 24:(c + 1) * 24], SC[:, c * P:(c + 1) * P], IDENT[0:24, 0:24])
            mm.then_inc(cs_ps.sem, 1)
            for c in range(4):
                pe.transpose(PS[0:3, 1, c * P:(c + 1) * P], EXTP[:, c, TP:TP + 3], IDENT[:, :])
            pe.wait_ge(*cnt_sb.nth(l, 0))
            for c in range(4):
                mm = pe.transpose(PS[0:24, 2, c * P:(c + 1) * P], CNT[:, c, :], IDENT[:, :])
            mm.then_inc(cn_ps.sem, 1)
            pe.wait_ge(*ge_sb.nth(l, 0))
            pe.wait_ge(*ext_sb.nth(l, 0))
            pe.wait_ge(*cn_sb.nth(l, 0))
            for t in range(TILES):
                pe.transpose(psf[:, t * P:(t + 1) * P], G3[:, t * P:(t + 1) * P], IDENT[:, :])
            for h in range(MH):
                mm = pe.matmul(PS[:, 2, h * 12:(h + 1) * 12], SEL[:, h, :], WIE[:, :], start=True, stop=True)
            mm.then_inc(gt_ps.sem, 1)
            pe.wait_ge(*gt_sb.nth(l, 0))
            pe.wait_ge(*qk_final.nth(l, 0))

            def intra(t):
                if t:
                    pe.wait_ge(*arg_sb.nth(l, t - 1))
                for h in range(MH):
                    mm = pe.matmul(PS[:, 2, h * P:(h + 1) * P], SEL[:, h, :], UB[0:MH, 1, t * P:(t + 1) * P],
                                   start=True, stop=True)
                mm.then_inc(nb_ps.sem, 1)
                if t:
                    pe.wait_ge(*wt_sb.nth(l, t - 1))
                    pe.wait_ge(*kw_sb.nth(l, t - 1))
                for h in range(MH):
                    rows = slice(64 * (h % 2), 64 * (h % 2) + 64)
                    pe.matmul(PS[:, 1 + 2 * (h % 2), h // 2 * P:h // 2 * P + P], QKC[rows, 2 + h // 2, t * P:(t + 1) * P],
                              QKC[rows, h // 2, t * P:(t + 1) * P], start=True, stop=True)
                for g in range(2):
                    mm = pe.transpose(PS[:, 0, g * P:(g + 1) * P], QKC[:, 2 + g, t * P:(t + 1) * P], IDENT[:, :])
                mm.then_inc(mk_ps.sem, 1)

            intra(0)
            for t in range(TILES):
                if t:
                    pe.wait_ge(*ni_sb.nth(l, t - 1))
                if t < PT_:
                    if t:
                        pe.wait_ge(*cst_sb.nth(l, t - 1))
                    for g in range(2):
                        pe.matmul(PS[:, 4, g * 130:(g + 1) * 130], QKC[:, g, t * P:(t + 1) * P], CST[:, g, :],
                                  start=True, stop=True)
                else:
                    pe.wait_ge(*msk_sb.nth(l, 0))
                    for g in range(2):
                        for b in range(NSEQ):
                            pe.matmul(PS[:, 4, g * 130:(g + 1) * 130], QM[:, g, b, :], CSS[:, g, b, :],
                                      start=b == 0, stop=b == NSEQ - 1)
                pe.wait_ge(*wt_sb.nth(l, t))
                for h in range(MH):
                    mm = pe.matmul(PS[:, 5, h * AUG:(h + 1) * AUG], WT[:, h, :], VA[:, t, h, :],
                                   start=True, stop=True)
                mm.then_inc(mo_ps.sem, 1)
                pe.wait_ge(*kw_sb.nth(l, t))
                kw = KW[:, :, :].rearrange("p h d -> p (h d)")
                if t < PT_:
                    for g in range(2):
                        mm = pe.matmul(PS[:, 6, g * 130:(g + 1) * 130], kw[:, g * P:(g + 1) * P],
                                       VA[:, t, 2 * g:2 * g + 2, :], start=True, stop=True)
                    mm.then_inc(upd_ps.sem, 1)
                else:
                    for g in range(2):
                        if g:
                            pe.wait_ge(*csu_sb.nth(l, 0))
                        for k in range(3):
                            b0, b1 = 3 * k, min(3 * k + 3, NSEQ)
                            mm = pe.matmul(PS[:, 1 + k, 0:(b1 - b0) * 130], kw[:, g * P:(g + 1) * P],
                                           VMSK[:, b0:b1, g * 130:(g + 1) * 130], start=True, stop=True)
                        mm.then_inc(csu_ps.sem, 1)
                if t + 1 < TILES:
                    intra(t + 1)
                pe.wait_ge(*hm_sb.nth(l, t))
                if t:
                    pe.wait_ge(*hmt_sb.nth(l, t - 1))
                for g in range(2):
                    mm = pe.transpose(PS[:, 7, g * P:(g + 1) * P], HM[:, g * P:(g + 1) * P], IDENT[:, :])
                mm.then_inc(hmt_ps.sem, 1)

        def hgrn(l):
            m = 0
            pe.wait_ge(*hmt_sb.nth(l, TILES - 1))
            pe.wait_ge(*csu_sb.nth(l, 1))
            for n in range(NLEV):
                pe.wait_ge(*hq_sb.nth(l, n))
                for t in range(PT_ if n < 3 else TILES):
                    if m >= 3:
                        pe.wait_ge(*lv_sb.nth(l, m - 3))
                    cut = slice(t * P, (t + 1) * P)
                    for h in range(MH):
                        rows = slice(64 * (h % 2), 64 * (h % 2) + 64)
                        if n < NLEV - 1:
                            k_, q_ = QKL[n % 2][rows, h // 2, cut], QKL[n % 2][rows, h // 2, cut]
                        else:
                            k_, q_ = KK[rows, h // 2, cut], HQ[rows, h // 2, cut]
                        mm = pe.matmul(PS[:, 2 * (m % 3) + h % 2, h // 2 * P:h // 2 * P + P], k_, q_,
                                       start=True, stop=True)
                    mm.then_inc(lv_ps.sem, 1)
                    m += 1
            pe.wait_ge(*lv_sb.nth(l, NLV - 1))
            pe.wait_ge(*kd_sb.nth(l, 1))
            pe.wait_ge(*qe_sb.nth(l, 1))
            pe.wait_ge(*hg_zero.nth(l, 0))
            for t in range(TILES):
                cut = slice(t * P, (t + 1) * P)
                if t:
                    pe.wait_ge(*kdt_sb.nth(l, t - 1))
                for g in range(2):
                    mm = pe.transpose(PS[:, 0, g * P:(g + 1) * P], KDF[:, g, cut], IDENT[:, :])
                mm.then_inc(kdt_ps.sem, 1)
                if t:
                    pe.wait_ge(*oo_sb.nth(l, t - 1))
                if 0 < t < PT_:
                    pe.wait_ge(*st_sb.nth(l, t - 1))
                if t == PT_:
                    pe.wait_ge(*hmsk_sb.nth(l, 0))
                for h in range(MH):
                    pe.matmul(PS[:, 1, h * DK:(h + 1) * DK], AT[:, t, h % 2, h // 2, :], HI[:, t, h, :],
                              start=h == 0, stop=False, skip_group_check=True)
                for g in range(2):
                    out = PS[:, 1, g * P:(g + 1) * P]
                    if t < PT_:
                        mm = pe.matmul(out, QE[:, g, cut], ST[:, g, :], start=False, stop=True, skip_group_check=True)
                    else:
                        for b in range(NSEQ):
                            mm = pe.matmul(out, QM2[:, g, b, :], SS[:, g, b, :], start=False,
                                           stop=b == NSEQ - 1, skip_group_check=True)
                mm.then_inc(ho_ps.sem, 1)
                pe.wait_ge(*kdt_sb.nth(l, t))
                hi = HI[:, t, :, :].rearrange("p h d -> p (h d)")
                if t < PT_:
                    for g in range(2):
                        mm = pe.matmul(PS[:, 2, g * P:(g + 1) * P], KDT[:, g * P:(g + 1) * P],
                                       hi[:, g * P:(g + 1) * P], start=True, stop=True)
                    mm.then_inc(hup_ps.sem, 1)
                else:
                    pe.wait_ge(*st_sb.nth(l, PT_ - 1))
                    for g in range(2):
                        for k in range(2):
                            mm = pe.matmul(PS[:, 2 + 2 * g + k, :], KDT[:, g * P:(g + 1) * P],
                                           IM[:, 4 * k:4 * k + 4, g * P:(g + 1) * P], start=True, stop=True)
                        mm.then_inc(hup_ps.sem, 1)
                pe.wait_ge(*oo_sb.nth(l, t))
                if t:
                    pe.wait_ge(*hot_sb.nth(l, t - 1))
                oo = OO[:, :, :].rearrange("p h d -> p (h d)")
                for g in range(2):
                    mm = pe.transpose(PS[:, 7, g * P:(g + 1) * P], oo[:, g * P:(g + 1) * P], IDENT[:, :])
                mm.then_inc(hot_ps.sem, 1)
            pe.wait_ge(*hot_sb.nth(l, TILES - 1))
            pe.wait_ge(*st_sb.nth(l, PT_ + 1))
            held(pe)

        pe.sem_inc(unit_done, CREDIT)
        pe.wait_ge(setup_in, 16 * SETUP_LOADS)
        pe.transpose(PS[:, 0, 0:96], PROW[0:96, 0, :], IDENT[0:96, 0:96])
        pe.transpose(PS[:, 0, 96:146], PROW[0:50, 1, :], IDENT[0:50, 0:50])
        pe.matmul(PS[:, 1, 0:LAYERS * DK], ONES[0:1, :], HROW[:, :], start=True, stop=True).then_inc(setup_ps, 1)
        pe.wait_ge(setup_sb, 1)
        for c in range(KD):
            if c >= 4:
                pe.wait_ge(x_init, c - 3)
            for t in range(TILES):
                at = (c % 4) * 1024 + t * P
                mm = pe.transpose(psf[:, at:at + P], XIO[:, t, c * P:(c + 1) * P], IDENT[:, :])
            mm.then_inc(xin_ps, 1)
        pe.wait_ge(x_init, KD)
        with pe.Fori(0, LAYERS) as l:
            ffn(l, 0, FFN0)
            proj(l)
            mla(l)
            mlstm(l)
            hgrn(l)
            wout(l)
            ffn(l, 1, FFN1)
        pe.wait_ge(*x_ready.nth(LAYERS - 1, 23))
        for t in range(TILES):
            if t >= 4:
                pe.wait_ge(y_sb, t - 3)
            for c in range(KD):
                at = (t % 4) * 1024 + c * P
                mm = pe.transpose(psf[:, at:at + P], X[:, c, t * P:(t + 1) * P], IDENT[:, :])
            mm.then_inc(y_ps, 1)

    def spread(ap, n):
        return ap.unsqueeze(2).broadcast_to([ap.shape[0], ap.shape[1], n])

    def over(ap, n):
        return ap.unsqueeze(1).broadcast_to([ap.shape[0], n, ap.shape[1]])

    def two(ap):
        if len(ap.shape) == 3:
            return ap.rearrange("p a (h t) -> p (a h) t", h=2)
        return ap.rearrange("p (h t) -> p h t", h=2)

    def level_end(n):
        return sum(PT_ if k < 3 else TILES for k in range(n + 1))

    def halves_of(h):
        def view(tile_):
            if 2 * h > TS:
                return tile_[:, :, 0:TP].rearrange("p g (n q) -> p g n q", q=2 * h)
            return tile_[:, :, :].rearrange("p g (n q) -> p (g n) q", q=2 * h)

        return (lambda x: view(x)[..., 0:h]), (lambda x: view(x)[..., h:2 * h])

    ENDS_P, ENDS_S = slice(P - 1, TP, P), slice(TP + TS - 1, T, TS)
    TB = GB

    @block.scalar
    def _(act):
        chain = Chain(act, act_chain, ACT_STEPS)

        def run(out, in_, func, **kw):
            return nc.scalar.activation(out, in_, func, **kw)

        def split_hi(l, base, i, j):
            act.wait_ge(loaded[j % 2], turn(l, base + j - j % 2, i, 0))
            act.wait_ge(unit_done, unit(l, base, i, j) + 1)
            run(WH[:, j % 2, :], RAW[:, j % 2, :], ACT.Copy).then_inc(hi_ready, 1)

        def inverse_rms(l, q, n=D):
            act.wait_ge(*ms_ready.nth(l, q))
            chain.link(run(two(R[:, :]), PS[:, 6:8, 0:HALF], ACT.Ln, bias=EPSC[:, 0:1], scale=1.0 / n))
            run(R[:, :], R[:, :], ACT.Exp, scale=-0.5).then_inc(r_ready.sem, 1)

        def square_y(l, i, j, u, sq):
            act.wait_ge(drained, u + 3)
            act.wait_ge(*sq_added.nth(l, sq + 2 * i + j - 2))
            run(two(GB[:, j, :]), two(Y[:, bass.ds(2 * i + j, 1), :]), ACT.Square).then_inc(sq_ready.sem, 1)

        def up(l, base, pairs, h0):
            with act.Fori(0, pairs) as i:
                for j in range(2):
                    split_hi(l, base, i, j + 1)
                    act.wait_ge(*gate_ready.nth(l, 2 * i + (h0 + j)))
                    run(GB[:, j, :], GB[:, j, :], ACT.Silu).then_inc(silu_ready.sem, 1)
                    act.wait_ge(*h_ready.nth(l, 2 * i + (h0 + j)))
                    run(HH[:, bass.ds(2 * i + j, 1), :].rearrange("p a t -> p (a t)"), UB[:, j, :], ACT.Copy)\
                        .then_inc(hh_ready.sem, 1)

        def down(l, base, sq=None):
            with act.Fori(0, DOWN // 2) as i:
                for j in range(2):
                    split_hi(l, base, i, j + 1)
                    if sq is not None:
                        square_y(l, i, j, unit(l, base, i, j), sq)

        def ffn(l, f, base):
            h0 = f * (UP_A + UP_B)
            inverse_rms(l, 4 * f)
            up(l, base, UP_A // 2, h0)
            down(l, base + UP_A)
            up(l, base + UP_A + DOWN, UP_B // 2, h0 + UP_A)
            down(l, base + UP_A + DOWN + UP_B, SQ_POST[2 * f])
            inverse_rms(l, 4 * f + 1)

        def square_x(l, c, pre):
            if c >= 2:
                act.wait_ge(*sq_added.nth(l, SQ_PRE[pre] + c - 2))
            run(GB[:, c % 2, :], X[:, c, :], ACT.Square).then_inc(sq_ready.sem, 1)

        def split_x(l, pre, stage):
            for c in range(KD):
                if stage is not None:
                    act.wait_ge(*x_ready.nth(l, KD * stage + c))
                g = 16 * pre + c
                run(XH[:, c, :], X[:, c, :], ACT.Copy, scale=LP[:, g:g + 1]).then_inc(xh_ready.sem, 1)
                square_x(l, c, pre)

        def split_normalised(l):
            for c in range(KD):
                act.wait_ge(*x_ready.nth(l, c))
                square_x(l, c, 1)
            inverse_rms(l, 2)
            for c in range(KD):
                act.wait_ge(*xt_ready.nth(l, c))
                run(XH[:, c, :], TB[:, c % 2, :], ACT.Copy).then_inc(xh_ready.sem, 1)

        def proj(l):
            for n in range(PROJ_UNITS):
                j = n % 2
                split_hi(l, PROJ + n - j, 0, j + 1)
                if n in (4, 9):
                    act.wait_ge(unit_done, unit(l, PROJ, 0, n) + 3)
                if n == 4:
                    run(HQ[:, :, :].rearrange("p c (h t) -> p (c h) t", h=2), PS[:, 0:4, 0:HALF], ACT.Silu)\
                        .then_inc(proj_sb.sem, 1)
                if n == 9:
                    run(HGG[:, :, :, :].rearrange("p t h v -> p (t h v)"), psf[:, 2048:2048 + 1280], ACT.Silu)\
                        .then_inc(proj_sb.sem, 1)

        def mla(l):
            act.wait_ge(drained, unit(l, PROJ, 0, 9) + 3)
            act.wait_ge(*xl_ready.nth(l, SPLIT_PRE[1] + KD - 1))
            run(GB[:, :, :], CQ[:, :, :], ACT.Square)
            run(R[:, :], CKVT[:, :], ACT.Square).then_inc(mla_sq.sem, 1)
            act.wait_ge(*wukt_ps.nth(l, 0))
            run(WUKT[:, :, :].rearrange("n (a h) c -> n a (h c)", a=2), PS[0:NOPE, 0:2, :], ACT.Copy)\
                .then_inc(wukt_sb.sem, 1)
            act.wait_ge(*mla_ms.nth(l, 0))
            run(two(GB[:, 0, :]), PS[:, 2:4, 0:HALF], ACT.Ln, bias=EPSC[:, 0:1], scale=1.0 / QL)
            chain.link(run(two(GB[:, 1, :]), PS[:, 4:6, 0:HALF], ACT.Ln, bias=EPSC[:, 0:1], scale=1.0 / KVL))
            run(GB[:, :, :], GB[:, :, :], ACT.Exp, scale=-0.5).then_inc(mla_r.sem, 1)
            act.wait_ge(*tok_ps.nth(l, 0))
            run(CTOK[:, :, :].rearrange("p t c -> p (t c)"), psf[:, 6 * 512:6 * 512 + T], ACT.Copy)
            run(R[:, 0:TILES * ROPE].rearrange("p (t c) -> p t c", c=ROPE),
                PS[:, 5, 0:TILES * QK].rearrange("p (t c) -> p t c", c=QK)[:, :, NOPE:QK], ACT.Copy)\
                .then_inc(tok_sb.sem, 1)
            for t in range(PT_):
                act.wait_ge(*v_ps.nth(l, t))
                run(VM[:, t, :], PS[:, t, :], ACT.Copy).then_inc(v_sb.sem, 1)

            def head(h):
                act.wait_ge(*qk_ps.nth(l, h))
                if h >= 2:
                    act.wait_ge(*pv_ps.nth(l, PT_ * (h - 1) - 1))
                run(two(QT[:, h % 2, :]), PS[0:QK, 0:2, 0:HALF], ACT.Copy)
                run(KT[0:NOPE, h % 2, :], PS[0:NOPE, 2, :], ACT.Copy).then_inc(qk_sb.sem, 1)

            def latent_queries(h):
                act.wait_ge(*ql_ps.nth(l, h))
                act.wait_ge(*q_ready.nth(l, h))
                run(QLAT[:, :, h, :], PS[:, 2, 0:P].rearrange("p (b t) -> p b t", t=TS), ACT.Copy)
                run(QPE[:, :, h, :], QT[NOPE:QK, h % 2, TP:T].rearrange("p (b t) -> p b t", t=TS), ACT.Copy).then_inc(ql_sb.sem, 1)

            def probabilities(n):
                i = n % PT_
                act.wait_ge(*nm_sb.nth(l, n))
                if n >= 2:
                    act.wait_ge(*t_ps.nth(l, n - 2))
                run(PB[:, n % 2, 0:(i + 1) * P], PS[:, 3 + n % 2, 0:(i + 1) * P], ACT.Exp,
                    bias=MX[:, n % 2, 1:2], scale=MLA_SCALE, accum_out=MX[:, n % 2, 2:3]).then_inc(exp_sb.sem, 1)

            def transposed(n):
                i = n % PT_
                act.wait_ge(*t_ps.nth(l, n))
                if n >= 2:
                    act.wait_ge(*pv_ps.nth(l, n - 2))
                run(PTB[:, n % 2, 0:(i + 1) * P], PS[:, 5 + n % 2, 0:(i + 1) * P], ACT.Copy).then_inc(pt_sb.sem, 1)

            head(0)
            latent_queries(0)
            probabilities(0)
            probabilities(1)
            transposed(0)
            for n in range(NT):
                if n % PT_ == 0 and n // PT_ + 1 < H:
                    head(n // PT_ + 1)
                if n + 1 < NT:
                    transposed(n + 1)
                if n % PT_ == 1 and n // PT_ + 1 < H:
                    latent_queries(n // PT_ + 1)
                if n % 8 == 7:
                    act.wait_ge(*pv_ps.nth(l, n))
                    run(Y[:, n // 8, 0:TP], PS[:, 7, :], ACT.Copy).then_inc(o_sb.sem, 1)
                if n + 2 < NT:
                    probabilities(n + 2)
            run(KN[:, :], KPER[NOPE:QK, TP:T], ACT.Copy).then_inc(kn_sb.sem, 1)

            def stream_keys(b):
                act.wait_ge(*ct_ps.nth(l, b))
                if b >= 2:
                    act.wait_ge(*ss_ps.nth(l, b - 2))
                run(CT[:, b % 2, :], PS[:, 0, :], ACT.Copy)
                run(KPT[0:ROPE, b % 2, 0:PAST], PS[0:ROPE, 1, :], ACT.Copy).then_inc(ct_sb.sem, 1)

            def stream_exp(b):
                bank = 4 + 2 * (b % 2)
                act.wait_ge(*snm_sb.nth(l, b))
                if b >= 2:
                    act.wait_ge(*spt_ps.nth(l, b - 2))
                run(SP[:, b % 2, :], psf[:, bank * 512:bank * 512 + PAST + TS], ACT.Exp,
                    bias=MX[:, b % 2, 1:2], scale=MLA_SCALE, accum_out=MX[:, b % 2, 2:3]).then_inc(sexp_sb.sem, 1)

            def stream_transposed(b):
                act.wait_ge(*spt_ps.nth(l, b))
                if b >= 2:
                    act.wait_ge(*spv_ps.nth(l, b - 2))
                run(SPT[:, b % 2, :], psf[:, 1024:1024 + T], ACT.Copy).then_inc(spt_sb.sem, 1)

            stream_keys(0)
            stream_keys(1)
            stream_exp(0)
            stream_transposed(0)
            stream_exp(1)
            for b in range(NSEQ):
                if b + 2 < NSEQ:
                    stream_keys(b + 2)
                if b + 1 < NSEQ:
                    stream_transposed(b + 1)
                if b + 2 < NSEQ:
                    stream_exp(b + 2)
            act.wait_ge(*uo_ps.nth(l, 0))
            run(Y[:, 0:4, TP:T], PS[:, 0, :].rearrange("p (c t) -> p c t", t=P), ACT.Copy).then_inc(mla_done.sem, 1)

        def mlstm(l):
            act.wait_ge(*ml_zero.nth(l, 0))
            run(R[0:MH, :], MISC[32:32 + MH, :], ACT.Identity, bias=GBL[32:36, 0:1])
            run(GB[0:MH, 0, :], MISC[0:MH, :], ACT.Identity, bias=GBL[0:4, 0:1]).then_inc(ga_sb.sem, 1)
            act.wait_ge(*cn_ps.nth(l, 0))
            run(Y[0:3, 6, 0:512], PS[0:3, 1, :], ACT.Copy)
            run(Y[0:24, 7, 0:512], PS[0:24, 2, :], ACT.Copy).then_inc(cn_sb.sem, 1)
            act.wait_ge(*conv_sb.nth(l, 0))
            run(QKC[:, :, :], QKC[:, :, :], ACT.Silu).then_inc(csilu_sb.sem, 1)
            act.wait_ge(*gab_sb.nth(l, 0))
            chain.link(run(GB[0:MH, 1, :], GB[0:MH, 1, :], ACT.Exp, scale=-1.0))
            run(GB[0:MH, 1, :], GB[0:MH, 1, :], ACT.Ln, bias=ONES[0:MH, 0:1]).then_inc(gl_sb.sem, 1)
            run(OG[:, :, :], OG[:, :, :], ACT.Exp, scale=-1.0).then_inc(oexp_sb.sem, 1)
            act.wait_ge(*gd_sb.nth(l, 0))
            run(G3[32:36, :], UB[0:MH, 0, :], ACT.Exp)
            run(G3[64:68, :], GB[0:MH, 0, :], ACT.Exp, scale=-1.0)
            run(G3[96:100, :], GB[0:MH, 1, :], ACT.Exp)
            run(WIE[:, 0:PT_], UB[0:MH, 0, ENDS_P], ACT.Exp)
            run(WIE[:, PT_:12], UB[0:MH, 0, ENDS_S], ACT.Exp).then_inc(ge_sb.sem, 1)
            act.wait_ge(*gt_ps.nth(l, 0))
            run(GT[:, :, :].rearrange("p t g -> p (t g)"), psf[:, 0:T], ACT.Copy)
            run(DGB[:, :, :].rearrange("p h n -> p (h n)"), PS[:, 2, 0:48], ACT.Copy).then_inc(gt_sb.sem, 1)
            for t in range(TILES):
                act.wait_ge(*arg_sb.nth(l, t))
                run(DARG[:, :, :], DARG[:, :, :], ACT.Exp).then_inc(wexp_sb.sem, 1)
                if t:
                    out_transposed(l, t - 1, hmt_ps, hmt_sb, 4)
            out_transposed(l, TILES - 1, hmt_ps, hmt_sb, 4)

        def out_transposed(l, t, full, done, chunk):
            act.wait_ge(*full.nth(l, t))
            run(Y[:, chunk:chunk + 2, t * P:(t + 1) * P], PS[:, 7, 0:256].rearrange("p (c t) -> p c t", t=P),
                ACT.Copy).then_inc(done.sem, 1)

        def hgrn(l):
            act.wait_ge(*za_sb.nth(l, 0))
            chain.link(run(DD0[:, :, :], DD0[:, :, :], ACT.Exp, scale=-1.0))
            run(DD0[:, :, :], DD0[:, :, :], ACT.Ln, bias=ONES[:, 0:1]).then_inc(zl_sb.sem, 1)
            act.wait_ge(*zs_sb.nth(l, 0))
            run(KK[:, :, :], KK[:, :, :], ACT.Exp).then_inc(zk_sb.sem, 1)
            act.wait_ge(*zd_sb.nth(l, 0))
            chain.link(run(QK0[:, :, :], QK0[:, :, :], ACT.Exp, scale=-1.0))
            run(QK0[:, :, :], QK0[:, :, :], ACT.Ln, bias=ONES[:, 0:1]).then_inc(ze_sb.sem, 1)
            act.wait_ge(*bc_sb.nth(l, 0))
            act.wait_ge(*hg_zero.nth(l, 0))
            for n in range(NLEV - 1):
                act.wait_ge(*hd_sb.nth(l, n))
                w = TP if n < 3 else T
                run(DD[n % 2][:, :, 0:w], DD[n % 2][:, :, 0:w], ACT.Exp).then_inc(he_sb.sem, 1)
            act.wait_ge(*kd_sb.nth(l, 0))
            run(KDF[:, :, :], KDF[:, :, :], ACT.Exp)
            run(EBL[:, :, 0:PT_], BC[:, :, ENDS_P], ACT.Exp)
            run(EBL[:, :, PT_:12], BC[:, :, ENDS_S], ACT.Exp)
            run(QE[:, :, :], BC[:, :, :], ACT.Exp).then_inc(qe_sb.sem, 1)
            for t in range(TILES):
                act.wait_ge(*kdt_ps.nth(l, t))
                if t:
                    act.wait_ge(*hup_ps.nth(l, t - 1))
                run(KDT[:, :], PS[:, 0, 0:256], ACT.Copy).then_inc(kdt_sb.sem, 1)
                act.wait_ge(*ho_ps.nth(l, t))
                run(OSQ[:, :, :].rearrange("p h v -> p (h v)"), PS[:, 1, 0:256], ACT.Square).then_inc(hsq_sb.sem, 1)
                act.wait_ge(*hrs_sb.nth(l, t))
                chain.link(run(ORM[:, 1, :], ORM[:, 0, :], ACT.Ln, bias=EPSC[:, 0:1], scale=1.0 / DK))
                run(ORM[:, 1, :], ORM[:, 1, :], ACT.Exp, scale=-0.5).then_inc(hr_sb.sem, 1)
                if t == 0:
                    act.wait_ge(cn_stored, 32 * (l + 1))
                out_transposed(l, t, hot_ps, hot_sb, 6)

        def wout(l):
            act.wait_ge(*st_sb.nth(l, PT_ + 1))
            act.wait_ge(*hot_sb.nth(l, TILES - 1))
            act.wait_ge(stored, (l + 1) * (16 * LAYER_STORES))
            for c in range(KD):
                run(XH[:, c, :], Y[:, c, :], ACT.Copy).then_inc(xh_ready.sem, 1)
            for n in range(OUT_UNITS):
                j = n % 2
                split_hi(l, WOUT + n - j, 0, j + 1)
                act.wait_ge(drained, unit(l, WOUT, 0, n) + 3)
                for c in range(2):
                    act.wait_ge(*sq_added.nth(l, SQ_POST[1] + 2 * n + c - 2))
                    run(GB[:, c, :], Y[:, 2 * n + c, :], ACT.Square).then_inc(sq_ready.sem, 1)
            inverse_rms(l, 3)

        split_hi(0, 0, 0, 0)
        for c in range(KD):
            act.wait_ge(xin_ps, c + 1)
            run(X[:, c, :], psf[:, (c % 4) * 1024:(c % 4) * 1024 + T], ACT.Copy).then_inc(x_init, 1)
        act.wait_ge(dve_setup, 5)
        run(LB[:, 2:4, :], LB[:, 2:4, :], ACT.Exp, scale=-1.0).then_inc(act_setup, 1)
        act.wait_ge(act_setup, 1)
        run(LB[:, 2:4, :], LB[:, 2:4, :], ACT.Ln, bias=ONES[:, 0:1]).then_inc(act_setup, 1)
        act.wait_ge(dve_setup, 6)
        run(HB[:, 1, 4:6], HB[:, 1, 2:4], ACT.Exp).then_inc(act_setup, 1)
        with act.Fori(0, LAYERS) as l:
            chain.l = l
            act.wait_ge(*lp_ready.nth(l, 0))
            split_x(l, 0, None)
            ffn(l, 0, FFN0)
            split_normalised(l)
            proj(l)
            mla(l)
            mlstm(l)
            hgrn(l)
            wout(l)
            split_x(l, 2, 1)
            ffn(l, 1, FFN1)
            chain.close()
        act.wait_ge(y_ps, 1)
        for t in range(TILES):
            act.wait_ge(y_ps, t + 1)
            run(XIO[:, t, :], psf[:, (t % 4) * 1024:(t % 4) * 1024 + D], ACT.Copy).then_inc(y_sb, 1)

    @block.vector
    def _(dve):
        chain = Chain(dve, dve_chain, DVE_STEPS)
        V = nc.vector

        def split_lo(l, base, i, j):
            dve.wait_ge(hi_ready, unit(l, base, i, j) + 1)
            V.tensor_tensor(WL[:, j % 2, :], RAW[:, j % 2, :], WH[:, j % 2, :].bitcast(F32), ALU.subtract)\
                .then_inc(lo_ready, 1)

        def up(l, base, pairs, h0):
            with dve.Fori(0, pairs) as i:
                for j in range(2):
                    split_lo(l, base, i, j + 1)
                    u = unit(l, base, i, j)
                    dve.wait_ge(unit_done, u + 3)
                    V.tensor_tensor(two(GB[:, j, :]), PS[:, 4 * j:4 * j + 2, 0:HALF], two(R[:, :]), ALU.mult)\
                        .then_inc(gate_ready.sem, 1)
                    dve.wait_ge(*hl_ready.nth(l, 2 * i + (h0 + j - 2)))
                    V.tensor_tensor(two(UB[:, j, :]), PS[:, 4 * j + 2:4 * j + 4, 0:HALF], two(R[:, :]), ALU.mult)\
                        .then_inc(drained, 1)
                    dve.wait_ge(drained, u + 3)
                    dve.wait_ge(*silu_ready.nth(l, 2 * i + (h0 + j)))
                    V.tensor_tensor(UB[:, j, :], GB[:, j, :], UB[:, j, :], ALU.mult).then_inc(h_ready.sem, 1)

        def down(l, base, add):
            with dve.Fori(0, DOWN // 2) as i:
                for j in range(2):
                    split_lo(l, base, i, j + 1)
                    dve.wait_ge(unit_done, unit(l, base, i, j) + 3)
                    y, ps = two(Y[:, bass.ds(2 * i + j, 1), :]), PS[:, 4 * j:4 * j + 2, 0:HALF]
                    ins = V.tensor_tensor(y, ps, y, ALU.add) if add else V.tensor_copy(y, ps)
                    ins.then_inc(drained, 1)

        def ffn(l, f, base):
            h0 = f * (UP_A + UP_B)
            dve.wait_ge(*r_ready.nth(l, 4 * f))
            held(dve)
            up(l, base, UP_A // 2, h0)
            down(l, base + UP_A, False)
            up(l, base + UP_A + DOWN, UP_B // 2, h0 + UP_A)
            down(l, base + UP_A + DOWN + UP_B, True)

        def lo_of_x(l, pre, c):
            dve.wait_ge(*xh_ready.nth(l, SPLIT_PRE[pre] + c))
            g = 16 * pre + c
            V.scalar_tensor_tensor(out=XL[:, c, :], in0=X[:, c, :], scalar=LP[:, g:g + 1],
                                   in1=XH[:, c, :].bitcast(F32), op0=ALU.mult, op1=ALU.subtract)\
                .then_inc(xl_ready.sem, 1)

        def residual(l, stage, pre):
            dve.wait_ge(*r_ready.nth(l, 2 * stage + 1))
            for c in range(KD):
                g = 16 * stage + 8 + c
                chain.link(V.scalar_tensor_tensor(out=Y[:, c, :], in0=Y[:, c, :], scalar=LP[:, g:g + 1],
                                                  in1=R[:, :], op0=ALU.mult, op1=ALU.mult))
                V.tensor_tensor(X[:, c, :], X[:, c, :], Y[:, c, :], ALU.add).then_inc(x_ready.sem, 1)
                if pre is not None and c:
                    lo_of_x(l, pre, c - 1)
            if pre is not None:
                lo_of_x(l, pre, KD - 1)

        def split_normalised(l):
            dve.wait_ge(*r_ready.nth(l, 2))

            def lo(c):
                dve.wait_ge(*xh_ready.nth(l, SPLIT_PRE[1] + c))
                V.tensor_tensor(XL[:, c, :], TB[:, c % 2, :], XH[:, c, :].bitcast(F32), ALU.subtract)\
                    .then_inc(xl_ready.sem, 1)

            for c in range(KD):
                g = 16 + c
                if c >= 2:
                    dve.wait_ge(*xl_ready.nth(l, SPLIT_PRE[1] + c - 2))
                V.scalar_tensor_tensor(out=TB[:, c % 2, :], in0=X[:, c, :], scalar=LP[:, g:g + 1], in1=R[:, :],
                                       op0=ALU.mult, op1=ALU.mult).then_inc(xt_ready.sem, 1)
                if c:
                    lo(c - 1)
            lo(KD - 1)

        def proj(l):
            for n in range(PROJ_UNITS):
                j = n % 2
                b = 4 * j
                split_lo(l, PROJ + n - j, 0, j + 1)
                if n in (4, 9):
                    dve.wait_ge(*proj_sb.nth(l, n // 9))
                    dve.sem_inc(drained, 1)
                    continue
                dve.wait_ge(unit_done, unit(l, PROJ, 0, n) + 3)
                four, flat = PS[:, b:b + 4, 0:HALF], psf[:, b * 512:b * 512 + 1280]
                if n == 0:
                    ins = V.tensor_copy(CQ[:, :, :].rearrange("p c (h t) -> p (c h) t", h=2), four)
                elif n == 1:
                    V.tensor_copy(two(CKVT[:, :]), PS[:, b:b + 2, 0:HALF])
                    ins = V.tensor_copy(two(MISC[:, :]), PS[:, b + 2:b + 4, 0:HALF])
                elif n in (2, 3):
                    for part in range(2):
                        c, q = 2 * (n - 2) + part, b + 2 * part
                        V.tensor_copy(EXTP[:, c, 3:3 + HALF], PS[:, q, 0:HALF])
                        V.tensor_copy(EXTP[:, c, 3 + HALF:3 + TP], PS[:, q + 1, 0:TP - HALF])
                        ins = V.tensor_copy(EXTS[:, c, :, 3:3 + TS],
                                            PS[:, q + 1, TP - HALF:HALF].rearrange("p (b t) -> p b t", t=TS))
                elif n == 5:
                    ins = V.tensor_copy(HF[:, :, :].rearrange("p c (h t) -> p (c h) t", h=2), four)
                elif n == 6:
                    ins = V.tensor_copy(VA[:, :, :, :].rearrange("p t h a -> p (t h) a")[:, :, 0:DK],
                                        flat.rearrange("p (n v) -> p n v", v=DK))
                elif n == 7:
                    ins = V.tensor_copy(OG[:, :, :].rearrange("p t v -> p (t v)"), flat)
                else:
                    ins = V.tensor_copy(HI[:, :, :, :].rearrange("p t h v -> p (t h v)"), flat)
                ins.then_inc(drained, 1)

        def mla(l):
            R_ = slice(NOPE, QK)
            cos, sin = ROPET[R_, 0, :], ROPET[R_, 1, :]
            dve.wait_ge(*mla_r.nth(l, 0))
            for c in range(2):
                V.scalar_tensor_tensor(out=CQ[:, c, :], in0=CQ[:, c, :], scalar=LP[:, G_Q + c:G_Q + c + 1],
                                       in1=GB[:, 0, :], op0=ALU.mult, op1=ALU.mult)
            V.scalar_tensor_tensor(out=CKVT[:, :], in0=CKVT[:, :], scalar=LP[:, G_KV:G_KV + 1],
                                   in1=GB[:, 1, :], op0=ALU.mult, op1=ALU.mult).then_inc(cq_ready.sem, 1)
            dve.wait_ge(mla_in, (l + 1) * 80)
            dve.wait_ge(*cq_ready.nth(l, 0))
            dve.wait_ge(*kswap_ps.nth(l, 0))
            V.tensor_tensor(KPER[R_, :], MISC[R_, :], cos, ALU.mult)
            chain.link(V.tensor_tensor(two(GB[R_, 0, :]), PS[R_, 6:8, 0:HALF], two(sin), ALU.mult))
            V.tensor_tensor(KPER[R_, :], KPER[R_, :], GB[R_, 0, :], ALU.add).then_inc(kpe_ready.sem, 1)

            def head(h):
                dve.wait_ge(*sw_ps.nth(l, h))
                V.tensor_tensor(two(GB[R_, 0, :]), PS[R_, 0:2, 0:HALF], two(sin), ALU.mult)
                chain.link(V.tensor_tensor(QT[R_, h % 2, :], QT[R_, h % 2, :], cos, ALU.mult))
                V.tensor_tensor(QT[R_, h % 2, :], QT[R_, h % 2, :], GB[R_, 0, :], ALU.add).then_inc(q_ready.sem, 1)

            def maximum(n):
                i = n % PT_
                dve.wait_ge(*s_ps.nth(l, n))
                chain.link(V.memset(PS[0:64, 3 + n % 2, i * P + 64:(i + 1) * P], -FAR))
                chain.link(V.reduce_max(MX[:, n % 2, 0:1], PS[:, 3 + n % 2, 0:(i + 1) * P], AX_X))
                V.tensor_scalar(MX[:, n % 2, 1:2], MX[:, n % 2, 0:1], -MLA_SCALE, None, ALU.mult)\
                    .then_inc(nm_sb.sem, 1)

            def normalise(n):
                i = n % PT_
                dve.wait_ge(*exp_sb.nth(l, n))
                chain.link(V.reciprocal(MX[:, n % 2, 3:4], MX[:, n % 2, 2:3]))
                V.tensor_scalar(PB[:, n % 2, 0:(i + 1) * P], PB[:, n % 2, 0:(i + 1) * P], MX[:, n % 2, 3:4], None,
                                ALU.mult).then_inc(p_sb.sem, 1)

            head(0)
            for n in range(NT):
                if n % PT_ == PT_ - 1 and n // PT_ + 1 < H:
                    head(n // PT_ + 1)
                maximum(n)
                normalise(n)

            def stream_maximum(b):
                bank = 4 + 2 * (b % 2)
                dve.wait_ge(*ss_ps.nth(l, b))
                chain.link(V.reduce_max(MX[:, b % 2, 0:1], psf[:, bank * 512:bank * 512 + PAST + TS], AX_X))
                V.tensor_scalar(MX[:, b % 2, 1:2], MX[:, b % 2, 0:1], -MLA_SCALE, None, ALU.mult)\
                    .then_inc(snm_sb.sem, 1)

            def stream_output(b):
                dve.wait_ge(*spv_ps.nth(l, b))
                V.tensor_copy(OLAT[:, :, b * TS:(b + 1) * TS],
                              latent_out(b).rearrange("p (h t) -> p h t", t=TS)).then_inc(ol_sb.sem, 1)

            dve.wait_ge(*pn_zero.nth(l, 0))
            for b in range(NSEQ):
                stream_maximum(b)
                dve.wait_ge(*sexp_sb.nth(l, b))
                chain.link(V.reciprocal(MX[:, b % 2, 3:4], MX[:, b % 2, 2:3]))
                V.tensor_scalar(PNEW[:, b, b * TS:(b + 1) * TS], SP[:, b % 2, PAST:PAST + TS], MX[:, b % 2, 3:4],
                                None, ALU.mult)
                V.tensor_scalar(SP[:, b % 2, 0:PAST], SP[:, b % 2, 0:PAST], MX[:, b % 2, 3:4], None, ALU.mult)\
                    .then_inc(sp_sb.sem, 1)
                if b >= 1:
                    stream_output(b - 1)
            stream_output(NSEQ - 1)

        def mlstm(l):
            dve.wait_ge(*ml_zero.nth(l, 0))
            V.tensor_copy(CNT[:, :, :].rearrange("p c (b r) -> p c b r", r=3), EXTS[:, :, :, TS:TS + 3])\
                .then_inc(cnt_sb.sem, 1)
            dve.wait_ge(ml_in, (l + 1) * 240)
            dve.wait_ge(*ga_sb.nth(l, 0))
            zf, ab = R[0:MH, :], GB[0:MH, 1, :]
            V.scalar_tensor_tensor(out=ab, in0=zf, scalar=-1.0, in1=zf, op0=ALU.mult, op1=ALU.max)\
                .then_inc(gab_sb.sem, 1)
            dve.wait_ge(*cs_ps.nth(l, 0))
            chain.link(V.tensor_copy(EXTS[:, :, :, 0:3],
                                     PS[:, 0, 0:96].rearrange("p (c b r) -> p c b r", c=4, r=3)))
            dve.sem_inc(ext_sb.sem, 1)
            for tap in range(4):
                for c in range(4):
                    w = LP[:, G_CW + 4 * tap + c:G_CW + 4 * tap + c + 1]
                    for out, in0 in (
                        (QKC[:, c, 0:TP], EXTP[:, c, tap:tap + TP]),
                        (QKC[:, c, TP:T].rearrange("p (b t) -> p b t", t=TS), EXTS[:, c, :, tap:tap + TS]),
                    ):
                        if tap == 0:
                            ins = V.tensor_scalar(out, in0, w, LP[:, G_CB + c:G_CB + c + 1], ALU.mult, ALU.add)
                        else:
                            ins = V.scalar_tensor_tensor(out=out, in0=in0, scalar=w, in1=out,
                                                         op0=ALU.mult, op1=ALU.add)
                if tap < 3:
                    chain.link(ins)
            ins.then_inc(conv_sb.sem, 1)
            lf, bc, a2, li, a = UB[0:MH, 0, :], UB[0:MH, 1, :], UB[0:MH, 0, :], GB[0:MH, 0, :], G3[0:MH, :]
            g, mt = R[0:MH, :], GB[0:MH, 0, :]
            dve.wait_ge(*gl_sb.nth(l, 0))
            chain.link(V.scalar_tensor_tensor(out=lf, in0=zf, scalar=0.0, in1=ab, op0=ALU.min, op1=ALU.subtract))
            chain.link(V.tensor_tensor_scan(bc, GOING[:, :], lf, 0.0, ALU.mult, ALU.add))
            chain.link(V.tensor_tensor(a, li, bc, ALU.subtract))
            V.tensor_copy(a2, a)
            V.tensor_copy(DROP[:, P:TP:P], UB[0:MH, 1, P - 1:TP - 1:P])
            V.memset(MPV[:, 0:1], 0.0)
            chain.link(V.tensor_copy(MPV[:, PT_:12], M0[:, :]))
            chain.link(V.tensor_tensor(UB[0:MH, 0, TP:T:TS], G3[0:MH, TP:T:TS], M0[:, :], ALU.max))
            chain.link(V.tensor_tensor_scan(g, DROP[:, :], a2, 0.0, ALU.add, ALU.max))
            V.tensor_copy(GE[:, 0:PT_], R[0:MH, ENDS_P])
            V.tensor_copy(GE[:, PT_:12], R[0:MH, ENDS_S])
            chain.link(V.tensor_tensor(mt, bc, g, ALU.add))
            chain.link(V.tensor_copy(MPV[:, 1:PT_], GB[0:MH, 0, P - 1:TP - 1:P]))
            for cut, n0, n1, w in ((slice(0, TP), 0, PT_, P), (slice(TP, T), PT_, 12, TS)):
                rows = lambda ap: ap.rearrange("h (n t) -> h n t", t=w)
                V.tensor_tensor(rows(UB[0:MH, 0, cut]), spread(MPV[:, n0:n1], w), rows(R[0:MH, cut]), ALU.subtract)
                V.tensor_tensor(rows(GB[0:MH, 1, cut]), rows(G3[0:MH, cut]), spread(GE[:, n0:n1], w), ALU.subtract)
            V.tensor_scalar(UB[0:MH, 1, :], g, -1.0, None, ALU.mult).then_inc(gd_sb.sem, 1)
            dve.wait_ge(*oexp_sb.nth(l, 0))
            chain.link(V.tensor_scalar(OG[:, :, :], OG[:, :, :], 1.0, None, ALU.add))
            chain.link(V.reciprocal(OG[:, :, :], OG[:, :, :]))
            dve.wait_ge(*gt_sb.nth(l, 0))

            def arguments(t):
                dve.wait_ge(*nb_ps.nth(l, t))
                for h in range(MH):
                    ins = V.scalar_tensor_tensor(out=DARG[:, h, :], in0=PS[:, 2, h * P:(h + 1) * P],
                                                 scalar=GT[:, t, h:h + 1], in1=MASK[:, t // PT_, :],
                                                 op0=ALU.add, op1=ALU.min)
                ins.then_inc(arg_sb.sem, 1)

            def weights(t):
                dve.wait_ge(*wexp_sb.nth(l, t))
                dve.wait_ge(*mk_ps.nth(l, t))
                if t:
                    dve.wait_ge(*mo_ps.nth(l, t - 1))
                by_bank = lambda ap: ap.rearrange("p (g e) t -> p e g t", e=2)
                V.tensor_tensor(by_bank(WT[:, :, :]), by_bank(DARG[:, :, :]),
                                PS[:, 1:4:2, 0:256].rearrange("p e (g t) -> p e g t", t=P),
                                ALU.mult).then_inc(wt_sb.sem, 1)
                if t:
                    dve.wait_ge(*upd_ps.nth(l, t - 1))
                V.tensor_tensor(KW[:, :, :], PS[:, 0, 0:256].rearrange("p (h d) -> p h d", d=DK),
                                spread(GT[:, t, 96:100], DK), ALU.mult).then_inc(kw_sb.sem, 1)

            arguments(0)
            weights(0)
            for t in range(TILES):
                dve.wait_ge(*mo_ps.nth(l, t))
                chain.link(V.tensor_tensor(NI[:, :, :], PS[:, 4, 0:260].rearrange("p (h a) -> p h a", a=AUG),
                                           spread(GT[:, t, 32:36], AUG), ALU.mult))
                V.tensor_tensor(NI[:, :, :], NI[:, :, :], PS[:, 5, 0:260].rearrange("p (h a) -> p h a", a=AUG),
                                ALU.add).then_inc(ni_sb.sem, 1)
                if t < PT_:
                    dve.wait_ge(*upd_ps.nth(l, t))
                    for h in range(MH):
                        rows, cols = slice(64 * (h % 2), 64 * (h % 2) + 64), slice(AUG * (h % 2), AUG * (h % 2) + AUG)
                        ins = V.scalar_tensor_tensor(out=CST[rows, h // 2, cols], in0=CST[rows, h // 2, cols],
                                                     scalar=DGB[rows, h, t:t + 1],
                                                     in1=PS[rows, 6, h * AUG:(h + 1) * AUG],
                                                     op0=ALU.mult, op1=ALU.add)
                    ins.then_inc(cst_sb.sem, 1)
                dve.wait_ge(*ni_sb.nth(l, t))
                chain.link(V.scalar_tensor_tensor(out=DEN[:, 0, :], in0=NI[:, :, DK], scalar=-1.0,
                                                  in1=NI[:, :, DK], op0=ALU.mult, op1=ALU.max))
                chain.link(V.tensor_tensor(DEN[:, 0, :], DEN[:, 0, :], GT[:, t, 64:68], ALU.max))
                chain.link(V.reciprocal(DEN[:, 1, :], DEN[:, 0, :]))
                if t:
                    dve.wait_ge(*hmt_ps.nth(l, t - 1))
                hm = HM[:, :].rearrange("p (h v) -> p h v", v=DK)
                chain.link(V.tensor_tensor(hm, NI[:, :, 0:DK], spread(DEN[:, 1, :], DK), ALU.mult))
                V.tensor_tensor(HM[:, :], HM[:, :], OG[:, t, :], ALU.mult).then_inc(hm_sb.sem, 1)
                if t + 1 < TILES:
                    arguments(t + 1)
                    weights(t + 1)
            for h in range(MH):
                rows, cols = slice(64 * (h % 2), 64 * (h % 2) + 64), slice(AUG * (h % 2), AUG * (h % 2) + AUG)
                ins = V.tensor_tensor(CSS[rows, h // 2, :, cols], CSS[rows, h // 2, :, cols],
                                      spread(DGB[rows, h, PT_:12], AUG), ALU.mult)
            chain.link(ins)
            for g_ in range(2):
                dve.wait_ge(*csu_ps.nth(l, g_))
                for k in range(3):
                    b0, b1 = 3 * k, min(3 * k + 3, NSEQ)
                    for half in range(2):
                        rows, cols = slice(64 * half, 64 * half + 64), slice(AUG * half, AUG * half + AUG)
                        ps = PS[rows, 1 + k, 0:(b1 - b0) * 130].rearrange("p (b n) -> p b n", n=130)[:, :, cols]
                        ins = V.tensor_tensor(CSS[rows, g_, b0:b1, cols], CSS[rows, g_, b0:b1, cols], ps, ALU.add)
                ins.then_inc(csu_sb.sem, 1)

        def hgrn(l):
            dve.wait_ge(*hg_zero.nth(l, 0))
            dve.wait_ge(hg_in, (l + 1) * 96)
            V.scalar_tensor_tensor(out=DD0[:, :, :].rearrange("p g t -> p (g t)"),
                                   in0=HF[:, :, :].rearrange("p g t -> p (g t)"), scalar=-1.0,
                                   in1=HF[:, :, :].rearrange("p g t -> p (g t)"), op0=ALU.mult, op1=ALU.max)\
                .then_inc(za_sb.sem, 1)
            dve.wait_ge(*zl_sb.nth(l, 0))
            chain.link(V.scalar_tensor_tensor(out=BC[:, :, :], in0=HF[:, :, :], scalar=0.0, in1=DD0[:, :, :],
                                              op0=ALU.min, op1=ALU.subtract))
            V.tensor_tensor(KK[:, :, :], BC[:, :, :], HF[:, :, :], ALU.subtract).then_inc(zs_sb.sem, 1)
            dve.wait_ge(*zs_sb.nth(l, 0))
            for g in range(2):
                ins = V.tensor_scalar(BC[:, g, :], BC[:, g, :], HBL[:, 2 + g:3 + g], None, ALU.add)
            chain.link(ins)
            for g in range(2):
                ins = V.tensor_scalar(QK0[:, g, :], BC[:, g, :], HBL[:, g:g + 1], None, ALU.subtract)
            chain.link(ins)
            for g in range(2):
                V.tensor_scalar(BC[:, g, :], BC[:, g, :], HBL[:, g:g + 1], None, ALU.max)
            ins = V.scalar_tensor_tensor(out=QK0[:, :, :], in0=QK0[:, :, :], scalar=-1.0, in1=QK0[:, :, :],
                                         op0=ALU.mult, op1=ALU.max)
            ins.then_inc(zd_sb.sem, 1)
            dve.wait_ge(*ze_sb.nth(l, 0))
            chain.link(V.tensor_tensor(HF[:, :, :], BC[:, :, :], QK0[:, :, :], ALU.add))
            for g in range(2):
                ins = V.tensor_tensor_scan(BC[:, g, :], HGO[:, :], HF[:, g, :], 0.0, ALU.mult, ALU.add)
            ins.then_inc(bc_sb.sem, 1)

            def scaled(n):
                dve.wait_ge(*he_sb.nth(l, n))
                if n == 0:
                    dve.wait_ge(*kk_sb.nth(l, 0))
                if n >= 2:
                    dve.wait_ge(*lv_ps.nth(l, level_end(n - 2) - 1))
                left, right = halves_of(LEVELS[n])
                q, e = QKL[n % 2], DD[n % 2]
                V.tensor_tensor(left(q), left(KK), left(e), ALU.mult)
                V.tensor_tensor(right(q), right(HQ), right(e), ALU.mult).then_inc(hq_sb.sem, 1)

            m = 0
            scaled(0)
            dve.wait_ge(*lvl_sb.nth(l, 0))
            for n in range(NLEV):
                if n + 1 < NLEV - 1:
                    scaled(n + 1)
                elif n + 1 == NLEV - 1:
                    dve.sem_inc(hq_sb.sem, 1)
                for t in range(PT_ if n < 3 else TILES):
                    dve.wait_ge(*lv_ps.nth(l, m))
                    held(dve)
                    V.copy_predicated(AT[:, t, :, :, :],
                                      LVL[:, n, :].unsqueeze(1).unsqueeze(1).broadcast_to([P, 2, 2, P]),
                                      PS[:, 2 * (m % 3):2 * (m % 3) + 2, 0:256].rearrange("p e (g t) -> p e g t", t=P))\
                        .then_inc(lv_sb.sem, 1)
                    dve.wait_ge(*lv_sb.nth(l, m))
                    m += 1
            dve.wait_ge(*qe_sb.nth(l, 0))
            V.tensor_tensor(KDF[:, :, :], KDF[:, :, :], KK[:, :, :], ALU.mult).then_inc(kd_sb.sem, 1)
            V.tensor_tensor(QE[:, :, :], QE[:, :, :], HQ[:, :, :], ALU.mult).then_inc(qe_sb.sem, 1)
            for t in range(TILES):
                dve.wait_ge(*hsq_sb.nth(l, t))
                V.reduce_sum(ORM[:, 0, :], OSQ[:, :, :], AX_X).then_inc(hrs_sb.sem, 1)
                dve.wait_ge(*hr_sb.nth(l, t))
                if t:
                    dve.wait_ge(*hot_ps.nth(l, t - 1))
                chain.link(V.tensor_tensor(OO[:, :, :], PS[:, 1, 0:256].rearrange("p (h v) -> p h v", v=DK),
                                           spread(ORM[:, 1, :], DK), ALU.mult))
                chain.link(V.tensor_tensor(OO[:, :, :], OO[:, :, :], over(HGNL[:, :], MH), ALU.mult))
                V.tensor_tensor(OO[:, :, :], OO[:, :, :], HGG[:, t, :, :], ALU.mult).then_inc(oo_sb.sem, 1)
                if t < PT_:
                    dve.wait_ge(*hup_ps.nth(l, t))
                    for h in range(MH):
                        rows, cols = slice(64 * (h % 2), 64 * (h % 2) + 64), slice(DK * (h % 2), DK * (h % 2) + DK)
                        ins = V.scalar_tensor_tensor(out=ST[rows, h // 2, cols], in0=ST[rows, h // 2, cols],
                                                     scalar=EBL[rows, h // 2, t:t + 1],
                                                     in1=PS[rows, 2, h * DK:(h + 1) * DK],
                                                     op0=ALU.mult, op1=ALU.add)
                    ins.then_inc(st_sb.sem, 1)
            for h in range(MH):
                rows, cols = slice(64 * (h % 2), 64 * (h % 2) + 64), slice(DK * (h % 2), DK * (h % 2) + DK)
                ins = V.tensor_tensor(SS[rows, h // 2, :, cols], SS[rows, h // 2, :, cols],
                                      spread(EBL[rows, h // 2, PT_:12], DK), ALU.mult)
            chain.link(ins)
            for g in range(2):
                dve.wait_ge(*hup_ps.nth(l, PT_ + g))
                for half in range(2):
                    rows, cols = slice(64 * half, 64 * half + 64), slice(DK * half, DK * half + DK)
                    for k in range(2):
                        ps = PS[rows, 2 + 2 * g + k, :].rearrange("p (b n) -> p b n", n=P)[:, :, cols]
                        ss = SS[rows, g, 4 * k:4 * k + 4, cols]
                        ins = V.tensor_tensor(ss, ss, ps, ALU.add)
                ins.then_inc(st_sb.sem, 1)

        def wout(l):
            for c in range(KD):
                dve.wait_ge(*xh_ready.nth(l, SPLIT_MIX + c))
                V.tensor_tensor(XL[:, c, :], Y[:, c, :], XH[:, c, :].bitcast(F32), ALU.subtract)\
                    .then_inc(xl_ready.sem, 1)
            for n in range(OUT_UNITS):
                j = n % 2
                split_lo(l, WOUT + n - j, 0, j + 1)
                dve.wait_ge(unit_done, unit(l, WOUT, 0, n) + 3)
                if n == 0:
                    dve.wait_ge(*xl_ready.nth(l, SPLIT_MIX + KD - 1))
                V.tensor_copy(Y[:, 2 * n:2 * n + 2, :].rearrange("p c (h t) -> p (c h) t", h=2),
                              PS[:, 4 * j:4 * j + 4, 0:HALF]).then_inc(drained, 1)

        dve.sem_inc(lo_ready, CREDIT)
        dve.sem_inc(drained, CREDIT)
        V.memset(EPSC[:, :], EPS)
        V.memset(HB[:, 0, 0:2], -FAR)
        V.memset(HB[:, 0, 2:4], 0.0)
        V.memset(HB[:, 0, 4:6], 1.0).then_inc(dve_setup, 1)
        dve.wait_ge(setup_ps, 1)
        V.tensor_copy(PAR[:, :], PS[:, 0, 0:PAR.shape[1]]).then_inc(dve_setup, 1)
        V.tensor_copy(HGN[:, :, :].rearrange("p l v -> p (l v)"), PS[:, 1, 0:LAYERS * DK]).then_inc(setup_sb, 1)
        b0 = LAYERS * G_END
        dve.wait_ge(dve_setup, 2)
        V.tensor_tensor(LB[:, 0, :], PAR[:, b0 + 2:b0 + 4], PAR[:, b0:b0 + 2], ALU.subtract).then_inc(dve_setup, 1)
        dve.wait_ge(dve_setup, 3)
        V.tensor_scalar(LB[:, 1, :], LB[:, 0, :], -1.0, None, ALU.mult).then_inc(dve_setup, 1)
        dve.wait_ge(dve_setup, 4)
        V.tensor_tensor(LB[:, 2, :], LB[:, 0, :], LB[:, 1, :], ALU.max)
        V.tensor_tensor(LB[:, 3, :], LB[:, 0, :], LB[:, 1, :], ALU.max).then_inc(dve_setup, 1)
        dve.wait_ge(act_setup, 2)
        V.scalar_tensor_tensor(out=HB[:, 1, 0:4].rearrange("p (a b) -> p a b", b=2), in0=LB[:, 0:2, :], scalar=0.0,
                               in1=LB[:, 2:4, :], op0=ALU.min, op1=ALU.subtract).then_inc(dve_setup, 1)
        dve.wait_ge(act_setup, 3)
        dve.wait_ge(hi_ready, 1)
        V.tensor_tensor(WL[:, 0, :], RAW[:, 0, :], WH[:, 0, :].bitcast(F32), ALU.subtract).then_inc(lo_ready, 1)
        dve.wait_ge(setup_sb, 1)
        dve.wait_ge(x_init, KD)
        with dve.Fori(0, LAYERS) as l:
            chain.l = l
            V.tensor_copy(LP[:, 0:G_Q], PAR[:, bass.ds(l * G_Q, G_Q)])
            V.tensor_copy(LP[:, G_Q:G_END], PAR[:, bass.ds(l * NB_COLS + LAYERS * G_Q, NB_COLS)])
            V.tensor_copy(GBL[0:4, :], GBIAS[0:4, bass.ds(l, 1)])
            V.tensor_copy(GBL[32:36, :], GBIAS[32:36, bass.ds(l, 1)])
            V.tensor_copy(HGNL[:, :], HGN[:, bass.ds(l, 1), :].rearrange("p a v -> p (a v)"))
            chain.link(V.tensor_copy(HBL[:, :], HB[:, bass.ds(l, 1), :].rearrange("p a v -> p (a v)")))
            for j in (1, 5):
                ins = V.tensor_scalar(LP[:, 8 * j:8 * j + 8], LP[:, 8 * j:8 * j + 8], 0.5, None, ALU.mult)
            ins.then_inc(lp_ready.sem, 1)
            for c in range(KD):
                lo_of_x(l, 0, c)
            ffn(l, 0, FFN0)
            residual(l, 0, None)
            split_normalised(l)
            proj(l)
            mla(l)
            mlstm(l)
            hgrn(l)
            wout(l)
            residual(l, 1, 2)
            ffn(l, 1, FFN1)
            residual(l, 2, None)
            chain.close()

    @block.gpsimd
    def _(pool):
        chain = Chain(pool, pool_chain, POOL_STEPS)
        G = nc.gpsimd

        def low_h(l, i, j, h0):
            pool.wait_ge(*hh_ready.nth(l, 2 * i + (h0 + j)))
            G.tensor_tensor(HL[:, bass.ds(2 * i + j, 1), :].rearrange("p a t -> p (a t)"), UB[:, j, :],
                            HH[:, bass.ds(2 * i + j, 1), :].rearrange("p a t -> p (a t)").bitcast(F32),
                            ALU.subtract).then_inc(hl_ready.sem, 1)

        def add_square(l, k, j, total):
            pool.wait_ge(*sq_ready.nth(l, k))
            G.tensor_tensor(total, total, GB[:, j, :], ALU.add).then_inc(sq_added.sem, 1)

        def sum_x(l, pre, extra=None):
            pool.wait_ge(*sq_ready.nth(l, SQ_PRE[pre]))
            held(pool)
            G.tensor_copy(SX, GB[:, 0, :]).then_inc(sq_added.sem, 1)
            for c in range(1, KD):
                pool.wait_ge(*sq_added.nth(l, SQ_PRE[pre] + c - 1))
                add_square(l, SQ_PRE[pre] + c, c % 2, SX)

        def ffn(l, f):
            h0 = f * (UP_A + UP_B)
            sum_x(l, 2 * f)
            with pool.Fori(0, UP_A // 2) as i:
                for j in range(2):
                    low_h(l, i, j, h0)
            with pool.Fori(0, UP_B // 2) as i:
                for j in range(2):
                    low_h(l, i, j, h0 + UP_A)
            sum_y(l, 2 * f)

        def sum_y(l, stage):
            pool.wait_ge(*sq_ready.nth(l, SQ_POST[stage]))
            held(pool)
            chain.link(G.memset(SY, 0.0))
            held(pool)
            with pool.Fori(0, KD // 2) as i:
                for j in range(2):
                    k = 2 * i + (SQ_POST[stage] + j)
                    pool.wait_ge(*sq_added.nth(l, k - 1))
                    pool.wait_ge(*sq_ready.nth(l, k))
                    G.tensor_tensor(SY, SY, GB[:, j, :], ALU.add).then_inc(sq_added.sem, 1)

        def load(s, dst, src):
            held(pool)
            pool.dma_start(dst, src).then_inc(s, 16)

        def store(dst, src):
            held(pool)
            pool.dma_start(dst, src).then_inc(stored, 16)

        def mla(l):
            pool.wait_ge(unit_done, unit(l, FFN0, 0, FFN_UNITS - 1) + 3)
            load(mla_in, WUQ[:, :, :], A["mla_w_uq"][l].rearrange("(c p) n -> p c n", p=P))
            load(mla_in, WUK[:, :, :], A["mla_w_uk"][l])
            load(mla_in, WUV[:, :], A["mla_w_uv"][l].rearrange("c h v -> c (h v)"))
            load(mla_in, SWAP[:, :], A["c_swap"])
            held(pool)
            G.memset(KPER[0:NOPE, :], 0.0).then_inc(kper_zero.sem, 1)
            pool.wait_ge(*r_ready.nth(l, 2))
            load(mla_in, UB[NOPE:QK, :, :], A["c_rope"][:, NOPE:QK, :].rearrange("a p t -> p a t"))
            pool.wait_ge(*kpe_ready.nth(l, 0))
            held(pool)
            for j in range(2):
                ins = G.tensor_copy(KT[NOPE:QK, j, :], KPER[NOPE:QK, 0:TP])
            ins.then_inc(kt_rope.sem, 1)
            pool.wait_ge(*tok_sb.nth(l, 0))
            ktok = R[:, 0:TILES * ROPE].rearrange("p (t c) -> p t c", c=ROPE)
            store(O["p_ckv"][l, 0].rearrange("(t p) c -> p t c", p=P), CTOK[:, 0:PT_, :])
            store(O["s_ckv"][l].rearrange("b t c -> (b t) c"), CTOK[:, PT_, :])
            store(O["p_kpe"][l, 0].rearrange("(t p) c -> p t c", p=P), ktok[:, 0:PT_, :])
            store(O["s_kpe"][l].rearrange("b t c -> (b t) c"), ktok[:, PT_, :])
            pool.wait_ge(*pv_ps.nth(l, NT - 1))
            pool.wait_ge(*o_sb.nth(l, H // 2 - 1))

            def cache(b):
                c = b % CBUF
                load(cache_in[c], CC[:, c, :, :], A["cache_ckv"][l, b].rearrange("(k p) c -> p k c", p=P))
                load(cache_in[c], CK[:, c, :, :], A["cache_kpe"][l, b].rearrange("(k p) c -> p k c", p=P))

            cache(0)
            held(pool)
            G.memset(PNEW[:, :, :], 0.0).then_inc(pn_zero.sem, 1)
            for b in range(1, NSEQ):
                if b >= CBUF:
                    pool.wait_ge(*spv_ps.nth(l, b - CBUF))
                cache(b)

        def blocks_of(tile_, w):
            for h in range(MH):
                yield h, slice(64 * (h % 2), 64 * (h % 2) + 64), h // 2, w * (h % 2)

        def mlstm(l):
            pool.wait_ge(*mla_done.nth(l, 0))
            pool.wait_ge(stored, l * (16 * LAYER_STORES) + 16 * 4)
            held(pool)
            chain.link(G.memset(CSS[:, :, :, :], 0.0))
            held(pool)
            G.memset(CST[:, :, :], 0.0)
            G.memset(G3[:, :], 0.0)
            G.memset(QM[:, :, :, :], 0.0)
            G.memset(EXTP[:, :, 0:3], 0.0)
            held(pool)
            chain.link(G.memset(VA[:, :, :, DK:AUG], 1.0))
            pool.sem_inc(ml_zero.sem, 1)
            load(ml_in, SC[:, :], A["state_mlstm_conv"][l].rearrange("b r n -> (b r) n"))
            load(ml_in, M0[:, :], A["state_mlstm_m"][l].rearrange("b h -> h b"))
            load(ml_in, MASK[:, :, :], A["c_mask"])
            load(ml_in, SEL[:, :, :], A["c_select"])
            load(ml_in, GOING[:, :], A["c_going"][0:MH, :])
            load(ml_in, DROP[:, :], A["c_drop"])
            load(ml_in, OWN[:, :], A["c_owner"])
            for h, rows, g, c in blocks_of(CSS, AUG):
                load(ml_in, CSS[rows, g, :, c:c + DK], A["state_mlstm_c"][l, :, h].rearrange("b d v -> d b v"))
                load(ml_in, CSS[rows, g, :, c + DK:c + AUG], A["state_mlstm_n"][l, :, h].rearrange("b (d a) -> d b a", a=1))
            pool.wait_ge(*cn_sb.nth(l, 0))
            held(pool)
            pool.dma_start(O["p_conv"][l, 0], Y[0:3, 6, 0:512]).then_inc(cn_stored, 16)
            pool.dma_start(O["s_conv"][l].rearrange("b r n -> (b r) n"), Y[0:24, 7, 0:512]).then_inc(cn_stored, 16)
            pool.wait_ge(*csilu_sb.nth(l, 0))
            held(pool)
            G.tensor_scalar(QKC[:, 2:4, :], QKC[:, 2:4, :], DK ** -0.5, None, ALU.mult).then_inc(qk_final.sem, 1)
            for b in range(NSEQ):
                G.tensor_copy(QM[:, :, b, b * TS:(b + 1) * TS], QKC[:, 0:2, TP + b * TS:TP + (b + 1) * TS])
            pool.wait_ge(ml_in, (l + 1) * 240)
            G.tensor_tensor(VMSK[:, :, :], over(VA[:, PT_, :, :].rearrange("p h a -> p (h a)"), NSEQ),
                            spread(OWN[:, :], MH * AUG), ALU.mult).then_inc(msk_sb.sem, 1)
            pool.wait_ge(*gd_sb.nth(l, 0))
            store(O["p_m"][l, 0].rearrange("(h a) -> h a", a=1), GB[0:MH, 0, TP - 1:TP])
            store(O["s_m"][l].rearrange("b (h a) -> h b a", a=1), GB[0:MH, 0, ENDS_S].unsqueeze(2))
            pool.wait_ge(*cst_sb.nth(l, PT_ - 1))
            for h, rows, g, c in blocks_of(CST, AUG):
                store(O["p_c"][l, 0, h], CST[rows, g, c:c + DK])
                store(O["p_n"][l, 0, h].rearrange("(d a) -> d a", a=1), CST[rows, g, c + DK:c + AUG])
            pool.wait_ge(*csu_sb.nth(l, 1))
            for h, rows, g, c in blocks_of(CSS, AUG):
                store(O["s_c"][l, :, h].rearrange("b d v -> d b v"), CSS[rows, g, :, c:c + DK])
                store(O["s_n"][l, :, h].rearrange("b (d a) -> d b a", a=1), CSS[rows, g, :, c + DK:c + AUG])

        def hgrn(l):
            pool.wait_ge(*hmt_sb.nth(l, TILES - 1))
            pool.wait_ge(stored, l * (16 * LAYER_STORES) + 16 * 22)
            held(pool)
            chain.link(G.memset(SS[:, :, :, :], 0.0))
            held(pool)
            G.memset(ST[:, :, :], 0.0)
            G.memset(QM2[:, :, :, :], 0.0)
            chain.link(G.memset(AT[:, :, :, :, :], 0.0))
            pool.sem_inc(hg_zero.sem, 1)
            raw_levels = KDF[:, :, :].rearrange("p g t -> p (g t)")[:, 0:NLEV * P].rearrange("p (n t) -> p n t", t=P)
            load(level_in, raw_levels, A["c_level"])
            load(hg_in, HGO[:, :], A["c_going"])
            load(hg_in, OWN2[:, :], A["c_owner"])
            for h, rows, g, c in blocks_of(SS, DK):
                load(hg_in, SS[rows, g, :, c:c + DK], A["state_hgrn"][l, :, h].rearrange("b d v -> d b v"))
            pool.wait_ge(*zk_sb.nth(l, 0))
            held(pool)
            for g in range(2):
                ins = G.tensor_scalar(KK[:, g, :], KK[:, g, :], HBL[:, 4 + g:5 + g], None, ALU.mult)
            ins.then_inc(kk_sb.sem, 1)
            pool.wait_ge(level_in, (l + 1) * 16)
            held(pool)
            G.tensor_copy(LVL[:, :, :], raw_levels).then_inc(lvl_sb.sem, 1)
            pool.wait_ge(*lvl_sb.nth(l, 0))
            pool.wait_ge(*bc_sb.nth(l, 0))
            for n, h in enumerate(LEVELS):
                if n >= 2:
                    pool.wait_ge(*hq_sb.nth(l, n - 2))
                left, right = halves_of(h)
                lb, rb = left(BC), right(BC)
                ref = lb[..., h - 1:h].broadcast_to(list(lb.shape))
                G.tensor_tensor(left(DD[n % 2]), ref, lb, ALU.subtract)
                G.tensor_tensor(right(DD[n % 2]), rb, ref, ALU.subtract).then_inc(hd_sb.sem, 1)
            for cut, w in ((slice(0, TP), P), (slice(TP, T), TS)):
                b = BC[:, :, cut].rearrange("p g (n t) -> p g n t", t=w)
                ins = G.tensor_tensor(KDF[:, :, cut].rearrange("p g (n t) -> p g n t", t=w),
                                      b[..., w - 1:w].broadcast_to(list(b.shape)), b, ALU.subtract)
            ins.then_inc(kd_sb.sem, 1)
            pool.wait_ge(*qe_sb.nth(l, 1))
            held(pool)
            for b in range(NSEQ):
                G.tensor_copy(QM2[:, :, b, b * TS:(b + 1) * TS], QE[:, :, TP + b * TS:TP + (b + 1) * TS])
            pool.wait_ge(hg_in, (l + 1) * 96)
            G.tensor_tensor(IM[:, :, :], over(HI[:, PT_, :, :].rearrange("p h v -> p (h v)"), NSEQ),
                            spread(OWN2[:, :], MH * DK), ALU.mult).then_inc(hmsk_sb.sem, 1)
            pool.wait_ge(*st_sb.nth(l, PT_ - 1))
            for h, rows, g, c in blocks_of(ST, DK):
                store(O["p_hgrn"][l, 0, h], ST[rows, g, c:c + DK])
            pool.wait_ge(*st_sb.nth(l, PT_ + 1))
            for h, rows, g, c in blocks_of(SS, DK):
                store(O["s_hgrn"][l, :, h].rearrange("b d v -> d b v"), SS[rows, g, :, c:c + DK])

        pool.sem_inc(hl_ready.sem, CREDIT)
        with pool.Fori(0, LAYERS) as l:
            chain.l = l
            ffn(l, 0)
            sum_x(l, 1)
            mla(l)
            mlstm(l)
            hgrn(l)
            sum_y(l, 1)
            ffn(l, 1)
            chain.close()

    ctx.close()


_INS = ['x_prompt', 'x_sample', 'cache_ckv', 'cache_kpe', 'state_mlstm_c', 'state_mlstm_n', 'state_mlstm_m',
        'state_mlstm_conv', 'state_hgrn', 'ln_gains', 'w_ffn_in', 'w_ffn_out', 'w_in', 'w_out',
        'mla_q_norm', 'mla_kv_norm', 'mla_w_uq', 'mla_w_uk', 'mla_w_uv', 'ml_conv_w', 'ml_conv_b',
        'ml_gate_bias', 'hg_lb_raw', 'hg_norm']
_OUT_NAMES = ['y_prompt', 'y_sample', 'p_ckv', 'p_kpe', 'p_c', 'p_n', 'p_m', 'p_conv', 'p_hgrn',
              's_ckv', 's_kpe', 's_c', 's_n', 's_m', 's_conv', 's_hgrn']


def _states(b, t):
    return [(LAYERS, b, t, KVL), (LAYERS, b, t, ROPE), (LAYERS, b, MH, DK, DK), (LAYERS, b, MH, DK),
            (LAYERS, b, MH), (LAYERS, b, 3, 2 * MH * DK), (LAYERS, b, MH, DK, DK)]


_OUTS = [((1, TP, D), 'float32'), ((NSEQ, TS, D), 'float32')] + \
    [(s, 'float32') for s in _states(1, TP) + _states(NSEQ, TS)]


def kernel(**inputs):
    import numpy as _np
    import concourse.bacc as _bacc
    from concourse import mybir as _mybir
    from concourse.bass_utils import run_bass_kernel_spmd as _run

    nc = _bacc.Bacc("TRN2", target_bir_lowering=False, num_devices=1)
    arrays, ins, outs = {}, {}, {}
    for name, a in [(n, _np.ascontiguousarray(inputs[n])) for n in _INS] + list(shape_constants().items()):
        arrays[f"in_{name}_dram"] = a
        ins[name] = nc.dram_tensor(f"in_{name}_dram", a.shape, _mybir.dt.from_np(a.dtype), kind="ExternalInput").ap()
    for i, (name, (shape, dtype)) in enumerate(zip(_OUT_NAMES, _OUTS)):
        dt = _mybir.dt.from_np(_np.dtype(dtype))
        outs[name] = nc.dram_tensor(f"out_{i}_dram", shape, dt, kind="ExternalOutput").ap()
    encoder(nc, ins, outs)
    r = _run(nc, [arrays], core_ids=[0])
    return tuple(r.results[0][f"out_{i}_dram"] for i in range(len(_OUTS)))
```

```python
from contextlib import ExitStack

import numpy as np

import concourse.bass as bass
from concourse import mybir

F32 = mybir.dt.float32
F32R = mybir.dt.float32r
U8 = mybir.dt.uint8
ACT = mybir.ActivationFunctionType
ALU = mybir.AluOpType
AX_X = mybir.AxisListType.X

P = 128
LAYERS, D, DFF = 2, 1024, 2816
TP, NSEQ, TS = 512, 8, 16
T = TP + NSEQ * TS
HALF = T // 2
KD = D // P
TILES = T // P
PT_ = TP // P
PAST = 512
CBUF = 4
CACHE_TURNS = [len(range(c, NSEQ, CBUF)) for c in range(CBUF)]
H, NOPE, ROPE, QL, KVL = 8, 64, 32, 256, 128
QK = NOPE + ROPE
MLA_SCALE = float(QK) ** -0.5
MH, DK = 4, 64
AUG = DK + 1
EPS = 1e-6
FAR = 1e30

UP_A, UP_B = 12, 10
DOWN = KD
FFN_UNITS = UP_A + DOWN + UP_B + DOWN
PROJ_UNITS, OUT_UNITS = 10, 4
FFN0 = 0
PROJ = FFN_UNITS
WOUT = PROJ + PROJ_UNITS
FFN1 = WOUT + OUT_UNITS
UNITS = FFN1 + FFN_UNITS
CREDIT = 2
LOAD_INC = 64
C_CQ, C_CKV, C_KPE, C_QK, C_V, C_O, C_I, C_F = 0, 256, 384, 416, 928, 1184, 1440, 1444
C_HQ, C_HF, C_HI, C_HG = 1448, 1704, 1960, 2216
SQ_PRE = {0: 0, 1: 16, 2: 32}
SQ_POST = {0: 8, 1: 24, 2: 40}
SPLIT_PRE = {0: 0, 1: 8, 2: 24}
SPLIT_MIX = 16
G_LN, G_Q, G_KV, G_CW, G_CB, G_END = 0, 48, 50, 51, 67, 71
NB_COLS = G_END - G_Q
LEVELS = (64, 32, 16, 8, 4, 2, 1)
NLEV = len(LEVELS) + 1


def shape_constants():
    inv = (10000.0 ** (-np.arange(0, ROPE, 2, dtype=np.float32) / ROPE)).astype(np.float32)
    pos = np.concatenate([np.arange(TP), np.tile(PAST + np.arange(TS), NSEQ)]).astype(np.float32)
    ang = inv[:, None] * pos[None, :]
    rope = np.zeros((2, QK, T), np.float32)
    rope[0, NOPE:] = np.concatenate([np.cos(ang)] * 2)
    rope[1, NOPE:] = np.concatenate([-np.sin(ang), np.sin(ang)])
    swap = np.zeros((QK, QK), np.float32)
    for j in range(ROPE):
        swap[NOPE + (j + ROPE // 2) % ROPE, NOPE + j] = 1.0
    s, t = np.arange(P)[:, None], np.arange(P)[None, :]
    causal = np.where(s <= t, 0.0, -FAR)
    streams = np.where((s <= t) & (s // TS == t // TS), 0.0, -FAR)
    masks = np.stack([causal, streams], axis=1).astype(np.float32)
    level = np.zeros((P, NLEV, P), np.float32)
    for n, h in enumerate(LEVELS):
        level[:, n] = (s // (2 * h) == t // (2 * h)) & (s % (2 * h) < h) & (t % (2 * h) >= h)
    level[:, NLEV - 1] = s == t
    starts = np.zeros(T, bool)
    starts[0:TP:P] = True
    starts[TP::TS] = True
    going = np.broadcast_to(1.0 - starts.astype(np.float32), (P, T))
    drop = np.zeros((MH, T), np.float32)
    drop[:, TP::TS] = -FAR
    select = np.zeros((MH, MH, P), np.float32)
    for h in range(MH):
        select[h, h] = 1.0
    owner = (np.arange(P)[:, None] // TS == np.arange(NSEQ)[None, :]).astype(np.float32)
    return {"c_rope": rope, "c_swap": swap, "c_mask": masks, "c_level": level,
            "c_going": np.ascontiguousarray(going), "c_drop": drop, "c_select": select, "c_owner": owner,
            "c_ident": np.eye(P, dtype=np.float32), "c_ones": np.ones((P, P), np.float32)}


ACT_STEPS, DVE_STEPS, POOL_STEPS = 15, 164, 4


class Event:

    def __init__(self, sem, per_layer, credit=0):
        self.sem, self.per_layer, self.credit = sem, per_layer, credit

    def nth(self, l, k):
        return self.sem, l * self.per_layer + (k + 1 + self.credit)


class Chain:

    def __init__(self, eng, sem, per_layer):
        self.eng, self.sem, self.per_layer, self.n, self.l = eng, sem, per_layer, 0, 0

    def link(self, ins):
        self.n += 1
        ins.then_inc(self.sem, 1)
        self.eng.wait_ge(self.sem, self.l * self.per_layer + self.n)

    def close(self):
        assert self.n == self.per_layer, (self.n, self.per_layer)


def encoder(nc, A, O):
    ctx = ExitStack()
    ctx.enter_context(nc.allow_non_contiguous_dma(reason="single columns of small states and biases"))

    def tile(stack, name, shape, dt=F32):
        return stack.enter_context(nc.sbuf_tensor(name, shape, dt))

    def sem(name):
        return ctx.enter_context(nc.semaphore(name))

    def event(name, per_layer, credit=0):
        return Event(sem(name), per_layer, credit)

    X = tile(ctx, "x", [P, KD, T])
    Y = tile(ctx, "y", [P, KD, T])
    RAW = tile(ctx, "raw", [P, 2, 2048])
    WH = tile(ctx, "wh", [P, 2, 2048], F32R)
    WL = tile(ctx, "wl", [P, 2, 2048], F32R)
    GB = tile(ctx, "gb", [P, 2, T])
    UB = tile(ctx, "ub", [P, 2, T])
    R = tile(ctx, "r", [P, T])
    IDENT = tile(ctx, "ident", [P, P])
    ONES = tile(ctx, "ones", [P, P])
    PAR = tile(ctx, "par", [P, LAYERS * G_END + 2 * LAYERS])
    LP = tile(ctx, "lp", [P, G_END])
    GBIAS = tile(ctx, "gbias", [36, LAYERS])
    GBL = tile(ctx, "gbl", [36, 1])
    HGN = tile(ctx, "hgn", [P, LAYERS, DK])
    HGNL = tile(ctx, "hgnl", [P, DK])
    HB = tile(ctx, "hb", [P, LAYERS, 6])
    HBL = tile(ctx, "hbl", [P, 6])
    EPSC = tile(ctx, "epsc", [P, 1])
    PS = ctx.enter_context(nc.psum_tensor("ps", [P, 8, 512], F32))
    SY, SX = UB[:, 0, :], UB[:, 1, :]
    psf = PS[:, :, :].rearrange("p b n -> p (b n)")

    s_io = ExitStack()
    XIO = tile(s_io, "xio", [P, TILES, D])
    PROW = tile(s_io, "prow", [P, 2, P])
    HROW = tile(s_io, "hrow", [1, LAYERS * DK])
    LB = tile(s_io, "lb", [P, 4, 2])
    s_io.close()

    s_xn = ExitStack()
    XH = tile(s_xn, "xh", [P, KD, T], F32R)
    XL = tile(s_xn, "xl", [P, KD, T], F32R)
    s_h = ExitStack()
    HH = tile(s_h, "hh", [P, UP_A, T], F32R)
    HL = tile(s_h, "hl", [P, UP_A, T], F32R)
    s_h.close()
    s_hg, s_ml, s_mla = ExitStack(), ExitStack(), ExitStack()
    HI = tile(s_hg, "hi", [P, TILES, MH, DK])
    HGG = tile(s_hg, "hgg", [P, TILES, MH, DK])
    HQ = tile(s_hg, "hq", [P, 2, T])
    HF = tile(s_hg, "hf", [P, 2, T])
    VA = tile(s_ml, "va", [P, TILES, MH, AUG])
    OG = tile(s_ml, "og", [P, TILES, MH * DK])
    EXTP = tile(s_ml, "extp", [P, 4, TP + 3])
    EXTS = tile(s_ml, "exts", [P, 4, NSEQ, TS + 3])
    MISC = tile(s_ml, "misc", [P, T])
    CQ = tile(s_mla, "cq", [P, 2, T])
    CKVT = tile(s_mla, "ckvt", [P, T])
    KPER = tile(s_mla, "kper", [QK, T])
    WUQ = tile(s_mla, "wuq", [P, 2, H * QK])
    WUK = tile(s_mla, "wuk", [P, H, NOPE])
    WUV = tile(s_mla, "wuv", [P, H * 64])
    SWAP = tile(s_mla, "swap", [QK, QK])
    MX = tile(s_mla, "mx", [P, 4, 4])
    s_mla.close()
    VMSK = tile(s_ml, "vmsk", [P, NSEQ, MH * AUG])
    G3 = tile(s_ml, "g3", [P, T])
    MASK = tile(s_ml, "mask", [P, 2, P])
    SEL = tile(s_ml, "sel", [MH, MH, P])
    GOING = tile(s_ml, "going", [MH, T])
    DROP = tile(s_ml, "drop", [MH, T])
    SC = tile(s_ml, "sc", [NSEQ * 3, 512])
    OWN = tile(s_ml, "own", [P, NSEQ])
    CNT = tile(s_ml, "cnt", [P, 4, NSEQ * 3])
    s_ml.close()
    QE = tile(s_hg, "qe", [P, 2, T])
    KDF = tile(s_hg, "kdf", [P, 2, T])
    LVL = tile(s_hg, "lvl", [P, NLEV, P], U8)
    DD0 = tile(s_hg, "dd0", [P, 2, T])
    QK0 = tile(s_hg, "qk0", [P, 2, T])
    DD1 = tile(s_hg, "dd1", [P, 2, T])
    QK1 = tile(s_hg, "qk1", [P, 2, T])
    AT = tile(s_hg, "at", [P, TILES, 2, 2, P])
    s_hg.close()
    s_xn.close()

    s_w = ExitStack()
    QLAT = tile(s_w, "qlat", [P, NSEQ, H, TS])
    QPE = tile(s_w, "qpe", [ROPE, NSEQ, H, TS])
    CTOK = tile(s_w, "ctok", [P, TILES, KVL])
    s_p = ExitStack()
    WUKT = tile(s_p, "wukt", [NOPE, H, P])
    QT = tile(s_p, "qt", [QK, 2, T])
    KT = tile(s_p, "kt", [QK, 2, TP])
    VM = tile(s_p, "vm", [P, PT_, H * 64])
    PB = tile(s_p, "pb", [P, 2, TP])
    PTB = tile(s_p, "ptb", [P, 2, TP])
    s_p.close()
    CC2 = tile(s_w, "cc2", [P, 2, 4, KVL])
    CK2 = tile(s_w, "ck2", [P, 2, 4, ROPE])
    CT = tile(s_w, "ct", [P, 2, PAST])
    SP = tile(s_w, "sp", [P, 2, PAST + TS])
    PNEW = tile(s_w, "pnew", [P, NSEQ, P])
    SPT = tile(s_w, "spt", [P, 2, T])
    OLAT = tile(s_w, "olat", [P, H, P])
    KN = tile(s_w, "kn", [ROPE, P])
    s_w.close()
    ROPET, TMP, KPT = UB, GB[:, 0, :], GB

    s_w = ExitStack()
    QKC = tile(s_w, "qkc", [P, 4, T])
    CST = tile(s_w, "cst", [P, 2, 2 * AUG])
    CSS = tile(s_w, "css", [P, 2, NSEQ, 2 * AUG])
    QM = tile(s_w, "qm", [P, 2, NSEQ, P])
    DGB = tile(s_w, "dgb", [P, MH, 12])
    GT = tile(s_w, "gt", [P, TILES, P])
    DARG = tile(s_w, "darg", [P, MH, P])
    WT = tile(s_w, "wt", [P, MH, P])
    NI = tile(s_w, "ni", [P, MH, AUG])
    HM = tile(s_w, "hm", [P, MH * DK])
    KW = tile(s_w, "kw", [P, MH, DK])
    DEN = tile(s_w, "den", [P, 2, MH])
    M0 = tile(s_w, "m0", [MH, NSEQ])
    MPV = tile(s_w, "mpv", [MH, 12])
    GE = tile(s_w, "ge", [MH, 12])
    WIE = tile(s_w, "wie", [MH, 12])
    s_w.close()

    s_w = ExitStack()
    QM2 = tile(s_w, "qm2", [P, 2, NSEQ, P])
    IM = tile(s_w, "im", [P, NSEQ, MH * DK])
    KDT = tile(s_w, "kdt", [P, MH * DK])
    OO = tile(s_w, "oo", [P, 2, MH, DK])
    OSQ = tile(s_w, "osq", [P, MH, DK])
    ORM = tile(s_w, "orm", [P, 2, MH])
    EBL = tile(s_w, "ebl", [P, 2, 12])
    OWN2 = tile(s_w, "own2", [P, NSEQ])
    work = 2 * (2 * NSEQ * P) + 4 * MH * DK + 2 * MH + 2 * 12 + NSEQ
    states = 2 * P + 2 * NSEQ * P
    tile(s_w, "gap", [P, 2 * KD * T - states - work])
    ST = tile(s_w, "st", [P, 2, P])
    SS = tile(s_w, "ss", [P, 2, NSEQ, P])
    s_w.close()
    y45 = Y[:, 4:6, :].rearrange("p c t -> p (c t)")
    CC = [y45[:, b * 512:(b + 1) * 512].rearrange("p (k c) -> p k c", k=4) for b in range(2)] + \
        [CC2[:, b, :, :] for b in range(2)]
    CK = [y45[:, 1024 + b * P:1024 + (b + 1) * P].rearrange("p (k c) -> p k c", k=4) for b in range(2)] + \
        [CK2[:, b, :, :] for b in range(2)]
    DD, QKL = (DD0, DD1), (QK0, QK1)
    raw_levels = KDF[:, :, :].rearrange("p g t -> p (g t)")[:, 0:NLEV * P].rearrange("p (n t) -> p n t", t=P)
    BC, KK = HF, Y[:, 6:8, :]
    ZA, ZL, ZE = Y[:, 0:2, :], Y[:, 2:4, :], Y[:, 4:6, :]

    loaded = [sem("loaded0"), sem("loaded1")]
    hi_ready = sem("hi_ready")
    lo_ready = sem("lo_ready")
    unit_done = sem("unit_done")
    drained = sem("drained")
    setup_in = sem("setup_in")
    setup_ps, setup_sb = sem("setup_ps"), sem("setup_sb")
    xin_ps, x_init = sem("xin_ps"), sem("x_init")
    lp_ready = event("lp_ready", 1)
    sq_ready = event("sq_ready", 48)
    sq_added = event("sq_added", 48)
    ms_ready = event("ms_ready", 6)
    r_ready = event("r_ready", 6)
    x_ready = event("x_ready", 24)
    xt_ready = event("xt_ready", KD)
    xh_ready = event("xh_ready", 32)
    xl_ready = event("xl_ready", 32)
    n_h = 2 * (UP_A + UP_B)
    gate_ready = event("gate_ready", n_h)
    silu_ready = event("silu_ready", n_h)
    h_ready = event("h_ready", n_h)
    hh_ready = event("hh_ready", n_h)
    hl_ready = event("hl_ready", n_h, 2)
    mla_in = sem("mla_in")
    wukt_ps, wukt_sb = event("wukt_ps", 1), event("wukt_sb", 1)
    proj_sb = event("proj_sb", 2)
    mla_sq, mla_ms, mla_r = event("mla_sq", 1), event("mla_ms", 1), event("mla_r", 1)
    cq_ready, kswap_ps, kpe_ready = event("cq_ready", 1), event("kswap_ps", 1), event("kpe_ready", 1)
    kper_zero, kt_rope = event("kper_zero", 1), event("kt_rope", 1)
    tok_ps, tok_sb = event("tok_ps", 1), event("tok_sb", 1)
    v_ps, v_sb = event("v_ps", PT_), event("v_sb", PT_)
    qk_ps, qk_sb, sw_ps = event("qk_ps", H), event("qk_sb", H), event("sw_ps", H)
    qc_sb = event("qc_sb", H)
    q_ready, ql_ps, ql_sb = event("q_ready", H), event("ql_ps", H), event("ql_sb", H)
    NT = H * PT_
    s_ps, nm_sb, exp_sb = event("s_ps", NT), event("nm_sb", NT), event("exp_sb", NT)
    t_ps, pt_sb = event("t_ps", NT), event("pt_sb", NT)
    pv_ps, on_sb = event("pv_ps", NT), event("on_sb", NT)
    ot_ps, o_sb = event("ot_ps", H // 2), event("o_sb", H // 2)
    cache_in = [sem(f"cache_in{c}") for c in range(CBUF)]
    pn_zero, kn_sb = event("pn_zero", 1), event("kn_sb", 1)
    ct_ps, ct_sb = event("ct_ps", NSEQ), event("ct_sb", NSEQ)
    ss_ps, snm_sb, sexp_sb = event("ss_ps", NSEQ), event("snm_sb", NSEQ), event("sexp_sb", NSEQ)
    sp_sb, spt_ps, spt_sb = event("sp_sb", NSEQ), event("spt_ps", NSEQ), event("spt_sb", NSEQ)
    spv_ps, ol_sb = event("spv_ps", NSEQ), event("ol_sb", NSEQ)
    uo_ps, mla_done = event("uo_ps", 1), event("mla_done", 1)
    ml_in, ml_st = sem("ml_in"), sem("ml_st")
    ext_zero, ml_zero, cst_zero, css_zero = (event(n, 1) for n in ("ext_zero", "ml_zero", "cst_zero", "css_zero"))
    cnt_sb = event("cnt_sb", 1)
    cs_ps, cn_ps, cn_sb = event("cs_ps", 1), event("cn_ps", 1), event("cn_sb", 1)
    ext_sb, conv_sb, csilu_sb = event("ext_sb", 1), event("conv_sb", 2), event("csilu_sb", 2)
    tap_sb = event("tap_sb", 1)
    ga_sb, gab_sb, gl_sb, gd_sb, ge_sb = (event(n, 1) for n in ("ga_sb", "gab_sb", "gl_sb", "gd_sb", "ge_sb"))
    gt_ps, gt_sb, oexp_sb, msk_sb = (event(n, 1) for n in ("gt_ps", "gt_sb", "oexp_sb", "msk_sb"))
    nb_ps, mk_ps, arg_sb, wexp_sb, wt_sb, kw_sb = (
        event(n, TILES) for n in ("nb_ps", "mk_ps", "arg_sb", "wexp_sb", "wt_sb", "kw_sb"))
    mo_ps, ni_sb, hm_sb, hmt_ps, hmt_sb = (
        event(n, TILES) for n in ("mo_ps", "ni_sb", "hm_sb", "hmt_ps", "hmt_sb"))
    cst_sb, upd_ps = event("cst_sb", PT_), event("upd_ps", PT_)
    csu_ps, csu_sb = event("csu_ps", 2), event("csu_sb", 2)
    hg_in = sem("hg_in")
    hg_zero, ss_zero = event("hg_zero", 1), event("ss_zero", 1)
    level_in, lvl_sb = sem("level_in"), event("lvl_sb", 1)
    za_sb, zl_sb, zs_sb, zk_sb, zd_sb, ze_sb, bc_sb = (
        event(n, 1) for n in ("za_sb", "zl_sb", "zs_sb", "zk_sb", "zd_sb", "ze_sb", "bc_sb"))
    kk_sb, hd_sb, he_sb, hq_sb = event("kk_sb", 1), event("hd_sb", 7), event("he_sb", 7), event("hq_sb", 8)
    NLV = 3 * PT_ + 5 * TILES
    lv_ps, lv_sb = event("lv_ps", NLV), event("lv_sb", NLV)
    kd_sb, qe_sb, hmsk_sb = event("kd_sb", 2), event("qe_sb", 2), event("hmsk_sb", 1)
    kdt_ps, kdt_sb, ho_ps, hsq_sb, hrs_sb, hr_sb, oo_sb, hot_ps, hot_sb = (
        event(n, TILES) for n in ("kdt_ps", "kdt_sb", "ho_ps", "hsq_sb", "hrs_sb", "hr_sb", "oo_sb",
                                  "hot_ps", "hot_sb"))
    hup_ps, st_sb = event("hup_ps", PT_ + 2), event("st_sb", PT_ + 2)
    passed = sem("passed")
    cn_stored = sem("cn_stored")
    stored = sem("stored")
    ml_stored = sem("ml_stored")
    y_ps, y_sb, y_stored = sem("y_ps"), sem("y_sb"), sem("y_stored")
    act_chain, dve_chain, pool_chain = sem("act_chain"), sem("dve_chain"), sem("pool_chain")
    act_setup, dve_setup = sem("act_setup"), sem("dve_setup")

    LAYER_STORES = 4 + 2 + 2 * MH
    SETUP_LOADS = 7 + 4 * LAYERS + 2
    block = ctx.enter_context(nc.Block())

    def unit(l, base, i, j):
        return l * UNITS + (base + j) + 2 * i

    def turn(l, base, i, j):
        return (l * (UNITS // 2) + (base // 2 + 1) + i) * LOAD_INC

    def held(eng):
        eng.sem_inc(passed, 1)

    def blocks_of(tile_, w):
        for h in range(MH):
            yield h, slice(64 * (h % 2), 64 * (h % 2) + 64), h // 2, w * (h % 2)

    def hgrn_out(t):
        return PS[:, 1 + 5 * (t % 2), 0:MH * DK]

    def latent_out(b):
        return PS[:, 5 + 2 * ((b + 1) % 2), 256:256 + P]

    @block.sync
    def _(sp):
        def load(u, j, pieces, hold=False):
            sp.wait_ge(lo_ready, u + 1)
            if hold:
                held(sp)
            for dst, src in pieces:
                sp.dma_start(dst, src).then_inc(loaded[j], LOAD_INC // len(pieces))

        def slot(j, n, w):
            return RAW[:, j, 0:n * w].rearrange("p (k n) -> p k n", n=w)

        def up(l, f, base, first, pairs):
            src = A["w_ffn_in"][l, f].rearrange("(k p) n -> p k n", p=P)
            with sp.Fori(0, pairs) as i:
                for j in range(2):
                    at = i * (2 * P) + (first + j) * P
                    load(unit(l, base, i, j), j,
                         [(slot(j, KD, 256)[:, :, g * P:(g + 1) * P], src[:, :, bass.ds(at + g * DFF, P)])
                          for g in range(2)])

        def down(l, f, base, first, n):
            src = A["w_ffn_out"][l, f].rearrange("(k p) n -> p k n", p=P)
            with sp.Fori(0, DOWN // 2) as i:
                for j in range(2):
                    at = i * (2 * P) + j * P
                    load(unit(l, base, i, j), j,
                         [(slot(j, n, P)[:, h * n // 2:(h + 1) * n // 2, :],
                           src[:, first + h * n // 2:first + (h + 1) * n // 2, bass.ds(at, P)])
                          for h in range(2)])

        def ffn(l, f, base):
            up(l, f, base, 0, UP_A // 2)
            down(l, f, base + UP_A, 0, UP_A)
            up(l, f, base + UP_A + DOWN, UP_A, UP_B // 2)
            down(l, f, base + UP_A + DOWN + UP_B, UP_A, UP_B)

        def proj(l):
            src = A["w_in"][l].rearrange("(k p) n -> p k n", p=P)
            for n, c in enumerate((C_HQ, C_HF, C_CQ, None, C_QK, C_QK + 256, C_V, C_O, C_HI, C_HG)):
                j = n % 2
                dst = slot(j, KD, 256)
                if c is None:
                    cuts = [(0, C_CKV, P), (P, C_I, 32), (P + 32, C_F, 32), (P + 64, C_KPE, 64)]
                else:
                    cuts = [(0, c, P), (P, c + P, P)]
                load(unit(l, PROJ, n // 2, j), j,
                     [(dst[:, :, o:o + w], src[:, :, s:s + w]) for o, s, w in cuts], hold=True)

        def mixers(l):
            def bring(s, dst, src):
                held(sp)
                sp.dma_start(dst, src).then_inc(s, 16)

            sp.wait_ge(*mla_done.nth(l, 0))
            bring(ml_in, SC[:, :], A["state_mlstm_conv"][l].rearrange("b r n -> (b r) n"))
            bring(ml_in, M0[:, :], A["state_mlstm_m"][l].rearrange("b h -> h b"))
            bring(ml_in, GOING[:, :], A["c_going"][0:MH, :])
            bring(ml_in, DROP[:, :], A["c_drop"])
            bring(ml_in, SEL[:, :, :], A["c_select"])
            bring(ml_in, MASK[:, :, :], A["c_mask"])
            bring(ml_in, OWN[:, :], A["c_owner"])
            sp.wait_ge(*css_zero.nth(l, 0))
            for h, rows, g, c in blocks_of(CSS, AUG):
                bring(ml_st, CSS[rows, g, :, c:c + DK], A["state_mlstm_c"][l, :, h].rearrange("b d v -> d b v"))
                bring(ml_st, CSS[rows, g, :, c + DK:c + AUG],
                      A["state_mlstm_n"][l, :, h].rearrange("b (d a) -> d b a", a=1))
            sp.wait_ge(*cst_sb.nth(l, PT_ - 1))
            for h, rows, g, c in blocks_of(CST, AUG):
                bring(ml_stored, O["p_c"][l, 0, h], CST[rows, g, c:c + DK])
                bring(ml_stored, O["p_n"][l, 0, h].rearrange("(d a) -> d a", a=1), CST[rows, g, c + DK:c + AUG])
            sp.wait_ge(*csu_sb.nth(l, 1))
            bring(level_in, raw_levels, A["c_level"])
            for h, rows, g, c in blocks_of(CSS, AUG):
                bring(ml_stored, O["s_c"][l, :, h].rearrange("b d v -> d b v"), CSS[rows, g, :, c:c + DK])
                bring(ml_stored, O["s_n"][l, :, h].rearrange("b (d a) -> d b a", a=1), CSS[rows, g, :, c + DK:c + AUG])
            sp.wait_ge(*ss_zero.nth(l, 0))
            bring(hg_in, OWN2[:, :], A["c_owner"])
            for h, rows, g, c in blocks_of(SS, DK):
                bring(hg_in, SS[rows, g, :, c:c + DK], A["state_hgrn"][l, :, h].rearrange("b d v -> d b v"))

        def wout(l):
            src = A["w_out"][l].rearrange("(k p) n -> p k n", p=P)
            for n in range(OUT_UNITS):
                j = n % 2
                load(unit(l, WOUT, n // 2, j), j,
                     [(slot(j, KD, 256)[:, :, g * P:(g + 1) * P], src[:, :, n * 256 + g * P:n * 256 + (g + 1) * P])
                      for g in range(2)])
                if n == 2:
                    mixers(l)

        for dst, src in (
            (XIO[:, 0:PT_, :], A["x_prompt"][0].rearrange("(t p) f -> p t f", p=P)),
            (XIO[:, PT_, :], A["x_sample"].rearrange("b t f -> (b t) f")),
            (PROW[0:96, 0, :], A["ln_gains"].rearrange("l j (c f) -> (l j c) f", f=P)),
            (HROW[:, :], A["hg_norm"].rearrange("l (a v) -> a (l v)", a=1)),
            (IDENT[:, :], A["c_ident"]), (ONES[:, :], A["c_ones"]),
            (GBIAS[0:4, :], A["ml_gate_bias"][:, 0, :].rearrange("l h -> h l")),
            (GBIAS[32:36, :], A["ml_gate_bias"][:, 1, :].rearrange("l h -> h l")),
            (PROW[46:50, 1, :], A["hg_lb_raw"].rearrange("l (c f) -> (l c) f", f=P)),
            *((PROW[b + l * NB_COLS:b + l * NB_COLS + n, 1, :], src) for l in range(LAYERS) for b, n, src in (
                (0, 2, A["mla_q_norm"][l].rearrange("(c f) -> c f", f=P)),
                (2, 1, A["mla_kv_norm"][l].rearrange("(c f) -> c f", f=P)),
                (3, 16, A["ml_conv_w"][l].rearrange("j (c f) -> (j c) f", f=P)),
                (19, 4, A["ml_conv_b"][l].rearrange("(c f) -> c f", f=P)))),
        ):
            sp.dma_start(dst, src).then_inc(setup_in, 16)
        with sp.Fori(0, LAYERS) as l:
            ffn(l, 0, FFN0)
            proj(l)
            wout(l)
            ffn(l, 1, FFN1)
        load(LAYERS * UNITS, 0, [(RAW[:, 0, h * 1024:(h + 1) * 1024],
                                  A["w_ffn_in"][0, 0, 0:P, h * 1024:(h + 1) * 1024]) for h in range(2)])
        for t in range(TILES):
            sp.wait_ge(y_sb, t + 1)
            dst = O["y_prompt"][0, t * P:(t + 1) * P, :] if t < PT_ else O["y_sample"].rearrange("b t f -> (b t) f")
            sp.dma_start(dst, XIO[:, t, :]).then_inc(y_stored, 16)
        sp.wait_ge(y_stored, 16 * TILES)
        sp.wait_ge(stored, 16 * LAYER_STORES * LAYERS)
        sp.wait_ge(cn_stored, 32 * LAYERS)
        sp.wait_ge(ml_stored, 256 * LAYERS)

    @block.tensor
    def _(pe):
        def three(out, wh, wl, xh, xl, first, last):
            pe.matmul(out, wh, xh, start=first, stop=False)
            pe.matmul(out, wh, xl, start=False, stop=False)
            return pe.matmul(out, wl, xh, start=False, stop=last)

        def halves(j, b, k, n, w, col, xh, xl, ncols):
            wh = WH[:, j, k * w + col:k * w + col + P]
            wl = WL[:, j, k * w + col:k * w + col + P]
            for h in range(2):
                mm = three(PS[:, b + h, 0:HALF], wh, wl, xh[:, k, h * HALF:(h + 1) * HALF],
                           xl[:, k, h * HALF:(h + 1) * HALF], k == 0, k == n - 1)
            return mm

        def begin(u):
            pe.wait_ge(lo_ready, u + 3)
            pe.wait_ge(drained, u + 1)

        def wide_unit(l, u, j, split_at):
            begin(u)
            for k in range(KD):
                if split_at is not None:
                    pe.wait_ge(*xl_ready.nth(l, split_at + k))
                for part in range(2):
                    mm = halves(j, 4 * j + 2 * part, k, KD, 256, part * P, XH, XL, None)
            mm.then_inc(unit_done, 1)

        def sum_squares(l, q, sq, total):
            pe.wait_ge(*sq_added.nth(l, sq + KD - 1))
            for h in range(2):
                mm = pe.matmul(PS[:, 6 + h, 0:HALF], ONES[:, :], total[:, h * HALF:(h + 1) * HALF],
                               start=True, stop=True)
            mm.then_inc(ms_ready.sem, 1)

        def up(l, base, pairs, pre):
            if pre is not None:
                wide_unit(l, unit(l, base, 0, 0), 0, SPLIT_PRE[pre])
                sum_squares(l, 2 * pre, SQ_PRE[pre], SX)
                pe.wait_ge(*r_ready.nth(l, 2 * pre))
                wide_unit(l, unit(l, base, 0, 1), 1, None)
            held(pe)
            with pe.Fori(0 if pre is None else 1, pairs) as i:
                for j in range(2):
                    wide_unit(l, unit(l, base, i, j), j, None)

        def down(l, base, n, h_from):
            def narrow_unit(i, j, by_chunk):
                begin(unit(l, base, i, j))
                for k in range(n):
                    if by_chunk:
                        pe.wait_ge(*hl_ready.nth(l, h_from + k))
                    mm = halves(j, 4 * j, k, n, P, 0, HH, HL, None)
                mm.then_inc(unit_done, 1)

            for j in range(2):
                narrow_unit(0, j, j == 0)
            with pe.Fori(1, DOWN // 2) as i:
                for j in range(2):
                    narrow_unit(i, j, False)

        def ffn(l, f, base):
            h0 = f * (UP_A + UP_B)
            up(l, base, UP_A // 2, 2 * f)
            down(l, base + UP_A, UP_A, h0)
            up(l, base + UP_A + DOWN, UP_B // 2, None)
            down(l, base + UP_A + DOWN + UP_B, UP_B, h0 + UP_A)
            sum_squares(l, 2 * (2 * f) + 1, SQ_POST[2 * f], SY)

        def proj(l):
            sum_squares(l, 2, SQ_PRE[1], SX)
            pe.wait_ge(*r_ready.nth(l, 2))
            held(pe)
            with pe.Fori(0, 3) as i:
                for j in range(2):
                    wide_unit(l, unit(l, PROJ, i, j), j, SPLIT_PRE[1] if j == 0 else None)
            with pe.Fori(0, 2) as i:
                for j in range(2):
                    begin(unit(l, PROJ + 6, i, j))
                    for t in range(TILES):
                        out = PS[:, 4 * j + t // 2, (t % 2) * 256:(t % 2) * 256 + 256]
                        for k in range(KD):
                            xh, xl = XH[:, k, t * P:(t + 1) * P], XL[:, k, t * P:(t + 1) * P]
                            mm = three(out, xh, xl, WH[:, j, k * 256:(k + 1) * 256],
                                       WL[:, j, k * 256:(k + 1) * 256], k == 0, k == KD - 1)
                    mm.then_inc(unit_done, 1)
            pe.wait_ge(drained, unit(l, PROJ, 0, 9) + 3)

        def wout(l):
            with pe.Fori(0, 2) as i:
                for j in range(2):
                    wide_unit(l, unit(l, WOUT, i, j), j, SPLIT_MIX if j == 0 else None)
            sum_squares(l, 3, SQ_POST[1], SY)

        def mla_prep(l):
            pe.wait_ge(mla_in, (l + 1) * 80)
            held(pe)
            for h in range(H):
                mm = pe.transpose(PS[0:NOPE, h // 4, (h % 4) * P:(h % 4) * P + P], WUK[:, h, :], IDENT[:, :])
            mm.then_inc(wukt_ps.sem, 1)
            pe.wait_ge(*mla_sq.nth(l, 0))
            for h in range(2):
                cut = slice(h * HALF, (h + 1) * HALF)
                for c in range(2):
                    pe.matmul(PS[:, 2 + h, 0:HALF], ONES[:, :], GB[:, c, cut], start=c == 0, stop=c == 1)
            for h in range(2):
                mm = pe.matmul(PS[:, 4 + h, 0:HALF], ONES[:, :], R[:, h * HALF:(h + 1) * HALF],
                               start=True, stop=True)
            mm.then_inc(mla_ms.sem, 1)
            for h in range(2):
                mm = pe.matmul(PS[0:QK, 6 + h, 0:HALF], SWAP[:, :], MISC[0:QK, h * HALF:(h + 1) * HALF],
                               start=True, stop=True)
            mm.then_inc(kswap_ps.sem, 1)
            pe.wait_ge(*cq_ready.nth(l, 0))
            pe.wait_ge(*kpe_ready.nth(l, 0))
            pe.wait_ge(*kper_zero.nth(l, 0))
            for t in range(TILES):
                pe.transpose(psf[:, 6 * 512 + t * P:6 * 512 + (t + 1) * P], CKVT[:, t * P:(t + 1) * P], IDENT[:, :])
            for t in range(TILES):
                mm = pe.transpose(PS[:, 5, t * QK:(t + 1) * QK], KPER[:, t * P:(t + 1) * P],
                                  IDENT[0:QK, 0:QK])
            mm.then_inc(tok_ps.sem, 1)
            pe.wait_ge(*wukt_sb.nth(l, 0))
            for t in range(PT_):
                pe.matmul(PS[:, t, :], CKVT[:, t * P:(t + 1) * P], WUV[:, :], start=True, stop=True)\
                    .then_inc(v_ps.sem, 1)
            pe.wait_ge(*v_sb.nth(l, PT_ - 1))
            pe.wait_ge(*tok_sb.nth(l, 0))

        def head_prep(l, h):
            if h:
                pe.wait_ge(*q_ready.nth(l, h - 1))
                pe.wait_ge(*ql_sb.nth(l, h - 1))
            if h >= 4 and h % 2 == 0:
                pe.wait_ge(*o_sb.nth(l, h // 2 - 2))
            for half in range(2):
                cut = slice(half * HALF, (half + 1) * HALF)
                for c in range(2):
                    pe.matmul(PS[0:QK, half, 0:HALF], WUQ[:, c, h * QK:(h + 1) * QK], CQ[:, c, cut],
                              start=c == 0, stop=c == 1)
            pe.matmul(PS[0:NOPE, 2, :], WUK[:, h, :], CKVT[:, 0:TP], start=True, stop=True)\
                .then_inc(qk_ps.sem, 1)

        def head_rotate(l, h):
            pe.wait_ge(*qk_sb.nth(l, h))
            for half in range(2):
                mm = pe.matmul(PS[0:QK, half, 0:HALF], SWAP[:, :], QT[:, h % 2, half * HALF:(half + 1) * HALF],
                               start=True, stop=True)
            mm.then_inc(sw_ps.sem, 1)
            pe.matmul(PS[:, 2, 0:P], WUKT[:, h, :], QT[0:NOPE, h % 2, TP:T], start=True, stop=True)\
                .then_inc(ql_ps.sem, 1)

        def attend_scores(l, n):
            h, i = divmod(n, PT_)
            if i == 0:
                pe.wait_ge(*q_ready.nth(l, h))
                if h == 0:
                    pe.wait_ge(*kt_rope.nth(l, 0))
            if n >= 2:
                pe.wait_ge(*exp_sb.nth(l, n - 2))
            pe.matmul(PS[:, 3 + n % 2, 0:(i + 1) * P], QT[:, h % 2, i * P:(i + 1) * P],
                      KT[:, h % 2, 0:(i + 1) * P], start=True, stop=True).then_inc(s_ps.sem, 1)

        def attend_transpose(l, n):
            h, i = divmod(n, PT_)
            pe.wait_ge(*exp_sb.nth(l, n))
            if n:
                pe.wait_ge(*pt_sb.nth(l, n - 1))
            for k in range(i + 1):
                mm = pe.transpose(PS[:, 5, k * P:(k + 1) * P], PB[:, n % 2, k * P:(k + 1) * P], IDENT[:, :])
            mm.then_inc(t_ps.sem, 1)

        def attend_values(l, n):
            h, i = divmod(n, PT_)
            pe.wait_ge(*pt_sb.nth(l, n))
            if n >= 2:
                pe.wait_ge(*on_sb.nth(l, n - 2))
            for k in range(i + 1):
                mm = pe.matmul(PS[:, 6 + n % 2, 0:64], PTB[:, n % 2, k * P:(k + 1) * P],
                               VM[:, k, h * 64:(h + 1) * 64], start=k == 0, stop=k == i)
            mm.then_inc(pv_ps.sem, 1)

        def pair_output(l, pair):
            pe.wait_ge(*on_sb.nth(l, 8 * pair + 7))
            pe.wait_ge(*ql_sb.nth(l, min(2 * pair + 3, H - 1)))
            for t in range(PT_):
                mm = pe.transpose(PS[:, 2, t * P:(t + 1) * P], Y[:, pair, t * P:(t + 1) * P], IDENT[:, :])
            mm.then_inc(ot_ps.sem, 1)

        def stream_keys(l, b):
            c = b % CBUF
            pe.wait_ge(cache_in[c], (l * CACHE_TURNS[c] + (b // CBUF + 1)) * 32)
            if b:
                pe.wait_ge(*ct_sb.nth(l, b - 1))
            for k in range(4):
                pe.transpose(PS[:, 0, k * P:(k + 1) * P], CC[c][:, k, :], IDENT[:, :])
            for k in range(4):
                mm = pe.transpose(PS[0:ROPE, 1, k * P:(k + 1) * P], CK[c][:, k, :], IDENT[:, :])
            mm.then_inc(ct_ps.sem, 1)

        def stream_scores(l, b):
            pe.wait_ge(*ct_sb.nth(l, b))
            if b >= 2:
                pe.wait_ge(*sexp_sb.nth(l, b - 2))
            if b >= 3:
                pe.wait_ge(*ol_sb.nth(l, b - 3))
            ql = QLAT[:, b, :, :].rearrange("c h t -> c (h t)")
            qp = QPE[:, b, :, :].rearrange("c h t -> c (h t)")
            bank = 4 + 2 * (b % 2)
            pe.matmul(PS[:, bank, :], ql, CT[:, b % 2, :], start=True, stop=False)
            pe.matmul(PS[:, bank, :], qp, KPT[0:ROPE, b % 2, 0:PAST], start=False, stop=True)
            pe.matmul(PS[:, bank + 1, 0:TS], ql, CKVT[:, TP + b * TS:TP + (b + 1) * TS], start=True, stop=False)
            pe.matmul(PS[:, bank + 1, 0:TS], qp, KN[:, b * TS:(b + 1) * TS], start=False, stop=True)\
                .then_inc(ss_ps.sem, 1)

        def stream_transpose(l, b):
            pe.wait_ge(*sp_sb.nth(l, b))
            if b:
                pe.wait_ge(*spt_sb.nth(l, b - 1))
            for k in range(4):
                pe.transpose(PS[:, 2, k * P:(k + 1) * P], SP[:, b % 2, k * P:(k + 1) * P], IDENT[:, :])
            pe.transpose(PS[:, 3, 0:P], PNEW[:, b, :], IDENT[:, :]).then_inc(spt_ps.sem, 1)

        def stream_values(l, b):
            pe.wait_ge(*spt_sb.nth(l, b))
            if b >= 2:
                pe.wait_ge(*ol_sb.nth(l, b - 2))
            for k in range(5):
                keys = CC[b % CBUF][:, k, :] if k < 4 else CTOK[:, PT_, :]
                mm = pe.matmul(latent_out(b), keys, SPT[:, b % 2, k * P:(k + 1) * P],
                               start=k == 0, stop=k == 4)
            mm.then_inc(spv_ps.sem, 1)

        def mla(l):
            mla_prep(l)
            head_prep(l, 0)
            head_rotate(l, 0)
            attend_scores(l, 0)
            attend_scores(l, 1)
            attend_transpose(l, 0)
            for n in range(NT):
                if n % PT_ == 0 and n // PT_ + 1 < H:
                    head_prep(l, n // PT_ + 1)
                if n % PT_ == 1 and n // PT_ + 1 < H:
                    head_rotate(l, n // PT_ + 1)
                if n + 2 < NT:
                    attend_scores(l, n + 2)
                if n + 1 < NT:
                    attend_transpose(l, n + 1)
                if n % 8 == 3 and n > 8:
                    pair_output(l, n // 8 - 1)
                attend_values(l, n)
            pair_output(l, H // 2 - 1)
            pe.wait_ge(*o_sb.nth(l, H // 2 - 1))
            pe.wait_ge(*pn_zero.nth(l, 0))
            pe.wait_ge(*kn_sb.nth(l, 0))
            stream_keys(l, 0)
            stream_scores(l, 0)
            stream_keys(l, 1)
            stream_transpose(l, 0)
            stream_scores(l, 1)
            for b in range(NSEQ):
                if b + 2 < NSEQ:
                    stream_keys(l, b + 2)
                if b + 1 < NSEQ:
                    stream_transpose(l, b + 1)
                if b + 2 < NSEQ:
                    stream_scores(l, b + 2)
                stream_values(l, b)
            pe.wait_ge(*ol_sb.nth(l, NSEQ - 1))
            for h in range(H):
                row = 64 * (h % 2)
                mm = pe.matmul(PS[row:row + 64, 0, (h // 2) * P:(h // 2 + 1) * P], WUV[:, h * 64:(h + 1) * 64],
                               OLAT[:, h, :], start=True, stop=True)
            mm.then_inc(uo_ps.sem, 1)

        def mlstm(l):
            pe.wait_ge(*mla_done.nth(l, 0))
            pe.wait_ge(ml_in, (l + 1) * 112)
            held(pe)
            for c in range(4):
                mm = pe.transpose(PS[:, 0, c * 24:(c + 1) * 24], SC[:, c * P:(c + 1) * P], IDENT[0:24, 0:24])
            mm.then_inc(cs_ps.sem, 1)
            for c in range(4):
                pe.transpose(PS[0:3, 1, c * P:(c + 1) * P], EXTP[:, c, TP:TP + 3], IDENT[:, :])
            pe.wait_ge(*cnt_sb.nth(l, 0))
            for c in range(4):
                mm = pe.transpose(PS[0:24, 2, c * P:(c + 1) * P], CNT[:, c, :], IDENT[:, :])
            mm.then_inc(cn_ps.sem, 1)
            pe.wait_ge(*ge_sb.nth(l, 0))
            pe.wait_ge(*ext_sb.nth(l, 0))
            pe.wait_ge(*cn_sb.nth(l, 0))
            for t in range(TILES):
                pe.transpose(psf[:, t * P:(t + 1) * P], G3[:, t * P:(t + 1) * P], IDENT[:, :])
            for h in range(MH):
                mm = pe.matmul(PS[:, 2, h * 12:(h + 1) * 12], SEL[:, h, :], WIE[:, :], start=True, stop=True)
            mm.then_inc(gt_ps.sem, 1)
            pe.wait_ge(*cst_zero.nth(l, 0))
            pe.wait_ge(*ext_zero.nth(l, 0))
            pe.wait_ge(*gt_sb.nth(l, 0))
            pe.wait_ge(*csilu_sb.nth(l, 1))

            def intra(t):
                if t:
                    pe.wait_ge(*arg_sb.nth(l, t - 1))
                for h in range(MH):
                    mm = pe.matmul(PS[:, 2, h * P:(h + 1) * P], SEL[:, h, :], UB[0:MH, 1, t * P:(t + 1) * P],
                                   start=True, stop=True)
                mm.then_inc(nb_ps.sem, 1)
                if t:
                    pe.wait_ge(*wt_sb.nth(l, t - 1))
                    pe.wait_ge(*kw_sb.nth(l, t - 1))
                for h in range(MH):
                    rows = slice(64 * (h % 2), 64 * (h % 2) + 64)
                    pe.matmul(PS[:, 1 + 2 * (h % 2), h // 2 * P:h // 2 * P + P], QKC[rows, 2 + h // 2, t * P:(t + 1) * P],
                              QKC[rows, h // 2, t * P:(t + 1) * P], start=True, stop=True)
                for g in range(2):
                    mm = pe.transpose(PS[:, 0, g * P:(g + 1) * P], QKC[:, 2 + g, t * P:(t + 1) * P], IDENT[:, :])
                mm.then_inc(mk_ps.sem, 1)

            intra(0)
            for t in range(TILES):
                if t:
                    pe.wait_ge(*ni_sb.nth(l, t - 1))
                if t < PT_:
                    if t:
                        pe.wait_ge(*cst_sb.nth(l, t - 1))
                    for g in range(2):
                        pe.matmul(PS[:, 4, g * 130:(g + 1) * 130], QKC[:, g, t * P:(t + 1) * P], CST[:, g, :],
                                  start=True, stop=True)
                else:
                    pe.wait_ge(*msk_sb.nth(l, 0))
                    pe.wait_ge(ml_st, (l + 1) * 128)
                    for g in range(2):
                        for b in range(NSEQ):
                            pe.matmul(PS[:, 4, g * 130:(g + 1) * 130], QM[:, g, b, :], CSS[:, g, b, :],
                                      start=b == 0, stop=b == NSEQ - 1)
                pe.wait_ge(*wt_sb.nth(l, t))
                for h in range(MH):
                    mm = pe.matmul(PS[:, 5, h * AUG:(h + 1) * AUG], WT[:, h, :], VA[:, t, h, :],
                                   start=True, stop=True)
                mm.then_inc(mo_ps.sem, 1)
                pe.wait_ge(*kw_sb.nth(l, t))
                kw = KW[:, :, :].rearrange("p h d -> p (h d)")
                if t < PT_:
                    for g in range(2):
                        mm = pe.matmul(PS[:, 6, g * 130:(g + 1) * 130], kw[:, g * P:(g + 1) * P],
                                       VA[:, t, 2 * g:2 * g + 2, :], start=True, stop=True)
                    mm.then_inc(upd_ps.sem, 1)
                else:
                    for g in range(2):
                        if g:
                            pe.wait_ge(*ni_sb.nth(l, t))
                        for k in range(3):
                            b0, b1 = 3 * k, min(3 * k + 3, NSEQ)
                            mm = pe.matmul(PS[:, 1 + 3 * g + k, 0:(b1 - b0) * 130], kw[:, g * P:(g + 1) * P],
                                           VMSK[:, b0:b1, g * 130:(g + 1) * 130], start=True, stop=True)
                        mm.then_inc(csu_ps.sem, 1)
                if t + 1 < TILES:
                    intra(t + 1)
                pe.wait_ge(*hm_sb.nth(l, t))
                if t:
                    pe.wait_ge(*hmt_sb.nth(l, t - 1))
                for g in range(2):
                    mm = pe.transpose(PS[:, 7, g * P:(g + 1) * P], HM[:, g * P:(g + 1) * P], IDENT[:, :])
                mm.then_inc(hmt_ps.sem, 1)

        def hgrn(l):
            m = 0
            pe.wait_ge(*hmt_sb.nth(l, TILES - 1))
            pe.wait_ge(*csu_sb.nth(l, 1))
            pe.wait_ge(*kk_sb.nth(l, 0))
            for n in range(NLEV):
                pe.wait_ge(*hq_sb.nth(l, n))
                for t in range(PT_ if n < 3 else TILES):
                    if m >= 3:
                        pe.wait_ge(*lv_sb.nth(l, m - 3))
                    cut = slice(t * P, (t + 1) * P)
                    for h in range(MH):
                        rows = slice(64 * (h % 2), 64 * (h % 2) + 64)
                        if n < NLEV - 1:
                            k_, q_ = QKL[n % 2][rows, h // 2, cut], QKL[n % 2][rows, h // 2, cut]
                        else:
                            k_, q_ = KK[rows, h // 2, cut], HQ[rows, h // 2, cut]
                        mm = pe.matmul(PS[:, 2 * (m % 3) + h % 2, h // 2 * P:h // 2 * P + P], k_, q_,
                                       start=True, stop=True)
                    mm.then_inc(lv_ps.sem, 1)
                    m += 1
            pe.wait_ge(*lv_sb.nth(l, NLV - 1))
            pe.wait_ge(*kd_sb.nth(l, 1))
            pe.wait_ge(*qe_sb.nth(l, 1))
            pe.wait_ge(*hg_zero.nth(l, 0))

            def outputs(t):
                pe.wait_ge(*oo_sb.nth(l, t))
                if t:
                    pe.wait_ge(*hot_sb.nth(l, t - 1))
                oo = OO[:, t % 2, :, :].rearrange("p h d -> p (h d)")
                for g in range(2):
                    mm = pe.transpose(PS[:, 7, g * P:(g + 1) * P], oo[:, g * P:(g + 1) * P], IDENT[:, :])
                mm.then_inc(hot_ps.sem, 1)

            for t in range(TILES):
                cut = slice(t * P, (t + 1) * P)
                if t:
                    pe.wait_ge(*kdt_sb.nth(l, t - 1))
                for g in range(2):
                    mm = pe.transpose(PS[:, 0, g * P:(g + 1) * P], KDF[:, g, cut], IDENT[:, :])
                mm.then_inc(kdt_ps.sem, 1)
                if t >= 2:
                    pe.wait_ge(*oo_sb.nth(l, t - 2))
                ho = hgrn_out(t)
                if 0 < t < PT_:
                    pe.wait_ge(*st_sb.nth(l, t - 1))
                if t == PT_:
                    pe.wait_ge(*hmsk_sb.nth(l, 0))
                for h in range(MH):
                    pe.matmul(ho[:, h * DK:(h + 1) * DK], AT[:, t, h % 2, h // 2, :], HI[:, t, h, :],
                              start=h == 0, stop=False, skip_group_check=True)
                for g in range(2):
                    out = ho[:, g * P:(g + 1) * P]
                    if t < PT_:
                        mm = pe.matmul(out, QE[:, g, cut], ST[:, g, :], start=False, stop=True, skip_group_check=True)
                    else:
                        for b in range(NSEQ):
                            mm = pe.matmul(out, QM2[:, g, b, :], SS[:, g, b, :], start=False,
                                           stop=b == NSEQ - 1, skip_group_check=True)
                mm.then_inc(ho_ps.sem, 1)
                pe.wait_ge(*kdt_sb.nth(l, t))
                hi = HI[:, t, :, :].rearrange("p h d -> p (h d)")
                if t < PT_:
                    for g in range(2):
                        mm = pe.matmul(PS[:, 2, g * P:(g + 1) * P], KDT[:, g * P:(g + 1) * P],
                                       hi[:, g * P:(g + 1) * P], start=True, stop=True)
                    mm.then_inc(hup_ps.sem, 1)
                else:
                    pe.wait_ge(*st_sb.nth(l, PT_ - 1))
                    for g in range(2):
                        for k in range(2):
                            mm = pe.matmul(PS[:, 2 + 2 * g + k, :], KDT[:, g * P:(g + 1) * P],
                                           IM[:, 4 * k:4 * k + 4, g * P:(g + 1) * P], start=True, stop=True)
                        mm.then_inc(hup_ps.sem, 1)
                if t:
                    outputs(t - 1)
            outputs(TILES - 1)
            pe.wait_ge(*hot_sb.nth(l, TILES - 1))
            pe.wait_ge(*st_sb.nth(l, PT_ + 1))
            held(pe)

        pe.sem_inc(unit_done, CREDIT)
        pe.wait_ge(setup_in, 16 * SETUP_LOADS)
        pe.transpose(PS[:, 0, 0:96], PROW[0:96, 0, :], IDENT[0:96, 0:96])
        pe.transpose(PS[:, 0, 96:146], PROW[0:50, 1, :], IDENT[0:50, 0:50])
        pe.matmul(PS[:, 1, 0:LAYERS * DK], ONES[0:1, :], HROW[:, :], start=True, stop=True).then_inc(setup_ps, 1)
        pe.wait_ge(setup_sb, 1)
        for c in range(KD):
            if c >= 4:
                pe.wait_ge(x_init, c - 3)
            for t in range(TILES):
                at = (c % 4) * 1024 + t * P
                mm = pe.transpose(psf[:, at:at + P], XIO[:, t, c * P:(c + 1) * P], IDENT[:, :])
            mm.then_inc(xin_ps, 1)
        pe.wait_ge(x_init, KD)
        with pe.Fori(0, LAYERS) as l:
            ffn(l, 0, FFN0)
            proj(l)
            mla(l)
            mlstm(l)
            hgrn(l)
            wout(l)
            ffn(l, 1, FFN1)
        pe.wait_ge(*x_ready.nth(LAYERS - 1, 23))
        for t in range(TILES):
            if t >= 4:
                pe.wait_ge(y_sb, t - 3)
            for c in range(KD):
                at = (t % 4) * 1024 + c * P
                mm = pe.transpose(psf[:, at:at + P], X[:, c, t * P:(t + 1) * P], IDENT[:, :])
            mm.then_inc(y_ps, 1)

    def spread(ap, n):
        return ap.unsqueeze(2).broadcast_to([ap.shape[0], ap.shape[1], n])

    def over(ap, n):
        return ap.unsqueeze(1).broadcast_to([ap.shape[0], n, ap.shape[1]])

    def two(ap):
        if len(ap.shape) == 3:
            return ap.rearrange("p a (h t) -> p (a h) t", h=2)
        return ap.rearrange("p (h t) -> p h t", h=2)

    def level_end(n):
        return sum(PT_ if k < 3 else TILES for k in range(n + 1))

    def halves_of(h):
        def view(tile_):
            if 2 * h > TS:
                return tile_[:, :, 0:TP].rearrange("p g (n q) -> p g n q", q=2 * h)
            return tile_[:, :, :].rearrange("p g (n q) -> p (g n) q", q=2 * h)

        return (lambda x: view(x)[..., 0:h]), (lambda x: view(x)[..., h:2 * h])

    ENDS_P, ENDS_S = slice(P - 1, TP, P), slice(TP + TS - 1, T, TS)
    TB = GB

    @block.scalar
    def _(act):
        chain = Chain(act, act_chain, ACT_STEPS)

        def run(out, in_, func, **kw):
            return nc.scalar.activation(out, in_, func, **kw)

        def logarithms():
            nc.scalar.preload_act_table_set("natural_log_exp_and_others")

        def split_hi(l, base, i, j):
            act.wait_ge(loaded[j % 2], turn(l, base + j - j % 2, i, 0))
            act.wait_ge(unit_done, unit(l, base, i, j) + 1)
            run(WH[:, j % 2, :], RAW[:, j % 2, :], ACT.Copy).then_inc(hi_ready, 1)

        def inverse_rms(l, q, n=D):
            logarithms()
            act.wait_ge(*ms_ready.nth(l, q))
            chain.link(run(two(R[:, :]), PS[:, 6:8, 0:HALF], ACT.Ln, bias=EPSC[:, 0:1], scale=1.0 / n))
            run(R[:, :], R[:, :], ACT.Exp, scale=-0.5).then_inc(r_ready.sem, 1)

        def square_y(l, i, j, u, sq):
            act.wait_ge(drained, u + 3)
            act.wait_ge(*sq_added.nth(l, sq + 2 * i + j - 2))
            run(two(GB[:, j, :]), two(Y[:, bass.ds(2 * i + j, 1), :]), ACT.Square).then_inc(sq_ready.sem, 1)

        def up(l, base, pairs, h0, first):
            def step(i, j, split):
                if split:
                    split_hi(l, base, i, j + 1)
                act.wait_ge(*gate_ready.nth(l, 2 * i + (h0 + j)))
                run(GB[:, j, :], GB[:, j, :], ACT.Silu).then_inc(silu_ready.sem, 1)
                act.wait_ge(*h_ready.nth(l, 2 * i + (h0 + j)))
                run(HH[:, bass.ds(2 * i + j, 1), :].rearrange("p a t -> p (a t)"), UB[:, j, :], ACT.Copy)\
                    .then_inc(hh_ready.sem, 1)

            if first:
                for j in range(2):
                    step(0, j, j == 1)
            with act.Fori(1 if first else 0, pairs) as i:
                for j in range(2):
                    step(i, j, True)

        def down(l, base, sq=None):
            with act.Fori(0, DOWN // 2) as i:
                for j in range(2):
                    split_hi(l, base, i, j + 1)
                    if sq is not None:
                        square_y(l, i, j, unit(l, base, i, j), sq)

        def ffn(l, f, base):
            h0 = f * (UP_A + UP_B)
            split_hi(l, base, 0, 1)
            inverse_rms(l, 4 * f)
            up(l, base, UP_A // 2, h0, True)
            down(l, base + UP_A)
            up(l, base + UP_A + DOWN, UP_B // 2, h0 + UP_A, False)
            down(l, base + UP_A + DOWN + UP_B, SQ_POST[2 * f])
            inverse_rms(l, 4 * f + 1)

        def square_x(l, c, pre):
            if c >= 2:
                act.wait_ge(*sq_added.nth(l, SQ_PRE[pre] + c - 2))
            run(GB[:, c % 2, :], X[:, c, :], ACT.Square).then_inc(sq_ready.sem, 1)

        def split_x(l, pre, stage):
            for c in range(KD):
                if stage is not None:
                    act.wait_ge(*x_ready.nth(l, KD * stage + c))
                g = 16 * pre + c
                run(XH[:, c, :], X[:, c, :], ACT.Copy, scale=LP[:, g:g + 1]).then_inc(xh_ready.sem, 1)
                square_x(l, c, pre)

        def split_normalised(l):
            for c in range(KD):
                act.wait_ge(*x_ready.nth(l, c))
                square_x(l, c, 1)
            inverse_rms(l, 2)
            for c in range(KD):
                act.wait_ge(*xt_ready.nth(l, c))
                run(XH[:, c, :], TB[:, c % 2, :], ACT.Copy).then_inc(xh_ready.sem, 1)

        def proj(l):
            for n in range(PROJ_UNITS):
                j = n % 2
                split_hi(l, PROJ + n - j, 0, j + 1)
                if n in (0, 9):
                    act.wait_ge(unit_done, unit(l, PROJ, 0, n) + 3)
                if n == 0:
                    run(HQ[:, :, :].rearrange("p c (h t) -> p (c h) t", h=2), PS[:, 0:4, 0:HALF], ACT.Silu)\
                        .then_inc(proj_sb.sem, 1)
                if n == 9:
                    run(HGG[:, :, :, :].rearrange("p t h v -> p (t h v)"), psf[:, 2048:2048 + 1280], ACT.Silu)\
                        .then_inc(proj_sb.sem, 1)
                if n == 2:
                    logarithms()
                    act.wait_ge(*za_sb.nth(l, 0))
                    chain.link(run(ZA, ZA, ACT.Exp, scale=-1.0))
                    run(ZA, ZA, ACT.Ln, bias=ONES[:, 0:1]).then_inc(zl_sb.sem, 1)
                if n == 8:
                    act.wait_ge(drained, unit(l, PROJ, 0, 7) + 3)
                    run(OG[:, :, :], OG[:, :, :], ACT.Exp, scale=-1.0).then_inc(oexp_sb.sem, 1)
                if n == 3:
                    act.wait_ge(*zs_sb.nth(l, 0))
                    run(KK, KK, ACT.Exp).then_inc(zk_sb.sem, 1)
                if n == 4:
                    act.wait_ge(*zd_sb.nth(l, 0))
                    chain.link(run(ZE, ZE, ACT.Exp, scale=-1.0))
                    run(ZE, ZE, ACT.Ln, bias=ONES[:, 0:1]).then_inc(ze_sb.sem, 1)

        def mla(l):
            logarithms()
            act.wait_ge(drained, unit(l, PROJ, 0, 9) + 3)
            act.wait_ge(*xl_ready.nth(l, SPLIT_PRE[1] + KD - 1))
            run(GB[:, :, :], CQ[:, :, :], ACT.Square)
            run(R[:, :], CKVT[:, :], ACT.Square).then_inc(mla_sq.sem, 1)
            act.wait_ge(*wukt_ps.nth(l, 0))
            run(WUKT[:, :, :].rearrange("n (a h) c -> n a (h c)", a=2), PS[0:NOPE, 0:2, :], ACT.Copy)\
                .then_inc(wukt_sb.sem, 1)
            act.wait_ge(*mla_ms.nth(l, 0))
            run(two(GB[:, 0, :]), PS[:, 2:4, 0:HALF], ACT.Ln, bias=EPSC[:, 0:1], scale=1.0 / QL)
            chain.link(run(two(GB[:, 1, :]), PS[:, 4:6, 0:HALF], ACT.Ln, bias=EPSC[:, 0:1], scale=1.0 / KVL))
            run(GB[:, :, :], GB[:, :, :], ACT.Exp, scale=-0.5).then_inc(mla_r.sem, 1)
            act.wait_ge(*tok_ps.nth(l, 0))
            run(CTOK[:, :, :].rearrange("p t c -> p (t c)"), psf[:, 6 * 512:6 * 512 + T], ACT.Copy)
            run(R[:, 0:TILES * ROPE].rearrange("p (t c) -> p t c", c=ROPE),
                PS[:, 5, 0:TILES * QK].rearrange("p (t c) -> p t c", c=QK)[:, :, NOPE:QK], ACT.Copy)\
                .then_inc(tok_sb.sem, 1)
            for t in range(PT_):
                act.wait_ge(*v_ps.nth(l, t))
                run(VM[:, t, :], PS[:, t, :], ACT.Copy).then_inc(v_sb.sem, 1)

            def head(h):
                act.wait_ge(*qk_ps.nth(l, h))
                if h >= 2:
                    act.wait_ge(*pv_ps.nth(l, PT_ * (h - 1) - 1))
                run(two(QT[:, h % 2, :]), PS[0:QK, 0:2, 0:HALF], ACT.Copy, scale=MLA_SCALE)
                run(KT[0:NOPE, h % 2, :], PS[0:NOPE, 2, :], ACT.Copy).then_inc(qk_sb.sem, 1)

            def latent_queries(h):
                act.wait_ge(*ql_ps.nth(l, h))
                act.wait_ge(*q_ready.nth(l, h))
                run(QLAT[:, :, h, :], PS[:, 2, 0:P].rearrange("p (b t) -> p b t", t=TS), ACT.Copy)
                run(QPE[:, :, h, :], QT[NOPE:QK, h % 2, TP:T].rearrange("p (b t) -> p b t", t=TS), ACT.Copy).then_inc(ql_sb.sem, 1)

            def probabilities(n):
                i = n % PT_
                act.wait_ge(*nm_sb.nth(l, n))
                if n >= 2:
                    act.wait_ge(*t_ps.nth(l, n - 2))
                run(PB[:, n % 2, 0:(i + 1) * P], PS[:, 3 + n % 2, 0:(i + 1) * P], ACT.Exp,
                    bias=MX[:, n % 4, 1:2], accum_out=MX[:, n % 4, 2:3]).then_inc(exp_sb.sem, 1)

            def transposed(n):
                i = n % PT_
                act.wait_ge(*t_ps.nth(l, n))
                if n >= 2:
                    act.wait_ge(*pv_ps.nth(l, n - 2))
                run(PTB[:, n % 2, 0:(i + 1) * P], PS[:, 5, 0:(i + 1) * P], ACT.Copy).then_inc(pt_sb.sem, 1)

            def pair_output(pair):
                act.wait_ge(*ot_ps.nth(l, pair))
                run(Y[:, pair, 0:TP], PS[:, 2, :], ACT.Copy).then_inc(o_sb.sem, 1)

            head(0)
            latent_queries(0)
            probabilities(0)
            probabilities(1)
            transposed(0)
            for n in range(NT):
                if n % PT_ == 0 and n // PT_ + 1 < H:
                    head(n // PT_ + 1)
                if n + 1 < NT:
                    transposed(n + 1)
                if n % PT_ == 1 and n // PT_ + 1 < H:
                    latent_queries(n // PT_ + 1)
                if n % 8 == 3 and n > 8:
                    pair_output(n // 8 - 1)
                if n + 2 < NT:
                    probabilities(n + 2)
            pair_output(H // 2 - 1)
            run(KN[:, :], KPER[NOPE:QK, TP:T], ACT.Copy).then_inc(kn_sb.sem, 1)

            def stream_keys(b):
                act.wait_ge(*ct_ps.nth(l, b))
                if b >= 2:
                    act.wait_ge(*ss_ps.nth(l, b - 2))
                run(CT[:, b % 2, :], PS[:, 0, :], ACT.Copy)
                run(KPT[0:ROPE, b % 2, 0:PAST], PS[0:ROPE, 1, :], ACT.Copy).then_inc(ct_sb.sem, 1)

            def stream_exp(b):
                bank = 4 + 2 * (b % 2)
                act.wait_ge(*snm_sb.nth(l, b))
                if b >= 2:
                    act.wait_ge(*spt_ps.nth(l, b - 2))
                run(SP[:, b % 2, :], psf[:, bank * 512:bank * 512 + PAST + TS], ACT.Exp,
                    bias=MX[:, b % 2, 1:2], accum_out=MX[:, b % 2, 2:3]).then_inc(sexp_sb.sem, 1)

            def stream_transposed(b):
                act.wait_ge(*spt_ps.nth(l, b))
                if b >= 2:
                    act.wait_ge(*spv_ps.nth(l, b - 2))
                run(SPT[:, b % 2, :], psf[:, 1024:1024 + T], ACT.Copy).then_inc(spt_sb.sem, 1)

            stream_keys(0)
            stream_keys(1)
            stream_exp(0)
            stream_transposed(0)
            stream_exp(1)
            for b in range(NSEQ):
                if b + 2 < NSEQ:
                    stream_keys(b + 2)
                if b + 1 < NSEQ:
                    stream_transposed(b + 1)
                if b + 2 < NSEQ:
                    stream_exp(b + 2)
            act.wait_ge(*uo_ps.nth(l, 0))
            run(Y[:, 0:4, TP:T], PS[:, 0, :].rearrange("p (c t) -> p c t", t=P), ACT.Copy).then_inc(mla_done.sem, 1)

        def mlstm(l):
            act.wait_ge(stored, l * (16 * LAYER_STORES) + 16 * 4)
            run(R[0:MH, :], MISC[32:32 + MH, :], ACT.Identity, bias=GBL[32:36, 0:1])
            run(GB[0:MH, 0, :], MISC[0:MH, :], ACT.Identity, bias=GBL[0:4, 0:1]).then_inc(ga_sb.sem, 1)
            act.wait_ge(*gab_sb.nth(l, 0))
            chain.link(run(GB[0:MH, 1, :], GB[0:MH, 1, :], ACT.Exp, scale=-1.0))
            run(GB[0:MH, 1, :], GB[0:MH, 1, :], ACT.Ln, bias=ONES[0:MH, 0:1]).then_inc(gl_sb.sem, 1)
            act.wait_ge(*ext_sb.nth(l, 0))
            for c in range(4):
                w, b = LP[:, G_CW + c:G_CW + c + 1], LP[:, G_CB + c:G_CB + c + 1]
                run(QKC[:, c, 0:TP], EXTP[:, c, 0:TP], ACT.Identity, scale=w, bias=b)
                ins = run(QKC[:, c, TP:T].rearrange("p (b t) -> p b t", t=TS), EXTS[:, c, :, 0:TS], ACT.Identity,
                          scale=w, bias=b)
            ins.then_inc(tap_sb.sem, 1)
            act.wait_ge(*cn_ps.nth(l, 0))
            run(Y[0:3, 4, 0:512], PS[0:3, 1, :], ACT.Copy)
            run(Y[0:24, 5, 0:512], PS[0:24, 2, :], ACT.Copy).then_inc(cn_sb.sem, 1)
            act.wait_ge(*gd_sb.nth(l, 0))
            act.wait_ge(*ml_zero.nth(l, 0))
            run(G3[32:36, :], UB[0:MH, 0, :], ACT.Exp)
            run(G3[64:68, :], GB[0:MH, 0, :], ACT.Exp, scale=-1.0)
            run(G3[96:100, :], GB[0:MH, 1, :], ACT.Exp)
            run(WIE[:, 0:PT_], UB[0:MH, 0, ENDS_P], ACT.Exp)
            run(WIE[:, PT_:12], UB[0:MH, 0, ENDS_S], ACT.Exp).then_inc(ge_sb.sem, 1)
            act.wait_ge(*gt_ps.nth(l, 0))
            run(GT[:, :, :].rearrange("p t g -> p (t g)"), psf[:, 0:T], ACT.Copy)
            run(DGB[:, :, :].rearrange("p h n -> p (h n)"), PS[:, 2, 0:48], ACT.Copy).then_inc(gt_sb.sem, 1)
            for k in range(2):
                act.wait_ge(*conv_sb.nth(l, k))
                run(QKC[:, k:4:2, :], QKC[:, k:4:2, :], ACT.Silu).then_inc(csilu_sb.sem, 1)
            logarithms()
            for t in range(TILES):
                act.wait_ge(*arg_sb.nth(l, t))
                run(DARG[:, :, :], DARG[:, :, :], ACT.Exp).then_inc(wexp_sb.sem, 1)
                if t == 2:
                    decays(l, 0)
                if t == 1:
                    act.wait_ge(cn_stored, 32 * (l + 1))
                if t:
                    out_transposed(l, t - 1, hmt_ps, hmt_sb, 4)
            out_transposed(l, TILES - 1, hmt_ps, hmt_sb, 4)

        def decays(l, n):
            act.wait_ge(*hd_sb.nth(l, n))
            w = TP if n < 3 else T
            run(DD[n % 2][:, :, 0:w], DD[n % 2][:, :, 0:w], ACT.Exp).then_inc(he_sb.sem, 1)

        def out_transposed(l, t, full, done, chunk):
            act.wait_ge(*full.nth(l, t))
            run(Y[:, chunk:chunk + 2, t * P:(t + 1) * P], PS[:, 7, 0:256].rearrange("p (c t) -> p c t", t=P),
                ACT.Copy).then_inc(done.sem, 1)

        def hgrn(l):
            for n in range(1, NLEV - 1):
                decays(l, n)
            act.wait_ge(*kd_sb.nth(l, 0))
            run(KDF[:, :, :], KDF[:, :, :], ACT.Exp)
            run(EBL[:, :, 0:PT_], BC[:, :, ENDS_P], ACT.Exp)
            run(EBL[:, :, PT_:12], BC[:, :, ENDS_S], ACT.Exp)
            run(QE[:, :, :], BC[:, :, :], ACT.Exp).then_inc(qe_sb.sem, 1)
            for t in range(TILES):
                act.wait_ge(*kdt_ps.nth(l, t))
                if t:
                    act.wait_ge(*hup_ps.nth(l, t - 1))
                run(KDT[:, :], PS[:, 0, 0:256], ACT.Copy).then_inc(kdt_sb.sem, 1)
                act.wait_ge(*ho_ps.nth(l, t))
                run(OSQ[:, :, :].rearrange("p h v -> p (h v)"), hgrn_out(t), ACT.Square).then_inc(hsq_sb.sem, 1)
                act.wait_ge(*hrs_sb.nth(l, t))
                chain.link(run(ORM[:, 1, :], ORM[:, 0, :], ACT.Ln, bias=EPSC[:, 0:1], scale=1.0 / DK))
                run(ORM[:, 1, :], ORM[:, 1, :], ACT.Exp, scale=-0.5).then_inc(hr_sb.sem, 1)
                if t:
                    out_transposed(l, t - 1, hot_ps, hot_sb, 6)
            out_transposed(l, TILES - 1, hot_ps, hot_sb, 6)

        def wout(l):
            act.wait_ge(*st_sb.nth(l, PT_ + 1))
            act.wait_ge(*hot_sb.nth(l, TILES - 1))
            for c in range(KD):
                run(XH[:, c, :], Y[:, c, :], ACT.Copy).then_inc(xh_ready.sem, 1)
            for n in range(OUT_UNITS):
                j = n % 2
                split_hi(l, WOUT + n - j, 0, j + 1)
                act.wait_ge(drained, unit(l, WOUT, 0, n) + 3)
                for c in range(2):
                    act.wait_ge(*sq_added.nth(l, SQ_POST[1] + 2 * n + c - 2))
                    run(GB[:, c, :], Y[:, 2 * n + c, :], ACT.Square).then_inc(sq_ready.sem, 1)
            inverse_rms(l, 3)

        logarithms()
        split_hi(0, 0, 0, 0)
        for c in range(KD):
            act.wait_ge(xin_ps, c + 1)
            run(X[:, c, :], psf[:, (c % 4) * 1024:(c % 4) * 1024 + T], ACT.Copy).then_inc(x_init, 1)
        act.wait_ge(dve_setup, 5)
        run(LB[:, 2:4, :], LB[:, 2:4, :], ACT.Exp, scale=-1.0).then_inc(act_setup, 1)
        act.wait_ge(act_setup, 1)
        run(LB[:, 2:4, :], LB[:, 2:4, :], ACT.Ln, bias=ONES[:, 0:1]).then_inc(act_setup, 1)
        act.wait_ge(dve_setup, 6)
        run(HB[:, 1, 4:6], HB[:, 1, 2:4], ACT.Exp).then_inc(act_setup, 1)
        with act.Fori(0, LAYERS) as l:
            chain.l = l
            act.wait_ge(*lp_ready.nth(l, 0))
            split_x(l, 0, None)
            ffn(l, 0, FFN0)
            split_normalised(l)
            proj(l)
            mla(l)
            mlstm(l)
            hgrn(l)
            wout(l)
            split_x(l, 2, 1)
            ffn(l, 1, FFN1)
            chain.close()
        act.wait_ge(y_ps, 1)
        for t in range(TILES):
            act.wait_ge(y_ps, t + 1)
            run(XIO[:, t, :], psf[:, (t % 4) * 1024:(t % 4) * 1024 + D], ACT.Copy).then_inc(y_sb, 1)

    @block.vector
    def _(dve):
        chain = Chain(dve, dve_chain, DVE_STEPS)
        V = nc.vector

        def split_lo(l, base, i, j):
            dve.wait_ge(hi_ready, unit(l, base, i, j) + 1)
            V.tensor_tensor(WL[:, j % 2, :], RAW[:, j % 2, :], WH[:, j % 2, :].bitcast(F32), ALU.subtract)\
                .then_inc(lo_ready, 1)

        def up(l, base, pairs, h0, first):
            def step(i, j, split):
                if split:
                    split_lo(l, base, i, j + 1)
                u = unit(l, base, i, j)
                dve.wait_ge(unit_done, u + 3)
                V.tensor_tensor(two(GB[:, j, :]), PS[:, 4 * j:4 * j + 2, 0:HALF], two(R[:, :]), ALU.mult)\
                    .then_inc(gate_ready.sem, 1)
                dve.wait_ge(*hl_ready.nth(l, 2 * i + (h0 + j - 2)))
                V.tensor_tensor(two(UB[:, j, :]), PS[:, 4 * j + 2:4 * j + 4, 0:HALF], two(R[:, :]), ALU.mult)\
                    .then_inc(drained, 1)
                dve.wait_ge(drained, u + 3)
                dve.wait_ge(*silu_ready.nth(l, 2 * i + (h0 + j)))
                V.tensor_tensor(UB[:, j, :], GB[:, j, :], UB[:, j, :], ALU.mult).then_inc(h_ready.sem, 1)

            if first:
                for j in range(2):
                    step(0, j, j == 1)
            with dve.Fori(1 if first else 0, pairs) as i:
                for j in range(2):
                    step(i, j, True)

        def down(l, base, add):
            with dve.Fori(0, DOWN // 2) as i:
                for j in range(2):
                    split_lo(l, base, i, j + 1)
                    dve.wait_ge(unit_done, unit(l, base, i, j) + 3)
                    y, ps = two(Y[:, bass.ds(2 * i + j, 1), :]), PS[:, 4 * j:4 * j + 2, 0:HALF]
                    ins = V.tensor_tensor(y, ps, y, ALU.add) if add else V.tensor_copy(y, ps)
                    ins.then_inc(drained, 1)

        def ffn(l, f, base):
            h0 = f * (UP_A + UP_B)
            split_lo(l, base, 0, 1)
            dve.wait_ge(*r_ready.nth(l, 4 * f))
            up(l, base, UP_A // 2, h0, True)
            down(l, base + UP_A, False)
            up(l, base + UP_A + DOWN, UP_B // 2, h0 + UP_A, False)
            down(l, base + UP_A + DOWN + UP_B, True)

        def lo_of_x(l, pre, c):
            dve.wait_ge(*xh_ready.nth(l, SPLIT_PRE[pre] + c))
            g = 16 * pre + c
            V.scalar_tensor_tensor(out=XL[:, c, :], in0=X[:, c, :], scalar=LP[:, g:g + 1],
                                   in1=XH[:, c, :].bitcast(F32), op0=ALU.mult, op1=ALU.subtract)\
                .then_inc(xl_ready.sem, 1)

        def residual(l, stage, pre):
            dve.wait_ge(*r_ready.nth(l, 2 * stage + 1))
            for c in range(KD):
                g = 16 * stage + 8 + c
                chain.link(V.scalar_tensor_tensor(out=Y[:, c, :], in0=Y[:, c, :], scalar=LP[:, g:g + 1],
                                                  in1=R[:, :], op0=ALU.mult, op1=ALU.mult))
                V.tensor_tensor(X[:, c, :], X[:, c, :], Y[:, c, :], ALU.add).then_inc(x_ready.sem, 1)
                if pre is not None and c:
                    lo_of_x(l, pre, c - 1)
            if pre is not None:
                lo_of_x(l, pre, KD - 1)

        def split_normalised(l):
            dve.wait_ge(*r_ready.nth(l, 2))

            def lo(c):
                dve.wait_ge(*xh_ready.nth(l, SPLIT_PRE[1] + c))
                V.tensor_tensor(XL[:, c, :], TB[:, c % 2, :], XH[:, c, :].bitcast(F32), ALU.subtract)\
                    .then_inc(xl_ready.sem, 1)

            for c in range(KD):
                g = 16 + c
                if c >= 2:
                    dve.wait_ge(*xl_ready.nth(l, SPLIT_PRE[1] + c - 2))
                V.scalar_tensor_tensor(out=TB[:, c % 2, :], in0=X[:, c, :], scalar=LP[:, g:g + 1], in1=R[:, :],
                                       op0=ALU.mult, op1=ALU.mult).then_inc(xt_ready.sem, 1)
                if c:
                    lo(c - 1)
            lo(KD - 1)

        def hgrn_abs(l):
            dve.wait_ge(drained, unit(l, PROJ, 0, 1) + 3)
            V.scalar_tensor_tensor(out=ZA.rearrange("p g t -> p (g t)"),
                                   in0=HF[:, :, :].rearrange("p g t -> p (g t)"), scalar=-1.0,
                                   in1=HF[:, :, :].rearrange("p g t -> p (g t)"), op0=ALU.mult, op1=ALU.max)\
                .then_inc(za_sb.sem, 1)

        def hgrn_log_sigmoids(l):
            dve.wait_ge(*zl_sb.nth(l, 0))
            chain.link(V.scalar_tensor_tensor(out=ZL, in0=HF[:, :, :], scalar=0.0, in1=ZA,
                                              op0=ALU.min, op1=ALU.subtract))
            V.tensor_tensor(KK, ZL, HF[:, :, :], ALU.subtract).then_inc(zs_sb.sem, 1)

        def hgrn_difference(l):
            dve.wait_ge(*zs_sb.nth(l, 0))
            for g in range(2):
                ins = V.tensor_scalar(ZL[:, g, :], ZL[:, g, :], HBL[:, 2 + g:3 + g], None, ALU.add)
            chain.link(ins)
            for g in range(2):
                ins = V.tensor_scalar(ZE[:, g, :], ZL[:, g, :], HBL[:, g:g + 1], None, ALU.subtract)
            chain.link(ins)
            for g in range(2):
                V.tensor_scalar(ZL[:, g, :], ZL[:, g, :], HBL[:, g:g + 1], None, ALU.max)
            V.scalar_tensor_tensor(out=ZE, in0=ZE, scalar=-1.0, in1=ZE, op0=ALU.mult, op1=ALU.max)\
                .then_inc(zd_sb.sem, 1)

        def hgrn_sums(l):
            dve.wait_ge(*ze_sb.nth(l, 0))
            chain.link(V.tensor_tensor(ZA, ZL, ZE, ALU.add))
            for g in range(2):
                for at in (*range(0, TP, P), *range(TP, T, TS)):
                    w = P if at < TP else TS
                    ins = V.tensor_tensor_scan(HF[:, g, at:at + w], ONES[:, 0:w], ZA[:, g, at:at + w], 0.0,
                                               ALU.mult, ALU.add)
            ins.then_inc(bc_sb.sem, 1)

        def output_gate(l):
            dve.wait_ge(*oexp_sb.nth(l, 0))
            chain.link(V.tensor_scalar(OG[:, :, :], OG[:, :, :], 1.0, None, ALU.add))
            chain.link(V.reciprocal(OG[:, :, :], OG[:, :, :]))

        gate_steps = {8: output_gate, 1: hgrn_abs, 2: hgrn_log_sigmoids, 3: hgrn_difference, 5: hgrn_sums}

        def proj(l):
            for n in range(PROJ_UNITS):
                j = n % 2
                b = 4 * j
                split_lo(l, PROJ + n - j, 0, j + 1)
                if n in (0, 9):
                    dve.wait_ge(*proj_sb.nth(l, n // 9))
                    dve.sem_inc(drained, 1)
                    continue
                dve.wait_ge(unit_done, unit(l, PROJ, 0, n) + 3)
                four, flat = PS[:, b:b + 4, 0:HALF], psf[:, b * 512:b * 512 + 1280]
                if n == 2:
                    ins = V.tensor_copy(CQ[:, :, :].rearrange("p c (h t) -> p (c h) t", h=2), four)
                elif n == 3:
                    V.tensor_copy(two(CKVT[:, :]), PS[:, b:b + 2, 0:HALF])
                    ins = V.tensor_copy(two(MISC[:, :]), PS[:, b + 2:b + 4, 0:HALF])
                elif n in (4, 5):
                    for part in range(2):
                        c, q = 2 * (n - 4) + part, b + 2 * part
                        V.tensor_copy(EXTP[:, c, 3:3 + HALF], PS[:, q, 0:HALF])
                        V.tensor_copy(EXTP[:, c, 3 + HALF:3 + TP], PS[:, q + 1, 0:TP - HALF])
                        ins = V.tensor_copy(EXTS[:, c, :, 3:3 + TS],
                                            PS[:, q + 1, TP - HALF:HALF].rearrange("p (b t) -> p b t", t=TS))
                elif n == 1:
                    ins = V.tensor_copy(HF[:, :, :].rearrange("p c (h t) -> p (c h) t", h=2), four)
                elif n == 6:
                    ins = V.tensor_copy(VA[:, :, :, :].rearrange("p t h a -> p (t h) a")[:, :, 0:DK],
                                        flat.rearrange("p (n v) -> p n v", v=DK))
                elif n == 7:
                    ins = V.tensor_copy(OG[:, :, :].rearrange("p t v -> p (t v)"), flat)
                else:
                    ins = V.tensor_copy(HI[:, :, :, :].rearrange("p t h v -> p (t h v)"), flat)
                ins.then_inc(drained, 1)
                if n in gate_steps:
                    gate_steps[n](l)

        def mla(l):
            R_ = slice(NOPE, QK)
            cos, sin = ROPET[R_, 0, :], ROPET[R_, 1, :]
            dve.wait_ge(mla_in, (l + 1) * 80)
            dve.wait_ge(*kswap_ps.nth(l, 0))
            chain.link(V.tensor_tensor(KPER[R_, :], MISC[R_, :], cos, ALU.mult))
            chain.link(V.tensor_tensor(two(MISC[R_, :]), PS[R_, 6:8, 0:HALF], two(sin), ALU.mult))
            V.tensor_tensor(KPER[R_, :], KPER[R_, :], MISC[R_, :], ALU.add).then_inc(kpe_ready.sem, 1)
            dve.wait_ge(*mla_r.nth(l, 0))
            for c in range(2):
                V.scalar_tensor_tensor(out=CQ[:, c, :], in0=CQ[:, c, :], scalar=LP[:, G_Q + c:G_Q + c + 1],
                                       in1=GB[:, 0, :], op0=ALU.mult, op1=ALU.mult)
            V.scalar_tensor_tensor(out=CKVT[:, :], in0=CKVT[:, :], scalar=LP[:, G_KV:G_KV + 1],
                                   in1=GB[:, 1, :], op0=ALU.mult, op1=ALU.mult).then_inc(cq_ready.sem, 1)
            dve.wait_ge(*cq_ready.nth(l, 0))

            def head(h):
                dve.wait_ge(*sw_ps.nth(l, h))
                chain.link(V.tensor_tensor(two(GB[R_, 0, :]), PS[R_, 0:2, 0:HALF], two(sin), ALU.mult))
                dve.wait_ge(*qc_sb.nth(l, h))
                V.tensor_tensor(QT[R_, h % 2, :], GB[R_, 1, :], GB[R_, 0, :], ALU.add).then_inc(q_ready.sem, 1)

            def maximum(n):
                i = n % PT_
                dve.wait_ge(*s_ps.nth(l, n))
                chain.link(V.memset(PS[0:64, 3 + n % 2, i * P + 64:(i + 1) * P], -FAR))
                if n >= 4:
                    dve.wait_ge(*on_sb.nth(l, n - 4))
                V.reduce_max(MX[:, n % 4, 1:2], PS[:, 3 + n % 2, 0:(i + 1) * P], AX_X, negate=True)\
                    .then_inc(nm_sb.sem, 1)

            def normalise(n):
                h, i = divmod(n, PT_)
                dve.wait_ge(*pv_ps.nth(l, n))
                chain.link(V.reciprocal(MX[:, n % 4, 3:4], MX[:, n % 4, 2:3]))
                at = i * P + 64 * (h % 2)
                V.tensor_scalar(Y[:, h // 2, at:at + 64], PS[:, 6 + n % 2, 0:64], MX[:, n % 4, 3:4], None,
                                ALU.mult).then_inc(on_sb.sem, 1)

            head(0)
            for n in range(NT):
                if n % PT_ == PT_ - 1 and n // PT_ + 1 < H:
                    head(n // PT_ + 1)
                maximum(n)
                if n >= 3:
                    normalise(n - 3)
            for n in range(NT - 3, NT):
                normalise(n)

            def stream_maximum(b):
                bank = 4 + 2 * (b % 2)
                dve.wait_ge(*ss_ps.nth(l, b))
                V.reduce_max(MX[:, b % 2, 1:2], psf[:, bank * 512:bank * 512 + PAST + TS], AX_X, negate=True)\
                    .then_inc(snm_sb.sem, 1)

            def stream_output(b):
                dve.wait_ge(*spv_ps.nth(l, b))
                V.tensor_copy(OLAT[:, :, b * TS:(b + 1) * TS],
                              latent_out(b).rearrange("p (h t) -> p h t", t=TS)).then_inc(ol_sb.sem, 1)

            dve.wait_ge(*pn_zero.nth(l, 0))
            for b in range(NSEQ):
                stream_maximum(b)
                dve.wait_ge(*sexp_sb.nth(l, b))
                chain.link(V.reciprocal(MX[:, b % 2, 3:4], MX[:, b % 2, 2:3]))
                V.tensor_scalar(PNEW[:, b, b * TS:(b + 1) * TS], SP[:, b % 2, PAST:PAST + TS], MX[:, b % 2, 3:4],
                                None, ALU.mult)
                V.tensor_scalar(SP[:, b % 2, 0:PAST], SP[:, b % 2, 0:PAST], MX[:, b % 2, 3:4], None, ALU.mult)\
                    .then_inc(sp_sb.sem, 1)
                if b >= 2:
                    stream_output(b - 2)
            for b in range(NSEQ - 2, NSEQ):
                stream_output(b)

        def scaled(l, n):
            dve.wait_ge(*he_sb.nth(l, n))
            if n == 0:
                dve.wait_ge(*kk_sb.nth(l, 0))
            if n >= 2:
                dve.wait_ge(*lv_ps.nth(l, level_end(n - 2) - 1))
            left, right = halves_of(LEVELS[n])
            q, e = QKL[n % 2], DD[n % 2]
            V.tensor_tensor(left(q), left(KK), left(e), ALU.mult)
            V.tensor_tensor(right(q), right(HQ), right(e), ALU.mult).then_inc(hq_sb.sem, 1)

        def mlstm(l):
            dve.wait_ge(*mla_done.nth(l, 0))
            dve.wait_ge(*ml_zero.nth(l, 0))
            dve.wait_ge(*ext_zero.nth(l, 0))
            V.tensor_copy(CNT[:, :, :].rearrange("p c (b r) -> p c b r", r=3), EXTS[:, :, :, TS:TS + 3])\
                .then_inc(cnt_sb.sem, 1)
            dve.wait_ge(ml_in, (l + 1) * 112)
            dve.wait_ge(*ga_sb.nth(l, 0))
            zf, ab = R[0:MH, :], GB[0:MH, 1, :]
            V.scalar_tensor_tensor(out=ab, in0=zf, scalar=-1.0, in1=zf, op0=ALU.mult, op1=ALU.max)\
                .then_inc(gab_sb.sem, 1)
            dve.wait_ge(*cs_ps.nth(l, 0))
            chain.link(V.tensor_copy(EXTS[:, :, :, 0:3],
                                     PS[:, 0, 0:96].rearrange("p (c b r) -> p c b r", c=4, r=3)))
            dve.sem_inc(ext_sb.sem, 1)
            lf, bc, a2, li, a = UB[0:MH, 0, :], UB[0:MH, 1, :], UB[0:MH, 0, :], GB[0:MH, 0, :], G3[0:MH, :]
            g, mt = R[0:MH, :], GB[0:MH, 0, :]
            dve.wait_ge(*gl_sb.nth(l, 0))
            chain.link(V.scalar_tensor_tensor(out=lf, in0=zf, scalar=0.0, in1=ab, op0=ALU.min, op1=ALU.subtract))
            chain.link(V.tensor_tensor_scan(bc, GOING[:, :], lf, 0.0, ALU.mult, ALU.add))
            chain.link(V.tensor_tensor(a, li, bc, ALU.subtract))
            V.tensor_copy(a2, a)
            V.tensor_copy(DROP[:, P:TP:P], UB[0:MH, 1, P - 1:TP - 1:P])
            V.memset(MPV[:, 0:1], 0.0)
            chain.link(V.tensor_copy(MPV[:, PT_:12], M0[:, :]))
            chain.link(V.tensor_tensor(UB[0:MH, 0, TP:T:TS], G3[0:MH, TP:T:TS], M0[:, :], ALU.max))
            chain.link(V.tensor_tensor_scan(g, DROP[:, :], a2, 0.0, ALU.add, ALU.max))
            V.tensor_copy(GE[:, 0:PT_], R[0:MH, ENDS_P])
            V.tensor_copy(GE[:, PT_:12], R[0:MH, ENDS_S])
            chain.link(V.tensor_tensor(mt, bc, g, ALU.add))
            chain.link(V.tensor_copy(MPV[:, 1:PT_], GB[0:MH, 0, P - 1:TP - 1:P]))
            for cut, n0, n1, w in ((slice(0, TP), 0, PT_, P), (slice(TP, T), PT_, 12, TS)):
                rows = lambda ap: ap.rearrange("h (n t) -> h n t", t=w)
                V.tensor_tensor(rows(UB[0:MH, 0, cut]), spread(MPV[:, n0:n1], w), rows(R[0:MH, cut]), ALU.subtract)
                V.tensor_tensor(rows(GB[0:MH, 1, cut]), rows(G3[0:MH, cut]), spread(GE[:, n0:n1], w), ALU.subtract)
            V.tensor_scalar(UB[0:MH, 1, :], g, -1.0, None, ALU.mult).then_inc(gd_sb.sem, 1)
            dve.wait_ge(*tap_sb.nth(l, 0))
            for k in range(2):
                for tap in range(1, 4):
                    for c in (k, k + 2):
                        w = LP[:, G_CW + 4 * tap + c:G_CW + 4 * tap + c + 1]
                        for out, in0 in (
                            (QKC[:, c, 0:TP], EXTP[:, c, tap:tap + TP]),
                            (QKC[:, c, TP:T].rearrange("p (b t) -> p b t", t=TS), EXTS[:, c, :, tap:tap + TS]),
                        ):
                            ins = V.scalar_tensor_tensor(out=out, in0=in0, scalar=w, in1=out,
                                                         op0=ALU.mult, op1=ALU.add)
                    if tap < 3:
                        chain.link(ins)
                ins.then_inc(conv_sb.sem, 1)
            dve.wait_ge(*gt_sb.nth(l, 0))

            def arguments(t):
                dve.wait_ge(*nb_ps.nth(l, t))
                for h in range(MH):
                    ins = V.scalar_tensor_tensor(out=DARG[:, h, :], in0=PS[:, 2, h * P:(h + 1) * P],
                                                 scalar=GT[:, t, h:h + 1], in1=MASK[:, t // PT_, :],
                                                 op0=ALU.add, op1=ALU.min)
                ins.then_inc(arg_sb.sem, 1)

            def weights(t):
                dve.wait_ge(*wexp_sb.nth(l, t))
                dve.wait_ge(*mk_ps.nth(l, t))
                if t:
                    dve.wait_ge(*mo_ps.nth(l, t - 1))
                for e in range(2):
                    ins = V.scalar_tensor_tensor(out=WT[:, e:4:2, :],
                                                 in0=PS[:, 1 + 2 * e, 0:256].rearrange("p (g t) -> p g t", t=P),
                                                 scalar=DK ** -0.5, in1=DARG[:, e:4:2, :],
                                                 op0=ALU.mult, op1=ALU.mult)
                ins.then_inc(wt_sb.sem, 1)
                if t:
                    dve.wait_ge(*upd_ps.nth(l, t - 1))
                V.scalar_tensor_tensor(out=KW[:, :, :], in0=PS[:, 0, 0:256].rearrange("p (h d) -> p h d", d=DK),
                                       scalar=DK ** -0.5, in1=spread(GT[:, t, 96:100], DK),
                                       op0=ALU.mult, op1=ALU.mult).then_inc(kw_sb.sem, 1)

            arguments(0)
            weights(0)
            for t in range(TILES):
                dve.wait_ge(*mo_ps.nth(l, t))
                chain.link(V.tensor_tensor(NI[:, :, :], PS[:, 4, 0:260].rearrange("p (h a) -> p h a", a=AUG),
                                           spread(GT[:, t, 32:36], AUG), ALU.mult))
                V.tensor_tensor(NI[:, :, :], NI[:, :, :], PS[:, 5, 0:260].rearrange("p (h a) -> p h a", a=AUG),
                                ALU.add).then_inc(ni_sb.sem, 1)
                if t < PT_:
                    dve.wait_ge(*upd_ps.nth(l, t))
                    for h in range(MH):
                        rows, cols = slice(64 * (h % 2), 64 * (h % 2) + 64), slice(AUG * (h % 2), AUG * (h % 2) + AUG)
                        ins = V.scalar_tensor_tensor(out=CST[rows, h // 2, cols], in0=CST[rows, h // 2, cols],
                                                     scalar=DGB[rows, h, t:t + 1],
                                                     in1=PS[rows, 6, h * AUG:(h + 1) * AUG],
                                                     op0=ALU.mult, op1=ALU.add)
                    ins.then_inc(cst_sb.sem, 1)
                dve.wait_ge(*ni_sb.nth(l, t))
                chain.link(V.scalar_tensor_tensor(out=DEN[:, 0, :], in0=NI[:, :, DK], scalar=-1.0,
                                                  in1=NI[:, :, DK], op0=ALU.mult, op1=ALU.max))
                chain.link(V.tensor_tensor(DEN[:, 0, :], DEN[:, 0, :], GT[:, t, 64:68], ALU.max))
                chain.link(V.reciprocal(DEN[:, 1, :], DEN[:, 0, :]))
                if t:
                    dve.wait_ge(*hmt_ps.nth(l, t - 1))
                hm = HM[:, :].rearrange("p (h v) -> p h v", v=DK)
                chain.link(V.tensor_tensor(hm, NI[:, :, 0:DK], spread(DEN[:, 1, :], DK), ALU.mult))
                V.tensor_tensor(HM[:, :], HM[:, :], OG[:, t, :], ALU.mult).then_inc(hm_sb.sem, 1)
                if t + 1 < TILES:
                    arguments(t + 1)
                    weights(t + 1)
                if t == 2:
                    scaled(l, 0)
            dve.wait_ge(ml_st, (l + 1) * 128)
            for h in range(MH):
                rows, cols = slice(64 * (h % 2), 64 * (h % 2) + 64), slice(AUG * (h % 2), AUG * (h % 2) + AUG)
                ins = V.tensor_tensor(CSS[rows, h // 2, :, cols], CSS[rows, h // 2, :, cols],
                                      spread(DGB[rows, h, PT_:12], AUG), ALU.mult)
            chain.link(ins)
            for g_ in range(2):
                dve.wait_ge(*csu_ps.nth(l, g_))
                for k in range(3):
                    b0, b1 = 3 * k, min(3 * k + 3, NSEQ)
                    for half in range(2):
                        rows, cols = slice(64 * half, 64 * half + 64), slice(AUG * half, AUG * half + AUG)
                        ps = PS[rows, 1 + 3 * g_ + k, 0:(b1 - b0) * 130].rearrange("p (b n) -> p b n", n=130)[:, :, cols]
                        ins = V.tensor_tensor(CSS[rows, g_, b0:b1, cols], CSS[rows, g_, b0:b1, cols], ps, ALU.add)
                ins.then_inc(csu_sb.sem, 1)

        def hgrn(l):
            dve.wait_ge(*csu_sb.nth(l, 1))
            chain.link(V.memset(AT[:, :, :, :, :], 0.0))
            dve.wait_ge(level_in, (l + 1) * 16)
            held(dve)
            V.tensor_copy(LVL[:, :, :], raw_levels).then_inc(lvl_sb.sem, 1)

            m = 0
            dve.wait_ge(*lvl_sb.nth(l, 0))
            for n in range(NLEV):
                if n + 1 < NLEV - 1:
                    scaled(l, n + 1)
                elif n + 1 == NLEV - 1:
                    dve.sem_inc(hq_sb.sem, 1)
                for t in range(PT_ if n < 3 else TILES):
                    dve.wait_ge(*lv_ps.nth(l, m))
                    held(dve)
                    V.copy_predicated(AT[:, t, :, :, :],
                                      LVL[:, n, :].unsqueeze(1).unsqueeze(1).broadcast_to([P, 2, 2, P]),
                                      PS[:, 2 * (m % 3):2 * (m % 3) + 2, 0:256].rearrange("p e (g t) -> p e g t", t=P))\
                        .then_inc(lv_sb.sem, 1)
                    dve.wait_ge(*lv_sb.nth(l, m))
                    m += 1
            dve.wait_ge(*qe_sb.nth(l, 0))
            V.tensor_tensor(KDF[:, :, :], KDF[:, :, :], KK[:, :, :], ALU.mult).then_inc(kd_sb.sem, 1)
            V.tensor_tensor(QE[:, :, :], QE[:, :, :], HQ[:, :, :], ALU.mult).then_inc(qe_sb.sem, 1)
            dve.wait_ge(*hg_zero.nth(l, 0))
            for t in range(TILES):
                dve.wait_ge(*hsq_sb.nth(l, t))
                V.reduce_sum(ORM[:, 0, :], OSQ[:, :, :], AX_X).then_inc(hrs_sb.sem, 1)
                if t < PT_:
                    dve.wait_ge(*hup_ps.nth(l, t))
                    for h in range(MH):
                        rows, cols = slice(64 * (h % 2), 64 * (h % 2) + 64), slice(DK * (h % 2), DK * (h % 2) + DK)
                        ins = V.scalar_tensor_tensor(out=ST[rows, h // 2, cols], in0=ST[rows, h // 2, cols],
                                                     scalar=EBL[rows, h // 2, t:t + 1],
                                                     in1=PS[rows, 2, h * DK:(h + 1) * DK],
                                                     op0=ALU.mult, op1=ALU.add)
                    ins.then_inc(st_sb.sem, 1)
                dve.wait_ge(*hr_sb.nth(l, t))
                oo = OO[:, t % 2, :, :]
                if t >= 2:
                    dve.wait_ge(*hot_ps.nth(l, t - 2))
                chain.link(V.tensor_tensor(oo, hgrn_out(t).rearrange("p (h v) -> p h v", v=DK),
                                           spread(ORM[:, 1, :], DK), ALU.mult))
                chain.link(V.tensor_tensor(oo, oo, over(HGNL[:, :], MH), ALU.mult))
                V.tensor_tensor(oo, oo, HGG[:, t, :, :], ALU.mult).then_inc(oo_sb.sem, 1)
            dve.wait_ge(hg_in, (l + 1) * 80)
            for h in range(MH):
                rows, cols = slice(64 * (h % 2), 64 * (h % 2) + 64), slice(DK * (h % 2), DK * (h % 2) + DK)
                ins = V.tensor_tensor(SS[rows, h // 2, :, cols], SS[rows, h // 2, :, cols],
                                      spread(EBL[rows, h // 2, PT_:12], DK), ALU.mult)
            chain.link(ins)
            for g in range(2):
                dve.wait_ge(*hup_ps.nth(l, PT_ + g))
                for half in range(2):
                    rows, cols = slice(64 * half, 64 * half + 64), slice(DK * half, DK * half + DK)
                    for k in range(2):
                        ps = PS[rows, 2 + 2 * g + k, :].rearrange("p (b n) -> p b n", n=P)[:, :, cols]
                        ss = SS[rows, g, 4 * k:4 * k + 4, cols]
                        ins = V.tensor_tensor(ss, ss, ps, ALU.add)
                ins.then_inc(st_sb.sem, 1)

        def wout(l):
            for c in range(KD):
                dve.wait_ge(*xh_ready.nth(l, SPLIT_MIX + c))
                if c == KD // 2:
                    dve.wait_ge(stored, (l + 1) * (16 * LAYER_STORES))
                V.tensor_tensor(XL[:, c, :], Y[:, c, :], XH[:, c, :].bitcast(F32), ALU.subtract)\
                    .then_inc(xl_ready.sem, 1)
            for n in range(OUT_UNITS):
                j = n % 2
                split_lo(l, WOUT + n - j, 0, j + 1)
                dve.wait_ge(unit_done, unit(l, WOUT, 0, n) + 3)
                if n == 0:
                    dve.wait_ge(*xl_ready.nth(l, SPLIT_MIX + KD - 1))
                V.tensor_copy(Y[:, 2 * n:2 * n + 2, :].rearrange("p c (h t) -> p (c h) t", h=2),
                              PS[:, 4 * j:4 * j + 4, 0:HALF]).then_inc(drained, 1)

        dve.sem_inc(lo_ready, CREDIT)
        dve.sem_inc(drained, CREDIT)
        V.memset(EPSC[:, :], EPS)
        V.memset(HB[:, 0, 0:2], -FAR)
        V.memset(HB[:, 0, 2:4], 0.0)
        V.memset(HB[:, 0, 4:6], 1.0).then_inc(dve_setup, 1)
        dve.wait_ge(setup_ps, 1)
        V.tensor_copy(PAR[:, :], PS[:, 0, 0:PAR.shape[1]]).then_inc(dve_setup, 1)
        V.tensor_copy(HGN[:, :, :].rearrange("p l v -> p (l v)"), PS[:, 1, 0:LAYERS * DK]).then_inc(setup_sb, 1)
        b0 = LAYERS * G_END
        dve.wait_ge(dve_setup, 2)
        V.tensor_tensor(LB[:, 0, :], PAR[:, b0 + 2:b0 + 4], PAR[:, b0:b0 + 2], ALU.subtract).then_inc(dve_setup, 1)
        dve.wait_ge(dve_setup, 3)
        V.tensor_scalar(LB[:, 1, :], LB[:, 0, :], -1.0, None, ALU.mult).then_inc(dve_setup, 1)
        dve.wait_ge(dve_setup, 4)
        V.tensor_tensor(LB[:, 2, :], LB[:, 0, :], LB[:, 1, :], ALU.max)
        V.tensor_tensor(LB[:, 3, :], LB[:, 0, :], LB[:, 1, :], ALU.max).then_inc(dve_setup, 1)
        dve.wait_ge(act_setup, 2)
        V.scalar_tensor_tensor(out=HB[:, 1, 0:4].rearrange("p (a b) -> p a b", b=2), in0=LB[:, 0:2, :], scalar=0.0,
                               in1=LB[:, 2:4, :], op0=ALU.min, op1=ALU.subtract).then_inc(dve_setup, 1)
        dve.wait_ge(act_setup, 3)
        dve.wait_ge(hi_ready, 1)
        V.tensor_tensor(WL[:, 0, :], RAW[:, 0, :], WH[:, 0, :].bitcast(F32), ALU.subtract).then_inc(lo_ready, 1)
        dve.wait_ge(setup_sb, 1)
        dve.wait_ge(x_init, KD)
        with dve.Fori(0, LAYERS) as l:
            chain.l = l
            V.tensor_copy(LP[:, 0:G_Q], PAR[:, bass.ds(l * G_Q, G_Q)])
            V.tensor_copy(LP[:, G_Q:G_END], PAR[:, bass.ds(l * NB_COLS + LAYERS * G_Q, NB_COLS)])
            V.tensor_copy(GBL[0:4, :], GBIAS[0:4, bass.ds(l, 1)])
            V.tensor_copy(GBL[32:36, :], GBIAS[32:36, bass.ds(l, 1)])
            V.tensor_copy(HGNL[:, :], HGN[:, bass.ds(l, 1), :].rearrange("p a v -> p (a v)"))
            chain.link(V.tensor_copy(HBL[:, :], HB[:, bass.ds(l, 1), :].rearrange("p a v -> p (a v)")))
            for j in (1, 5):
                ins = V.tensor_scalar(LP[:, 8 * j:8 * j + 8], LP[:, 8 * j:8 * j + 8], 0.5, None, ALU.mult)
            ins.then_inc(lp_ready.sem, 1)
            for c in range(KD):
                lo_of_x(l, 0, c)
            ffn(l, 0, FFN0)
            residual(l, 0, None)
            split_normalised(l)
            proj(l)
            mla(l)
            mlstm(l)
            hgrn(l)
            wout(l)
            residual(l, 1, 2)
            ffn(l, 1, FFN1)
            residual(l, 2, None)
            chain.close()

    @block.gpsimd
    def _(pool):
        chain = Chain(pool, pool_chain, POOL_STEPS)
        G = nc.gpsimd

        def low_h(l, i, j, h0):
            pool.wait_ge(*hh_ready.nth(l, 2 * i + (h0 + j)))
            G.tensor_tensor(HL[:, bass.ds(2 * i + j, 1), :].rearrange("p a t -> p (a t)"), UB[:, j, :],
                            HH[:, bass.ds(2 * i + j, 1), :].rearrange("p a t -> p (a t)").bitcast(F32),
                            ALU.subtract).then_inc(hl_ready.sem, 1)

        def add_square(l, k, j, total):
            pool.wait_ge(*sq_ready.nth(l, k))
            G.tensor_tensor(total, total, GB[:, j, :], ALU.add).then_inc(sq_added.sem, 1)

        def sum_x(l, pre, extra=None):
            pool.wait_ge(*sq_ready.nth(l, SQ_PRE[pre]))
            held(pool)
            G.tensor_copy(SX, GB[:, 0, :]).then_inc(sq_added.sem, 1)
            for c in range(1, KD):
                pool.wait_ge(*sq_added.nth(l, SQ_PRE[pre] + c - 1))
                add_square(l, SQ_PRE[pre] + c, c % 2, SX)

        def ffn(l, f):
            h0 = f * (UP_A + UP_B)
            sum_x(l, 2 * f)
            with pool.Fori(0, UP_A // 2) as i:
                for j in range(2):
                    low_h(l, i, j, h0)
            with pool.Fori(0, UP_B // 2) as i:
                for j in range(2):
                    low_h(l, i, j, h0 + UP_A)
            sum_y(l, 2 * f)

        def sum_y(l, stage):
            pool.wait_ge(*sq_ready.nth(l, SQ_POST[stage]))
            held(pool)
            chain.link(G.memset(SY, 0.0))
            held(pool)
            with pool.Fori(0, KD // 2) as i:
                for j in range(2):
                    k = 2 * i + (SQ_POST[stage] + j)
                    pool.wait_ge(*sq_added.nth(l, k - 1))
                    pool.wait_ge(*sq_ready.nth(l, k))
                    G.tensor_tensor(SY, SY, GB[:, j, :], ALU.add).then_inc(sq_added.sem, 1)

        def load(s, dst, src):
            held(pool)
            pool.dma_start(dst, src).then_inc(s, 16)

        def store(dst, src):
            held(pool)
            pool.dma_start(dst, src).then_inc(stored, 16)

        def mla(l):
            pool.wait_ge(unit_done, unit(l, FFN0, 0, FFN_UNITS - 1) + 3)
            load(mla_in, WUQ[:, :, :], A["mla_w_uq"][l].rearrange("(c p) n -> p c n", p=P))
            load(mla_in, WUK[:, :, :], A["mla_w_uk"][l])
            load(mla_in, WUV[:, :], A["mla_w_uv"][l].rearrange("c h v -> c (h v)"))
            load(mla_in, SWAP[:, :], A["c_swap"])
            held(pool)
            G.memset(KPER[0:NOPE, :], 0.0).then_inc(kper_zero.sem, 1)
            pool.wait_ge(*r_ready.nth(l, 2))
            load(mla_in, UB[NOPE:QK, :, :], A["c_rope"][:, NOPE:QK, :].rearrange("a p t -> p a t"))
            pool.wait_ge(*zk_sb.nth(l, 0))
            held(pool)
            for g in range(2):
                ins = G.tensor_scalar(KK[:, g, :], KK[:, g, :], HBL[:, 4 + g:5 + g], None, ALU.mult)
            ins.then_inc(kk_sb.sem, 1)

            def cache(b):
                c = b % CBUF
                load(cache_in[c], CC[c], A["cache_ckv"][l, b].rearrange("(k p) c -> p k c", p=P))
                load(cache_in[c], CK[c], A["cache_kpe"][l, b].rearrange("(k p) c -> p k c", p=P))

            pool.wait_ge(drained, unit(l, PROJ, 0, 6) + 3)
            held(pool)
            G.memset(EXTP[:, :, 0:3], 0.0)
            G.memset(VA[:, :, :, DK:AUG], 1.0).then_inc(ext_zero.sem, 1)
            pool.wait_ge(*bc_sb.nth(l, 0))
            for b in range(2):
                cache(b)
            pool.wait_ge(*kpe_ready.nth(l, 0))
            pool.wait_ge(*kk_sb.nth(l, 0))
            pool.wait_ge(*ext_zero.nth(l, 0))
            held(pool)
            for j in range(2):
                ins = G.tensor_copy(KT[NOPE:QK, j, :], KPER[NOPE:QK, 0:TP])
            ins.then_inc(kt_rope.sem, 1)
            pool.wait_ge(*tok_sb.nth(l, 0))
            ktok = R[:, 0:TILES * ROPE].rearrange("p (t c) -> p t c", c=ROPE)
            store(O["p_ckv"][l, 0].rearrange("(t p) c -> p t c", p=P), CTOK[:, 0:PT_, :])
            store(O["s_ckv"][l].rearrange("b t c -> (b t) c"), CTOK[:, PT_, :])
            store(O["p_kpe"][l, 0].rearrange("(t p) c -> p t c", p=P), ktok[:, 0:PT_, :])
            store(O["s_kpe"][l].rearrange("b t c -> (b t) c"), ktok[:, PT_, :])
            for h in range(H):
                pool.wait_ge(*qk_sb.nth(l, h))
                if h:
                    pool.wait_ge(*q_ready.nth(l, h - 1))
                held(pool)
                G.tensor_tensor(GB[NOPE:QK, 1, :], QT[NOPE:QK, h % 2, :], ROPET[NOPE:QK, 0, :], ALU.mult)\
                    .then_inc(qc_sb.sem, 1)
            pool.wait_ge(*pv_ps.nth(l, NT - 1))
            pool.wait_ge(*o_sb.nth(l, H // 2 - 1))

            held(pool)
            G.memset(PNEW[:, :, :], 0.0).then_inc(pn_zero.sem, 1)
            cache(2)
            for b in range(3, NSEQ):
                if b >= CBUF:
                    pool.wait_ge(*spv_ps.nth(l, b - CBUF))
                cache(b)

        def distances(l, n):
            h = LEVELS[n]
            if n >= 2:
                pool.wait_ge(*hq_sb.nth(l, n - 2))
            left, right = halves_of(h)
            lb, rb = left(BC), right(BC)
            ref = lb[..., h - 1:h].broadcast_to(list(lb.shape))
            G.tensor_tensor(left(DD[n % 2]), ref, lb, ALU.subtract)
            G.tensor_tensor(right(DD[n % 2]), rb, ref, ALU.subtract).then_inc(hd_sb.sem, 1)

        def mlstm(l):
            pool.wait_ge(*mla_done.nth(l, 0))
            pool.wait_ge(stored, l * (16 * LAYER_STORES) + 16 * 4)
            held(pool)
            G.memset(G3[:, :], 0.0).then_inc(ml_zero.sem, 1)
            G.memset(CST[:, :, :], 0.0).then_inc(cst_zero.sem, 1)
            G.memset(CSS[:, :, :, :], 0.0).then_inc(css_zero.sem, 1)
            chain.link(G.memset(QM[:, :, :, :], 0.0))
            pool.wait_ge(*cn_sb.nth(l, 0))
            held(pool)
            pool.dma_start(O["p_conv"][l, 0], Y[0:3, 4, 0:512]).then_inc(cn_stored, 16)
            pool.dma_start(O["s_conv"][l].rearrange("b r n -> (b r) n"), Y[0:24, 5, 0:512]).then_inc(cn_stored, 16)
            pool.wait_ge(*csilu_sb.nth(l, 1))
            held(pool)
            for b in range(NSEQ):
                G.tensor_copy(QM[:, :, b, b * TS:(b + 1) * TS], QKC[:, 0:2, TP + b * TS:TP + (b + 1) * TS])
            pool.wait_ge(ml_in, (l + 1) * 112)
            G.tensor_tensor(VMSK[:, :, :], over(VA[:, PT_, :, :].rearrange("p h a -> p (h a)"), NSEQ),
                            spread(OWN[:, :], MH * AUG), ALU.mult).then_inc(msk_sb.sem, 1)
            pool.wait_ge(*msk_sb.nth(l, 0))
            held(pool)
            distances(l, 0)
            pool.wait_ge(*gd_sb.nth(l, 0))
            store(O["p_m"][l, 0].rearrange("(h a) -> h a", a=1), GB[0:MH, 0, TP - 1:TP])
            store(O["s_m"][l].rearrange("b (h a) -> h b a", a=1), GB[0:MH, 0, ENDS_S].unsqueeze(2))

        def hgrn(l):
            pool.wait_ge(*csu_sb.nth(l, 1))
            held(pool)
            distances(l, 1)
            distances(l, 2)
            pool.wait_ge(*hmt_sb.nth(l, TILES - 1))
            held(pool)
            G.memset(SS[:, :, :, :], 0.0).then_inc(ss_zero.sem, 1)
            distances(l, 3)
            pool.wait_ge(ml_stored, (l + 1) * 256)
            held(pool)
            G.memset(ST[:, :, :], 0.0)
            G.memset(QM2[:, :, :, :], 0.0).then_inc(hg_zero.sem, 1)
            for n in range(4, NLEV - 1):
                distances(l, n)
            pool.wait_ge(*lvl_sb.nth(l, 0))
            held(pool)
            for cut, w in ((slice(0, TP), P), (slice(TP, T), TS)):
                b = BC[:, :, cut].rearrange("p g (n t) -> p g n t", t=w)
                ins = G.tensor_tensor(KDF[:, :, cut].rearrange("p g (n t) -> p g n t", t=w),
                                      b[..., w - 1:w].broadcast_to(list(b.shape)), b, ALU.subtract)
            ins.then_inc(kd_sb.sem, 1)
            pool.wait_ge(hg_in, (l + 1) * 80)
            held(pool)
            G.tensor_tensor(IM[:, :, :], over(HI[:, PT_, :, :].rearrange("p h v -> p (h v)"), NSEQ),
                            spread(OWN2[:, :], MH * DK), ALU.mult)
            pool.wait_ge(*qe_sb.nth(l, 1))
            pool.wait_ge(*hg_zero.nth(l, 0))
            held(pool)
            for b in range(NSEQ):
                ins = G.tensor_copy(QM2[:, :, b, b * TS:(b + 1) * TS], QE[:, :, TP + b * TS:TP + (b + 1) * TS])
            ins.then_inc(hmsk_sb.sem, 1)
            pool.wait_ge(*st_sb.nth(l, PT_ - 1))
            for h, rows, g, c in blocks_of(ST, DK):
                store(O["p_hgrn"][l, 0, h], ST[rows, g, c:c + DK])
            pool.wait_ge(*st_sb.nth(l, PT_ + 1))
            for h, rows, g, c in blocks_of(SS, DK):
                store(O["s_hgrn"][l, :, h].rearrange("b d v -> d b v"), SS[rows, g, :, c:c + DK])

        pool.sem_inc(hl_ready.sem, CREDIT)
        with pool.Fori(0, LAYERS) as l:
            chain.l = l
            ffn(l, 0)
            sum_x(l, 1)
            mla(l)
            mlstm(l)
            hgrn(l)
            sum_y(l, 1)
            ffn(l, 1)
            chain.close()

    ctx.close()


_INS = ['x_prompt', 'x_sample', 'cache_ckv', 'cache_kpe', 'state_mlstm_c', 'state_mlstm_n', 'state_mlstm_m',
        'state_mlstm_conv', 'state_hgrn', 'ln_gains', 'w_ffn_in', 'w_ffn_out', 'w_in', 'w_out',
        'mla_q_norm', 'mla_kv_norm', 'mla_w_uq', 'mla_w_uk', 'mla_w_uv', 'ml_conv_w', 'ml_conv_b',
        'ml_gate_bias', 'hg_lb_raw', 'hg_norm']
_OUT_NAMES = ['y_prompt', 'y_sample', 'p_ckv', 'p_kpe', 'p_c', 'p_n', 'p_m', 'p_conv', 'p_hgrn',
              's_ckv', 's_kpe', 's_c', 's_n', 's_m', 's_conv', 's_hgrn']


def _states(b, t):
    return [(LAYERS, b, t, KVL), (LAYERS, b, t, ROPE), (LAYERS, b, MH, DK, DK), (LAYERS, b, MH, DK),
            (LAYERS, b, MH), (LAYERS, b, 3, 2 * MH * DK), (LAYERS, b, MH, DK, DK)]


_OUTS = [((1, TP, D), 'float32'), ((NSEQ, TS, D), 'float32')] + \
    [(s, 'float32') for s in _states(1, TP) + _states(NSEQ, TS)]


def kernel(**inputs):
    import numpy as _np
    import concourse.bacc as _bacc
    from concourse import mybir as _mybir
    from concourse.bass_utils import run_bass_kernel_spmd as _run

    nc = _bacc.Bacc("TRN2", target_bir_lowering=False, num_devices=1)
    arrays, ins, outs = {}, {}, {}
    for name, a in [(n, _np.ascontiguousarray(inputs[n])) for n in _INS] + list(shape_constants().items()):
        arrays[f"in_{name}_dram"] = a
        ins[name] = nc.dram_tensor(f"in_{name}_dram", a.shape, _mybir.dt.from_np(a.dtype), kind="ExternalInput").ap()
    for i, (name, (shape, dtype)) in enumerate(zip(_OUT_NAMES, _OUTS)):
        dt = _mybir.dt.from_np(_np.dtype(dtype))
        outs[name] = nc.dram_tensor(f"out_{i}_dram", shape, dt, kind="ExternalOutput").ap()
    encoder(nc, ins, outs)
    r = _run(nc, [arrays], core_ids=[0])
    return tuple(r.results[0][f"out_{i}_dram"] for i in range(len(_OUTS)))
```
